# Optimizing a Trainium2 kernel written in Bass

```python
import jax, jax.numpy as jnp
from jax import lax
import numpy as np
import math

D_MODEL = 1024
BATCH = 1
SEQ = 512
DEPTH = 2

N_EVEN = (DEPTH + 1) // 2
N_ODD = DEPTH // 2

GLA_HEADS = 4
GLA_DK = 64
GLA_DV = 128
GLA_GATE_RANK = 16
GLA_GATE_TAU = 16.0
GLA_CHUNK = 64

DSA_HEADS = 4
DSA_HEAD_DIM = 128
IDX_HEADS = 8
IDX_DIM = 64
DSA_TOPK = 256

POOL_WINDOWS = (2, 4, 8, 16)
POOL_GROUPS = 4
POOL_CH = 128

SB_HEADS = 4
SB_HEAD_DIM = 128

BLOCK_Q = 128
ROPE_THETA = 10000.0
NORM_EPS = 1e-6
D_FF = ((8 * D_MODEL + 3 * 256 - 1) // (3 * 256)) * 256

AB_SPLITS = (GLA_HEADS * GLA_DK, GLA_HEADS * GLA_DK, GLA_HEADS * GLA_DV, GLA_GATE_RANK,
             GLA_HEADS * GLA_DV,
             DSA_HEADS * DSA_HEAD_DIM, DSA_HEADS * DSA_HEAD_DIM, DSA_HEADS * DSA_HEAD_DIM,
             IDX_HEADS * IDX_DIM, IDX_DIM, IDX_HEADS)
AB_IN = sum(AB_SPLITS)
D_MIX_AB = GLA_HEADS * GLA_DV + DSA_HEADS * DSA_HEAD_DIM
CD_SPLITS = (POOL_GROUPS * POOL_CH, SB_HEADS * SB_HEAD_DIM, SB_HEADS * SB_HEAD_DIM,
             SB_HEADS * SB_HEAD_DIM)
CD_IN = sum(CD_SPLITS)
D_MIX_CD = POOL_GROUPS * POOL_CH + SB_HEADS * SB_HEAD_DIM


def split_cols(t, sizes):
    offsets = np.cumsum(sizes)[:-1].tolist()
    return jnp.split(t, offsets, axis=-1)

def rms_norm(t, w):
    tf = t.astype(jnp.float32)
    y = tf * lax.rsqrt(jnp.mean(tf * tf, axis=-1, keepdims=True) + NORM_EPS)
    return (y * w.astype(jnp.float32)).astype(t.dtype)

def modulate(h, shift, scale):
    return h * (1.0 + scale[:, None, :]) + shift[:, None, :]

def rope(t, positions):
    half = t.shape[-1] // 2
    inv_freq = ROPE_THETA ** (-jnp.arange(half, dtype=jnp.float32) / half)
    ang = positions.astype(jnp.float32)[:, :, None, None] * inv_freq
    cos, sin = jnp.cos(ang), jnp.sin(ang)
    tf = t.astype(jnp.float32)
    t1, t2 = tf[..., :half], tf[..., half:]
    return jnp.concatenate([t1 * cos - t2 * sin, t2 * cos + t1 * sin], axis=-1).astype(t.dtype)

def swiglu(h, w1, w2):
    gate, up = jnp.split(h @ w1, 2, axis=-1)
    return (jax.nn.silu(gate) * up) @ w2

def gla_chunked(q, k, v, log_a):
    B, S, H, DK = q.shape
    DV = v.shape[-1]
    C = GLA_CHUNK
    N = S // C

    def chunks(t):
        return t.astype(jnp.float32).reshape(B, N, C, H, t.shape[-1]).transpose(0, 3, 1, 2, 4)

    q, k, v, g = chunks(q), chunks(k), chunks(v), chunks(log_a)
    q = q * (DK ** -0.5)
    b = jnp.cumsum(g, axis=3)
    b_mid = b[:, :, :, C // 2 - 1:C // 2, :]
    att = jnp.einsum('bhnid,bhnjd->bhnij', q * jnp.exp(b - b_mid), k * jnp.exp(b_mid - b))
    causal = jnp.tril(jnp.ones((C, C), dtype=bool))
    att = jnp.where(causal, att, 0.0)
    o_intra = jnp.einsum('bhnij,bhnjv->bhniv', att, v)
    b_last = b[:, :, :, -1:, :]
    k_dec = k * jnp.exp(b_last - b)
    q_dec = q * jnp.exp(b)
    decay = jnp.exp(b_last[:, :, :, 0, :])
    kv = jnp.einsum('bhncd,bhncv->bhndv', k_dec, v)

    def step(state, inp):
        dec, kv_n = inp
        return dec[..., None] * state + kv_n, state

    init = jnp.zeros((B, H, DK, DV), jnp.float32)
    _, prev = lax.scan(step, init, (jnp.moveaxis(decay, 2, 0), jnp.moveaxis(kv, 2, 0)))
    prev = jnp.moveaxis(prev, 0, 2)
    o_inter = jnp.einsum('bhncd,bhndv->bhncv', q_dec, prev)
    o = o_intra + o_inter
    return o.transpose(0, 2, 3, 1, 4).reshape(B, S, H, DV)

def dsa_attention(q, k, v, iq, ik, iw, n_sel):
    B, S, H, Dh = q.shape
    bidx = jnp.arange(B)[:, None, None]
    key_pos = jnp.arange(S)
    idx_scale = (IDX_HEADS ** -0.5) * (IDX_DIM ** -0.5)
    att_scale = Dh ** -0.5

    def block(i):
        t0 = i * BLOCK_Q
        tpos = t0 + jnp.arange(BLOCK_Q)
        qb = lax.dynamic_slice_in_dim(q, t0, BLOCK_Q, axis=1)
        iqb = lax.dynamic_slice_in_dim(iq, t0, BLOCK_Q, axis=1)
        iwb = lax.dynamic_slice_in_dim(iw, t0, BLOCK_Q, axis=1)
        rel = jax.nn.relu(jnp.einsum('bqhd,bsd->bqhs', iqb, ik).astype(jnp.float32))
        score = jnp.einsum('bqhs,bqh->bqs', rel, iwb.astype(jnp.float32)) * idx_scale
        causal = key_pos[None, :] <= tpos[:, None]
        score = jnp.where(causal[None], score, -jnp.inf)
        _, sel = lax.top_k(score, n_sel)
        kg = k[bidx, sel]
        vg = v[bidx, sel]
        logits = jnp.einsum('bqhd,bqkhd->bhqk', qb, kg).astype(jnp.float32) * att_scale
        valid = (sel <= tpos[None, :, None])[:, None]
        logits = jnp.where(valid, logits, -jnp.inf)
        p = jax.nn.softmax(logits, axis=-1).astype(v.dtype)
        return jnp.einsum('bhqk,bqkhd->bqhd', p, vg)

    out = lax.map(block, jnp.arange(S // BLOCK_Q))
    return jnp.moveaxis(out, 0, 1).reshape(B, S, H, Dh)

def stick_breaking_attention(q, k, v):
    B, S, H, Dh = q.shape
    key_pos = jnp.arange(S)
    scale = Dh ** -0.5

    def block(i):
        t0 = i * BLOCK_Q
        tpos = t0 + jnp.arange(BLOCK_Q)
        qb = lax.dynamic_slice_in_dim(q, t0, BLOCK_Q, axis=1)
        z = jnp.einsum('bqhd,bshd->bhqs', qb, k).astype(jnp.float32) * scale
        strict = (key_pos[None, :] < tpos[:, None])[None, None]
        log_beta = jax.nn.log_sigmoid(z)
        log_1m = jnp.where(strict, jax.nn.log_sigmoid(-z), 0.0)
        after = lax.cumsum(log_1m, axis=3, reverse=True) - log_1m
        w = jnp.where(strict, jnp.exp(log_beta + after), 0.0)
        return jnp.einsum('bhqs,bshd->bqhd', w.astype(v.dtype), v)

    out = lax.map(block, jnp.arange(S // BLOCK_Q))
    return jnp.moveaxis(out, 0, 1).reshape(B, S, H, Dh)

def multiscale_pool(u, pool_w, pool_scale):
    B, S, _ = u.shape
    ug = u.astype(jnp.float32).reshape(B, S, POOL_GROUPS, POOL_CH)
    cs = jnp.cumsum(ug, axis=1)
    cs0 = jnp.concatenate([jnp.zeros((B, 1, POOL_GROUPS, POOL_CH), jnp.float32), cs], axis=1)
    t = jnp.arange(S, dtype=jnp.float32)
    pooled = []
    for g, w in enumerate(POOL_WINDOWS):
        lo = jnp.pad(cs0[:, :S + 1 - w, g], ((0, 0), (w - 1, 0), (0, 0)))
        count = jnp.minimum(t + 1.0, float(w))[None, :, None]
        pooled.append((cs[:, :, g] - lo) / count - ug[:, :, g])
    pooled = jnp.stack(pooled, axis=2)
    y = jnp.einsum('bsgc,gcd->bsgd', pooled, pool_w.astype(jnp.float32))
    y = y * pool_scale.astype(jnp.float32).reshape(POOL_GROUPS, POOL_CH)
    return y.reshape(B, S, POOL_GROUPS * POOL_CH).astype(u.dtype)

def ab_mixer(h, positions, w_in, gate_up, gate_b, out_norm, q_norm, k_norm, w_out):
    B, S, _ = h.shape
    (gq, gk, gv, glow, gr, dq, dk, dv, iq, ik, iw) = split_cols(h @ w_in, AB_SPLITS)
    log_a = jax.nn.log_sigmoid((glow @ gate_up + gate_b).astype(jnp.float32)) / GLA_GATE_TAU
    o_gla = gla_chunked(gq.reshape(B, S, GLA_HEADS, GLA_DK), gk.reshape(B, S, GLA_HEADS, GLA_DK),
                        gv.reshape(B, S, GLA_HEADS, GLA_DV), log_a.reshape(B, S, GLA_HEADS, GLA_DK))
    o_gla = rms_norm(o_gla.astype(h.dtype), out_norm) * jax.nn.silu(gr.reshape(B, S, GLA_HEADS, GLA_DV))
    q = rope(rms_norm(dq.reshape(B, S, DSA_HEADS, DSA_HEAD_DIM), q_norm), positions)
    k = rope(rms_norm(dk.reshape(B, S, DSA_HEADS, DSA_HEAD_DIM), k_norm), positions)
    v = dv.reshape(B, S, DSA_HEADS, DSA_HEAD_DIM)
    iq = rope(iq.reshape(B, S, IDX_HEADS, IDX_DIM), positions)
    ik = rope(ik[:, :, None, :], positions)[:, :, 0, :]
    n_sel = min(DSA_TOPK, S // 4)
    o_dsa = dsa_attention(q, k, v, iq, ik, iw, n_sel)
    mix = jnp.concatenate([o_gla.reshape(B, S, -1), o_dsa.reshape(B, S, -1)], axis=-1)
    return mix @ w_out

def cd_mixer(h, w_in, pool_w, pool_scale, q_norm, k_norm, w_out):
    B, S, _ = h.shape
    u, sq, sk, sv = split_cols(h @ w_in, CD_SPLITS)
    o_pool = multiscale_pool(u, pool_w, pool_scale)
    q = rms_norm(sq.reshape(B, S, SB_HEADS, SB_HEAD_DIM), q_norm)
    k = rms_norm(sk.reshape(B, S, SB_HEADS, SB_HEAD_DIM), k_norm)
    v = sv.reshape(B, S, SB_HEADS, SB_HEAD_DIM)
    o_sb = stick_breaking_attention(q, k, v)
    mix = jnp.concatenate([o_pool, o_sb.reshape(B, S, -1)], axis=-1)
    return mix @ w_out

def first_inputs(seed: int = 0) -> dict:
    key = jax.random.key(seed)
    ks = jax.random.split(key, 24)
    f32 = jnp.float32

    def nrm(k, shape, scale):
        return jax.random.normal(k, shape, f32) * scale

    def gain(k, shape):
        return 1.0 + 0.1 * jax.random.normal(k, shape, f32)

    x = nrm(ks[0], (BATCH, SEQ, D_MODEL), 1.0)
    c = nrm(ks[1], (BATCH, D_MODEL), 1.0)
    positions = (jnp.arange(SEQ, dtype=jnp.int32)[None, :]
                 + jax.random.randint(ks[2], (BATCH, 1), 0, 4096, dtype=jnp.int32))
    return {
        "x": x,
        "c": c,
        "positions": positions,
        "ada_w": nrm(ks[3], (DEPTH, D_MODEL, 6 * D_MODEL), 0.5 * D_MODEL ** -0.5),
        "ada_b": nrm(ks[4], (DEPTH, 6 * D_MODEL), 0.01),
        "mix_norm": gain(ks[5], (DEPTH, D_MODEL)),
        "ffn_norm": gain(ks[6], (DEPTH, D_MODEL)),
        "ffn_w1": nrm(ks[7], (DEPTH, D_MODEL, 2 * D_FF), D_MODEL ** -0.5),
        "ffn_w2": nrm(ks[8], (DEPTH, D_FF, D_MODEL), D_FF ** -0.5),
        "ab_w_in": nrm(ks[9], (N_EVEN, D_MODEL, AB_IN), D_MODEL ** -0.5),
        "gla_gate_up": nrm(ks[10], (N_EVEN, GLA_GATE_RANK, GLA_HEADS * GLA_DK), GLA_GATE_RANK ** -0.5),
        "gla_gate_b": nrm(ks[11], (N_EVEN, GLA_HEADS * GLA_DK), 0.01),
        "gla_out_norm": gain(ks[12], (N_EVEN, GLA_DV)),
        "dsa_q_norm": gain(ks[13], (N_EVEN, DSA_HEAD_DIM)),
        "dsa_k_norm": gain(ks[14], (N_EVEN, DSA_HEAD_DIM)),
        "ab_w_out": nrm(ks[15], (N_EVEN, D_MIX_AB, D_MODEL), D_MIX_AB ** -0.5),
        "cd_w_in": nrm(ks[16], (N_ODD, D_MODEL, CD_IN), D_MODEL ** -0.5),
        "pool_w": nrm(ks[17], (N_ODD, POOL_GROUPS, POOL_CH, POOL_CH), POOL_CH ** -0.5),
        "pool_scale": gain(ks[18], (N_ODD, POOL_GROUPS * POOL_CH)),
        "sb_q_norm": gain(ks[19], (N_ODD, SB_HEAD_DIM)),
        "sb_k_norm": gain(ks[20], (N_ODD, SB_HEAD_DIM)),
        "cd_w_out": nrm(ks[21], (N_ODD, D_MIX_CD, D_MODEL), D_MIX_CD ** -0.5),
    }

def first_block(x, c, positions, ada_w, ada_b, mix_norm, ffn_norm, ffn_w1, ffn_w2,
              ab_w_in, gla_gate_up, gla_gate_b, gla_out_norm, dsa_q_norm, dsa_k_norm, ab_w_out,
              cd_w_in, pool_w, pool_scale, sb_q_norm, sb_k_norm, cd_w_out):
    cond = jax.nn.silu(c)
    for layer in range(DEPTH):
        mod = cond @ ada_w[layer] + ada_b[layer]
        sh1, sc1, g1, sh2, sc2, g2 = jnp.split(mod, 6, axis=-1)
        h = modulate(rms_norm(x, mix_norm[layer]), sh1, sc1)
        if layer % 2 == 0:
            i = layer // 2
            y = ab_mixer(h, positions, ab_w_in[i], gla_gate_up[i], gla_gate_b[i], gla_out_norm[i],
                         dsa_q_norm[i], dsa_k_norm[i], ab_w_out[i])
        else:
            i = layer // 2
            y = cd_mixer(h, cd_w_in[i], pool_w[i], pool_scale[i], sb_q_norm[i], sb_k_norm[i],
                         cd_w_out[i])
        x = x + g1[:, None, :] * y
        h = modulate(rms_norm(x, ffn_norm[layer]), sh2, sc2)
        x = x + g2[:, None, :] * swiglu(h, ffn_w1[layer], ffn_w2[layer])
    return x


DEPTH_2 = 1

N_META = 16
BLOCK = 128
META_PAD = BLOCK - N_META
RET_HEADS = 4
RET_DK = D_MODEL // 8
RET_DV = D_MODEL // 4
DIFF_HEADS = 8
DIFF_HD = D_MODEL // 16
DIFF_VD = 2 * DIFF_HD
CONV_WIDTH = D_MODEL
CONV_K = 3
N_BRANCH = 3
BRANCH_W = D_MODEL
D_FF_2 = 4 * D_MODEL
EPS = 1e-6
NEG_INF = -1e30
IN_WIDTHS = (RET_HEADS * RET_DK, RET_HEADS * RET_DK, RET_HEADS * RET_DV, RET_HEADS * RET_DV,
             2 * DIFF_HEADS * DIFF_HD, 2 * DIFF_HEADS * DIFF_HD, DIFF_HEADS * DIFF_VD,
             CONV_WIDTH, CONV_WIDTH, CONV_WIDTH, N_BRANCH * D_MODEL)
D_IN = sum(IN_WIDTHS)


def rms_norm_2(x, w):
    xf = x.astype(jnp.float32)
    y = xf * lax.rsqrt(jnp.mean(xf * xf, axis=-1, keepdims=True) + EPS)
    return (y * w.astype(jnp.float32)).astype(x.dtype)

def head_layer_norm(y):
    yf = y.astype(jnp.float32)
    mu = jnp.mean(yf, axis=-1, keepdims=True)
    var = jnp.mean(jnp.square(yf - mu), axis=-1, keepdims=True)
    return ((yf - mu) * lax.rsqrt(var + EPS)).astype(y.dtype)

def pad_front(t, n):
    return jnp.pad(t, [(0, 0), (n, 0)] + [(0, 0)] * (t.ndim - 2))

def column_bounds():
    bounds, start = [], 0
    for w in IN_WIDTHS:
        bounds.append((start, start + w))
        start += w
    return bounds

def retention(q, k, v):
    b = q.shape[0]
    dt = q.dtype
    k = k * (RET_DK ** -0.5)
    q, k, v = (pad_front(t, META_PAD) for t in (q, k, v))
    nc = q.shape[1] // BLOCK

    def chunks(t):
        return t.reshape(b, nc, BLOCK, RET_HEADS, t.shape[-1]).transpose(1, 0, 3, 2, 4)

    log_g = jnp.log1p(-jnp.exp2(-5.0 - jnp.arange(RET_HEADS, dtype=jnp.float32)))
    i = jnp.arange(BLOCK, dtype=jnp.float32)
    dist = i[:, None] - i[None, :]
    intra = jnp.where(dist >= 0, jnp.exp(log_g[:, None, None] * jnp.maximum(dist, 0.0)), 0.0).astype(dt)
    q_decay = jnp.exp(log_g[:, None] * (i + 1.0)).astype(dt)
    k_decay = jnp.exp(log_g[:, None] * (BLOCK - 1.0 - i)).astype(dt)
    s_decay = jnp.exp(log_g * BLOCK).astype(dt)

    def step(state, qkv):
        qc, kc, vc = qkv
        scores = jnp.einsum('bhid,bhjd->bhij', qc, kc) * intra
        out = (jnp.einsum('bhij,bhjv->bhiv', scores, vc)
               + jnp.einsum('bhid,bhdv->bhiv', qc * q_decay[:, :, None], state))
        state = state * s_decay[:, None, None] + jnp.einsum('bhjd,bhjv->bhdv', kc * k_decay[:, :, None], vc)
        return state, out

    s0 = jnp.zeros((b, RET_HEADS, RET_DK, RET_DV), dt)
    _, out = lax.scan(step, s0, (chunks(q), chunks(k), chunks(v)))
    out = out.transpose(1, 0, 3, 2, 4).reshape(b, nc * BLOCK, RET_HEADS, RET_DV)
    return out[:, META_PAD:]

def diff_attention(q, k, v, lam, subln_w, lam_init):
    b = q.shape[0]
    q, k, v = (pad_front(t, META_PAD) for t in (q, k, v))
    p = q.shape[1]
    nb = p // BLOCK
    kt = k.transpose(0, 2, 3, 1, 4)
    vt = v.transpose(0, 2, 1, 3)
    qb = q.reshape(b, nb, BLOCK, DIFF_HEADS, 2, DIFF_HD).transpose(1, 0, 3, 4, 2, 5)
    slopes = jnp.exp2(-8.0 / DIFF_HEADS * (jnp.arange(DIFF_HEADS, dtype=jnp.float32) + 1.0))
    kpos = jnp.arange(p)
    scale = DIFF_HD ** -0.5

    def block(args):
        qblk, bi = args
        qpos = bi * BLOCK + jnp.arange(BLOCK)
        dist = (qpos[:, None] - kpos[None, :]).astype(jnp.float32)
        valid = (dist >= 0) & (kpos[None, :] >= META_PAD)
        logits = (jnp.einsum('bhmqd,bhmkd->bhmqk', qblk, kt, preferred_element_type=jnp.float32) * scale
                  - slopes[:, None, None, None] * dist)
        probs = jax.nn.softmax(jnp.where(valid, logits, NEG_INF), axis=-1)
        attn = probs[:, :, 0] - lam * probs[:, :, 1]
        return jnp.einsum('bhqk,bhkv->bhqv', attn.astype(vt.dtype), vt)

    out = lax.map(block, (qb, jnp.arange(nb)))
    out = out.transpose(1, 0, 3, 2, 4).reshape(b, p, DIFF_HEADS, DIFF_VD)[:, META_PAD:]
    return rms_norm_2(out, subln_w) * (1.0 - lam_init)

def short_conv(u, w):
    return lax.conv_general_dilated(
        u, w[:, None, :].astype(u.dtype), window_strides=(1,), padding=[(CONV_K - 1, 0)],
        dimension_numbers=('NWC', 'WIO', 'NWC'), feature_group_count=u.shape[-1])

def hybrid_layer(x, layer, norm1_w, w_in, conv_w, lam_vecs, subln_w, w_branch, w_out, norm2_w, w_up, w_down):
    b, l, _ = x.shape
    h = rms_norm_2(x, norm1_w)
    (rq, rk, rv, rg, dq, dk, dv, cb, cc, cx, gates) = [h @ w_in[:, s:e] for s, e in column_bounds()]

    ret = retention(rq.reshape(b, l, RET_HEADS, RET_DK), rk.reshape(b, l, RET_HEADS, RET_DK),
                    rv.reshape(b, l, RET_HEADS, RET_DV))
    ret = head_layer_norm(ret).reshape(b, l, BRANCH_W) * jax.nn.silu(rg)

    lam_init = 0.8 - 0.6 * math.exp(-0.3 * layer)
    lv = lam_vecs.astype(jnp.float32)
    lam = jnp.exp(jnp.sum(lv[0] * lv[1])) - jnp.exp(jnp.sum(lv[2] * lv[3])) + lam_init
    diff = diff_attention(dq.reshape(b, l, DIFF_HEADS, 2, DIFF_HD), dk.reshape(b, l, DIFF_HEADS, 2, DIFF_HD),
                          dv.reshape(b, l, DIFF_HEADS, DIFF_VD), lam, subln_w, lam_init).reshape(b, l, BRANCH_W)

    conv = cb * short_conv(cc * cx, conv_w)

    g = jax.nn.sigmoid(gates.astype(jnp.float32)).astype(x.dtype).reshape(b, l, N_BRANCH, D_MODEL)
    merged = (g[:, :, 0] * (ret @ w_branch[0]) + g[:, :, 1] * (diff @ w_branch[1])
              + g[:, :, 2] * (conv @ w_branch[2]))
    x = x + merged @ w_out

    u = jnp.square(jax.nn.relu(rms_norm_2(x, norm2_w) @ w_up))
    return x + u @ w_down

def second_inputs(seed: int = 0) -> dict:
    key = jax.random.key(seed)
    ks = jax.random.split(key, 13)
    nrm = jax.random.normal
    f32 = jnp.float32
    return {
        "x": nrm(ks[0], (BATCH, SEQ, D_MODEL), f32),
        "meta_tokens": nrm(ks[1], (N_META, D_MODEL), f32),
        "norm1_w": 1.0 + 0.02 * nrm(ks[2], (DEPTH_2, D_MODEL), f32),
        "w_in": nrm(ks[3], (DEPTH_2, D_MODEL, D_IN), f32) * D_MODEL ** -0.5,
        "conv_w": nrm(ks[4], (DEPTH_2, CONV_K, CONV_WIDTH), f32) * CONV_K ** -0.5,
        "diff_lambda": 0.1 * nrm(ks[5], (DEPTH_2, 4, DIFF_HD), f32),
        "diff_subln_w": 1.0 + 0.02 * nrm(ks[6], (DEPTH_2, DIFF_VD), f32),
        "w_branch": nrm(ks[7], (DEPTH_2, N_BRANCH, BRANCH_W, D_MODEL), f32) * BRANCH_W ** -0.5,
        "w_out": nrm(ks[8], (DEPTH_2, D_MODEL, D_MODEL), f32) * D_MODEL ** -0.5,
        "norm2_w": 1.0 + 0.02 * nrm(ks[9], (DEPTH_2, D_MODEL), f32),
        "w_up": nrm(ks[10], (DEPTH_2, D_MODEL, D_FF_2), f32) * D_MODEL ** -0.5,
        "w_down": nrm(ks[11], (DEPTH_2, D_FF_2, D_MODEL), f32) * D_FF_2 ** -0.5,
        "final_norm_w": 1.0 + 0.02 * nrm(ks[12], (D_MODEL,), f32),
    }

def second_block(x, meta_tokens, norm1_w, w_in, conv_w, diff_lambda, diff_subln_w, w_branch, w_out,
              norm2_w, w_up, w_down, final_norm_w):
    b = x.shape[0]
    meta = jnp.broadcast_to(meta_tokens.astype(x.dtype)[None], (b, N_META, D_MODEL))
    h = jnp.concatenate([meta, x], axis=1)
    for layer in range(DEPTH_2):
        h = hybrid_layer(h, layer, norm1_w[layer], w_in[layer], conv_w[layer], diff_lambda[layer],
                         diff_subln_w[layer], w_branch[layer], w_out[layer], norm2_w[layer],
                         w_up[layer], w_down[layer])
    return rms_norm_2(h[:, N_META:], final_norm_w)


def setup_inputs(seed=0):
    out = dict(first_inputs(seed))
    for name, value in second_inputs(seed + 1).items():
        if name != "x":
            out[name + "_2"] = value
    return out


def reference(
    x, c, positions, ada_w, ada_b, mix_norm, ffn_norm, ffn_w1, ffn_w2, ab_w_in, gla_gate_up,
    gla_gate_b, gla_out_norm, dsa_q_norm, dsa_k_norm, ab_w_out, cd_w_in, pool_w, pool_scale,
    sb_q_norm, sb_k_norm, cd_w_out, meta_tokens_2, norm1_w_2, w_in_2, conv_w_2, diff_lambda_2,
    diff_subln_w_2, w_branch_2, w_out_2, norm2_w_2, w_up_2, w_down_2, final_norm_w_2,
):
    x = first_block(
        x, c, positions, ada_w, ada_b, mix_norm, ffn_norm, ffn_w1, ffn_w2, ab_w_in, gla_gate_up,
        gla_gate_b, gla_out_norm, dsa_q_norm, dsa_k_norm, ab_w_out, cd_w_in, pool_w, pool_scale,
        sb_q_norm, sb_k_norm, cd_w_out,
    )
    return second_block(
        x, meta_tokens_2, norm1_w_2, w_in_2, conv_w_2, diff_lambda_2, diff_subln_w_2,
        w_branch_2, w_out_2, norm2_w_2, w_up_2, w_down_2, final_norm_w_2,
    )


_drawn_inputs = setup_inputs


def setup_inputs(seed=0):
    import zlib

    import numpy as np

    out = dict(_drawn_inputs(seed))
    spreads = {}
    factors = {'gla_gate_b': 8.0,
     'gla_out_norm': 2.89,
     'dsa_q_norm': 8.0,
     'dsa_k_norm': 8.0,
     'sb_q_norm': 6.277,
     'sb_k_norm': 6.545,
     'diff_lambda_2': 6.458,
     'diff_subln_w_2': 7.854,
     'norm2_w_2': 3.494,
     'final_norm_w_2': 2.838}
    for name, (base, spread) in spreads.items():
        noise = np.random.default_rng([zlib.crc32(name.encode()), seed]).standard_normal(out[name].shape)
        drawn = base * np.exp(spread * noise) if base else spread * noise
        out[name] = __import__('jax').numpy.asarray(drawn.astype(out[name].dtype))
    for name, factor in factors.items():
        out[name] = (out[name] * factor).astype(out[name].dtype)
    return out
```

```python
import numpy as np
from contextlib import ExitStack
import concourse.bass as bass
from concourse import mybir

F32 = mybir.dt.float32
I32 = mybir.dt.int32
ALU = mybir.AluOpType
ACT = mybir.ActivationFunctionType
AX = mybir.AxisListType.X

P = 128
D = 1024
KC = D // P
S = 512
NT = S // P
META = 16
SM = S + META
UNIT = 1024
RING = 4
DEPTH = 2
D_FF = 2816
FF = D_FF // P
FFU = 3
D_FF2 = 4096
FF2 = D_FF2 // P
GH, GDK, GDV, GRANK, GCH = 4, 64, 128, 16, 64
NCH = S // GCH
DH = 4
IH, IDIM = 8, 64
TOPK = 128
RH, RDV = 4, 256
FH, FHD = 8, 64
EPS = 1e-6
IDX_SCALE = (IH ** -0.5) * (IDIM ** -0.5)
HEAD_SCALE = 128.0 ** -0.5
LAM_INIT = 0.8 - 0.6 * 1.0
NEG = -1.0e30
TAKEN = -3.0e38
WINDOWS = (2, 4, 8, 16)

_C = {}


def _lay(table, *items):
    at = 0
    for name, width in items:
        table[name] = (at, at + width)
        at += width
    return at


NC_A = _lay(_C, ("ident", P), ("swap128", P), ("swap64", P), ("tri_bias", P), ("gla_mask", P),
            ("after", P), ("strict", P), ("chunk_carry", S), ("invf", 2), ("sign", 2), ("pool_rc", 64))
_E = {}
NC_B = _lay(_E, ("decay", RH * SM), ("dist", SM))
_V = {}
NV = _lay(_V, ("mix_norm", 2 * KC), ("ffn_norm", 2 * KC), ("ada_b", 2 * 48), ("c", KC), ("gate_b", 2),
          ("gla_out", 1), ("dsa_q", 1), ("dsa_k", 1), ("pool_scale", 4), ("sb_q", 1), ("sb_k", 1),
          ("norm1", KC), ("conv", 3 * KC), ("subln", 1), ("norm2", KC), ("final", KC), ("lam", 4))

ADA_UNITS = 4
ADA_FIRST = 2 * D // S
ADA_REST = DEPTH * 6 * D // S - ADA_FIRST
ADA_ADDS = 2 * ADA_UNITS - 1

ADA_SUMS = {place: (g, b) for g, (place, b) in enumerate([
    (("gr", 1), 7), (("gr", 3), 7), (("gv", 1), 0), (("gv", 3), 0),
    (("qk", 1), 5), (("qk", 3), 5), (("qk", 6), 5), (("qk", 8), 5), (("qk", 11), 5), (("dv", 1), 0),
    (("head", 1), 7), (("head", 3), 7), (("rel", 4), 7), (("rel", 12), 7), (("rel", 20), 7),
    (("dsa", 1), 0), (("dsa", 4), 0), (("dsa", 7), 0), (("dsa", 10), 0), (("dsa", 13), 0)])}
assert len(ADA_SUMS) == ADA_REST

N_UNITS = (ADA_FIRST * ADA_UNITS + 30 + KC + 16 + KC + 2 * (2 * FF + KC * FFU) + 72 + 3 * 2 * KC + KC + FF2 + KC * FF2 // 8)


def build(nc, A, plan):
    ctx = ExitStack()
    with ctx:
        def sb(name, shape, dt=F32):
            return ctx.enter_context(nc.sbuf_tensor(name, shape, dt))

        sems = {}

        def sem(name):
            if name not in sems:
                sems[name] = ctx.enter_context(nc.semaphore(name))
            return sems[name]

        filled = [sem(f"filled{s}") for s in range(RING)]
        emptied = [sem(f"emptied{s}") for s in range(RING)]
        full = [sem(f"full{b}") for b in range(8)]
        drained = [sem(f"drained{b}") for b in range(8)]

        ring = sb("ring", [P, RING, UNIT])
        xres = sb("xres", [P, KC, S])
        hbuf = sb("hbuf", [P, KC, SM])
        consts = sb("consts", [P, NC_A])
        vecs = sb("vecs", [P, NV])
        mod = sb("mod", [P, 2 * 48])
        coef = sb("coef", [P, KC])
        ones = sb("ones", [P, P])
        small = sb("small", [P, 64])
        sq = sb("sq", [P, 2, S])
        rs = sb("rs", [P, 2, S])
        gate = sb("gate", [P, 2, S])
        cond = sb("cond", [P, KC])
        gate_up = sb("gate_up", [GRANK, GH * GDK])
        metaT = sb("metaT", [P, KC, META])
        lamp = sb("lamp", [FHD, 2])
        BIG = 34800
        big = sb("big", [P, BIG])
        ps = ctx.enter_context(nc.psum_tensor("ps", [P, 8, S], F32))

        def C(name):
            return consts[:, _C[name][0]:_C[name][1]]

        def V(name, i=0, n=1):
            a = _V[name][0] + i
            return vecs[:, a:a + n]

        def area(start, *items):
            out, at = {}, start
            for name, *dims in items:
                n = int(np.prod(dims))
                v = big[:, at:at + n]
                if len(dims) == 2:
                    v = v.rearrange("p (a b) -> p a b", b=dims[1])
                elif len(dims) == 3:
                    v = v.rearrange("p (a b c) -> p a b c", b=dims[1], c=dims[2])
                out[name] = v
                at += n
            assert at <= BIG, at
            return out, at

        eps_col, one_col = small[:, 0:1], small[:, 1:2]
        neg_lam, subln_s, sbq_s = small[:, 2:3], small[:, 3:4], small[:, 4:5]
        lam_e = small[:, 6:8]

        L0, at0 = area(0, ("mix", KC, S), ("cos128", S), ("sin128", S), ("cos64", S), ("sin64", S),
                     ("gk", 2, S), ("gq", 2, S), ("gr", 4, S), ("gv", NT, S), ("qk", 8, S), ("dv", NT, S),
                     ("idx", 5, S), ("iw", 3, IH), ("glow", S))
        G, _ = area(at0, ("gb", 2, S), ("gL", 2, S), ("eb", 2, S), ("QD", 2, S), ("KD", 2, S),
                    ("kd_tm", NT, 2 * P), ("st", 2, NCH, P), ("att", 4, P), ("o", 2, S), ("dec", 2, NCH),
                    ("ada_acc", 2, S), ("ada_w", 2, 2, S))
        ada_first = G["st"].rearrange("p a b c -> p (a b c)").rearrange("p (a b) -> p a b", b=S)
        QD, KD = G["QD"], G["KD"]
        T, _ = area(at0, ("keep", NT, S), ("rel", 2, S), ("P", 2, S), ("PT", 2, S), ("stat", 2, 4),
                    ("score", S), ("top", 8))
        L1, at1 = area(0, ("mix", KC, S), ("qk", 8, S), ("sv", NT, S), ("u", 4, SM), ("s", 2, SM),
                       ("pooled", 2, S), ("poolw", 4, P))
        poolw = L1["poolw"]
        B1, _ = area(at1, ("L", 4, S), ("nl", 4, S), ("lb", 4, S), ("w", 4, S))
        HID, _ = area(0, ("hid", FF2, S))
        RET, atr = area(0, ("rq", 4, S), ("rk", 4, SM), ("rg", 8, S), ("rv", NT, D), ("rvm", D),
                        ("merged", KC, S))
        DF, atd = area(atr, ("dq", 8, S), ("dk", 8, SM), ("dv", NT, D), ("dvm", D))
        R2, _ = area(atd, ("decay", RH, SM), ("dist", SM), ("sT", 2, S))
        F2, atf = area(0, ("L", 2, 2, SM), ("PT", 2, S), ("PTm", 2, P), ("stat", 2, 8))
        OD, _ = area(4 * S + 4 * SM + 8 * S, ("od", 8, S))
        assert atf <= 4 * S + 4 * SM
        CV, _ = area(atr, ("u", 2, SM), ("cv", KC, S))

        uses = {}
        full_count = {}
        by_unit = {}

        def ready(eng, name, i=None):
            b, k = uses[name]
            if name in by_unit:
                s, n, step = by_unit[name]
                eng.wait_ge(emptied[s], n if i is None else i * step + n)
            else:
                eng.wait_ge(full[b], full_count[name])
            return b

        def was_drained(eng, name, i=None):
            b, k = uses[name]
            eng.wait_ge(drained[b], k + 1 if i is None else i + (k + 1))

        def x_chunk(eng, st, k):
            b, use = uses[(st, "y", k % 4)]
            eng.wait_ge(drained[b], use + k // 4 + 1)

        block = ctx.enter_context(nc.Block())
        units = []
        state = {"u": 0}
        nuse = [0] * 8
        nfull = [0] * 8

        @block.tensor
        def _(pe):
            def claim(b, name, unit_ends=False):
                if nuse[b]:
                    pe.wait_ge(drained[b], nuse[b])
                uses[name] = (b, nuse[b])
                nuse[b] += 1
                if not unit_ends:
                    nfull[b] += 1
                    full_count[name] = nfull[b]

            def with_unit(*names):
                u = state["u"] - 1
                for name in names:
                    by_unit[name] = (u % RING, u // RING + 1, 0)

            def unit():
                u = state["u"]
                state["u"] += 1
                pe.wait_ge(filled[u % RING], 16 * (u // RING + 1))
                return u % RING

            def stream(name, first, count):
                units.append((name, first, count))

            def fm_tile(name, b, rhs, cols=P, col0=0):
                claim(b, name, True)
                s = unit()
                with_unit(name)
                for k in range(KC):
                    mm = pe.matmul(ps[0:cols, b, :], ring[:, s, k * P + col0:k * P + col0 + cols], rhs(k),
                                   start=k == 0, stop=k == KC - 1)
                mm.then_inc(emptied[s], 1)

            def wide_tile(name, b):
                claim(b, (name, 0), True)
                claim(b + 1, (name, 1), True)
                s = unit()
                with_unit((name, 0), (name, 1))
                for k in range(KC):
                    for n in range(2):
                        mm = pe.matmul(ps[:, b + n, 0:SM // 2], ring[:, s, k * P:(k + 1) * P],
                                       hbuf[:, k, n * SM // 2:(n + 1) * SM // 2],
                                       start=k == 0, stop=k == KC - 1)
                mm.then_inc(emptied[s], 1)

            def tm_group(name, off, meta=None):
                for i in range(NT):
                    claim(4 + i, (name, i), True)
                if meta is not None:
                    claim(meta, (name, "m"), True)
                for j in range(4):
                    s = unit()
                    for kk in range(2):
                        k = 2 * j + kk
                        w = ring[:, s, kk * S:(kk + 1) * S]
                        for i in range(NT):
                            mm = pe.matmul(ps[:, 4 + i, :], hbuf[:, k, off + i * P:off + (i + 1) * P], w,
                                           start=k == 0, stop=k == KC - 1)
                        if meta is not None:
                            mm = pe.matmul(ps[0:META, meta, :], hbuf[:, k, 0:META], w,
                                           start=k == 0, stop=k == KC - 1)
                    mm.then_inc(emptied[s], 1)
                    ada_sum(name, j)
                with_unit(*[(name, i) for i in (*range(NT), *(["m"] if meta is not None else []))])

            def column_sum(name, b, src, sem_in, count, n=S):
                claim(b, name)
                pe.wait_ge(sem_in, count)
                pe.matmul(ps[:, b, 0:n], ones[:, :], src, start=True, stop=True).then_inc(full[b], 1)

            def norm_sum(st, n=S):
                claim(6, (st, "ss"))
                for k in range(KC):
                    pe.wait_ge(sem(st + "_squared"), k + 1)
                    mm = pe.matmul(ps[:, 6, 0:n], ones[:, :], sq[:, k % 2, 0:n], start=k == 0, stop=k == KC - 1)
                    if k < KC - 1:
                        mm.then_inc(sem(st + "_summed"), 1)
                mm.then_inc(full[6], 1)

            def h_of(st, off=0):
                def f(k):
                    return hbuf[:, k, off:off + S]
                return f

            loop = {}

            def ring_loop(n_iter, per_iter):
                assert per_iter % RING == 0
                base = state["u"]
                state["u"] += n_iter * per_iter
                loop.update(base=base, step=per_iter // RING)

                def slot(i, n):
                    u = base + n
                    pe.wait_ge(filled[u % RING], i * (16 * per_iter // RING) + 16 * (u // RING + 1))
                    return u % RING
                return slot

            def bank_loop(n_iter, banks, names, per_result=1):
                base = {}
                for n, (b, name) in enumerate(zip(banks, names)):
                    uses[name] = (b, nuse[b])
                    u = loop["base"] + (n + 1) * per_result - 1
                    by_unit[name] = (u % RING, u // RING + 1, loop["step"])
                    base[b] = nuse[b]
                    nuse[b] += n_iter

                def take(i, b):
                    pe.wait_ge(drained[b], i + base[b])
                return take

            def ada_sum(*place):
                if place not in ADA_SUMS:
                    return
                g, b = ADA_SUMS[place]
                claim(b, ("ada", g), True)
                pe.wait_ge(sem("ada_added"), ADA_ADDS * (g + 1))
                for c in range(NT):
                    mm = pe.matmul(ps[:, b, c:c + 1], G["ada_acc"][:, g % 2, c * P:(c + 1) * P], ones[:, 0:1],
                                   start=True, stop=True)
                mm.then_inc(sem(f"ada_summed{g % 2}"), 1)

            stream("ada_first", 0, ADA_FIRST * ADA_UNITS)
            state["u"] += ADA_FIRST * ADA_UNITS
            norm_sum("n0")
            claim(7, "ada_first")
            for g in range(ADA_FIRST):
                pe.wait_ge(emptied[ADA_UNITS - 1], g + 1)
                for c in range(NT):
                    mm = pe.matmul(ps[:, 7, g * NT + c:g * NT + c + 1], ada_first[:, g, c * P:(c + 1) * P],
                                   ones[:, 0:1], start=True, stop=True, skip_group_check=True)
            mm.then_inc(full[7], 1)

            def ffn(st, layer):
                norm_sum(st)
                pe.wait_ge(sem(st + "_h"), KC)
                stream(f"w1_{layer}", 0, 2 * FF)
                slot = ring_loop(FF // 2, 4)
                take = bank_loop(FF // 2, range(4), [(st, "up", q) for q in range(4)])
                with pe.Fori(0, FF // 2) as i:
                    for q in range(4):
                        take(i, q)
                        s = slot(i, q)
                        for k in range(KC):
                            mm = pe.matmul(ps[:, q, :], ring[:, s, k * P:(k + 1) * P], hbuf[:, k, 0:S],
                                           start=k == 0, stop=k == KC - 1)
                        mm.then_inc(emptied[s], 1)
                stream(f"w2_{layer}", 0, KC * FFU)
                slot = ring_loop(2, 4 * FFU)
                for b in (1, 3):
                    pe.wait_ge(drained[b], nuse[b])
                take = bank_loop(2, range(4), [(st, "y", q) for q in range(4)], FFU)
                with pe.Fori(0, 2) as i:
                    for q in range(4):
                        take(i, q)
                        for f in range(FF):
                            if f % 8 == 0:
                                s = slot(i, FFU * q + f // 8)
                            mm = pe.matmul(ps[:, q, :], ring[:, s, (f % 8) * P:(f % 8 + 1) * P],
                                           HID["hid"][:, f, :], start=f == 0, stop=f == FF - 1)
                            if f % 8 == 7:
                                mm.then_inc(emptied[s], 1)
                        mm.then_inc(emptied[s], 1)

            def mix_out(st, name, mixv):
                stream(name, 0, KC)
                slot = ring_loop(2, 4)
                take = bank_loop(2, range(4), [(st, "y", q) for q in range(4)])
                with pe.Fori(0, 2) as i:
                    for q in range(4):
                        take(i, q)
                        s = slot(i, q)
                        for k in range(KC):
                            mm = pe.matmul(ps[:, q, :], ring[:, s, k * P:(k + 1) * P], mixv[:, k, :],
                                           start=k == 0, stop=k == KC - 1)
                        mm.then_inc(emptied[s], 1)

            pe.wait_ge(sem("n0_h"), KC)
            stream("ab", 0, 30)
            h = h_of("n0")
            claim(0, "glow")
            claim(1, "iw", True)
            s = unit()
            with_unit("iw")
            for k in range(KC):
                mm = pe.matmul(ps[0:GRANK, 0, :], ring[:, s, k * P:k * P + GRANK], h(k), start=k == 0, stop=k == KC - 1)
            mm.then_inc(full[0], 1)
            for i in range(1, NT):
                for k in range(KC):
                    mm = pe.matmul(ps[:, 1, (i - 1) * IH:i * IH], hbuf[:, k, i * P:(i + 1) * P],
                                   ring[:, s, k * P + GRANK:k * P + GRANK + IH], start=k == 0, stop=k == KC - 1)
            mm.then_inc(emptied[s], 1)
            for t in range(2):
                fm_tile(("gk", t), 2 + t, h)
            for p in range(2):
                claim(4 + p, ("gz", p))
                was_drained(pe, "glow")
                pe.wait_ge(sem("gate_up_loaded"), 16)
                pe.matmul(ps[:, 4 + p, :], gate_up[0:GRANK, p * P:(p + 1) * P], L0["glow"][0:GRANK, :],
                          start=True, stop=True).then_inc(full[4 + p], 1)
            for t in range(2):
                fm_tile(("gq", t), t, h)
            for t in range(4):
                fm_tile(("gr", t), (2 + t) % 4, h)
                ada_sum("gr", t)
            tm_group("gv", 0)

            def qk_sum(t):
                column_sum(("qk_ss", t), 6, sq[:, t % 2, :], sem("qk_squared"), t + 1)

            def qk_swap(t):
                claim(7, ("qk_swap", t))
                if t < 8:
                    pe.wait_ge(sem("qk_normed"), t + 1)
                    pe.matmul(ps[:, 7, :], C("swap128"), L0["qk"][:, t, :], start=True, stop=True).then_inc(full[7], 1)
                else:
                    was_drained(pe, ("qk", t))
                    pe.matmul(ps[:, 7, :], C("swap64"), L0["idx"][:, t - 8, :], start=True, stop=True).then_inc(full[7], 1)
            for t in range(15):
                if t < 13:
                    fm_tile(("qk", t), (2 + t) % 4, h)
                    ada_sum("qk", t)
                if 1 <= t <= 8:
                    qk_sum(t - 1)
                if 2 <= t:
                    qk_swap(t - 2)
            tm_group("dv", 0)

            pe.wait_ge(sem("gla_in"), 2)
            for p in range(2):
                claim(p, ("kdT", p))
                for i in range(NT):
                    mm = pe.transpose(ps[:, p, i * P:(i + 1) * P], KD[:, p, i * P:(i + 1) * P], C("ident"))
                mm.then_inc(full[p], 1)
            for p in range(2):
                was_drained(pe, ("kdT", p))
                for n in range(NCH - 1):
                    if n < 2:
                        claim(2 + n, ("kv", p, n))
                    r = (n % 2) * GCH
                    for hh in range(2):
                        head = 2 * p + hh
                        b, c = 2 + n % 2, (n // 2) * P
                        mm = pe.matmul(ps[hh * GDK:(hh + 1) * GDK, b, c:c + P],
                                       G["kd_tm"][r:r + GCH, n // 2, p * P + hh * GDK:p * P + (hh + 1) * GDK],
                                       L0["gv"][r:r + GCH, n // 2, head * GDV:(head + 1) * GDV],
                                       start=True, stop=True, skip_group_check=True)
                    if n >= NCH - 3:
                        mm.then_inc(full[2 + n % 2], 1)
            for head in range(GH):
                p, r = head // 2, (head % 2) * GDK
                claim(0, ("att", head))
                for i in range(NT):
                    mm = pe.matmul(ps[:, 0, i * P:(i + 1) * P], L0["gk"][r:r + GDK, p, i * P:(i + 1) * P],
                                   L0["gq"][r:r + GDK, p, i * P:(i + 1) * P], start=True, stop=True)
                mm.then_inc(full[0], 1)
                claim(4 + head % 2, ("go", head))
                was_drained(pe, ("att", head))
                was_drained(pe, ("kv", 1, 0))
                for i in range(NT):
                    pe.matmul(ps[:, 4 + head % 2, i * P:(i + 1) * P], L0["gv"][:, i, head * GDV:(head + 1) * GDV],
                              G["att"][:, i, :], start=True, stop=True, skip_group_check=True)
                    for n in (2 * i, 2 * i + 1):
                        if n:
                            mm = pe.matmul(ps[:, 4 + head % 2, n * GCH:(n + 1) * GCH],
                                           G["st"][r:r + GDK, p, n, :], QD[r:r + GDK, p, n * GCH:(n + 1) * GCH],
                                           start=False, stop=True, skip_group_check=True)
                mm.then_inc(full[4 + head % 2], 1)
                ada_sum("head", head)
                column_sum(("go_ss", head), 6, sq[:, head % 2, :], sem("go_squared"), head + 1)

            n = 0
            for i in range(1, NT):
                for hd in range(IH):
                    b = n % 2
                    r = (hd % 2) * IDIM
                    claim(b, ("rel", i, hd))
                    if n == 0:
                        pe.wait_ge(sem("qk_rotated"), 13)
                    pe.matmul(ps[:, b, 0:(i + 1) * P], L0["idx"][r:r + IDIM, hd // 2, i * P:(i + 1) * P],
                              L0["idx"][r:r + IDIM, 4, 0:(i + 1) * P], start=True, stop=True).then_inc(full[b], 1)
                    ada_sum("rel", n)
                    n += 1

            steps = [(i, hd) for i in range(NT) for hd in range(DH)]

            def dsa_scores(n):
                i, hd = steps[n]
                claim(2 + n % 2, ("dsa_s", n))
                pe.matmul(ps[:, 2 + n % 2, 0:(i + 1) * P], L0["qk"][:, hd, i * P:(i + 1) * P],
                          L0["qk"][:, 4 + hd, 0:(i + 1) * P], start=True, stop=True).then_inc(full[2 + n % 2], 1)

            def dsa_rest(n):
                i, hd = steps[n]
                claim(4 + n % 2, ("dsa_pt", n))
                pe.wait_ge(sem("dsa_probs"), n + 1)
                for j in range(i + 1):
                    mm = pe.transpose(ps[:, 4 + n % 2, j * P:(j + 1) * P], T["P"][:, n % 2, j * P:(j + 1) * P],
                                      C("ident"))
                mm.then_inc(full[4 + n % 2], 1)
                claim(6 + n % 2, ("dsa_o", n))
                was_drained(pe, ("dsa_pt", n))
                for j in range(i + 1):
                    mm = pe.matmul(ps[:, 6 + n % 2, 0:P], L0["dv"][:, j, hd * P:(hd + 1) * P],
                                   T["PT"][:, n % 2, j * P:(j + 1) * P], start=j == 0, stop=j == i)
                mm.then_inc(full[6 + n % 2], 1)
            for n in range(len(steps) + 1):
                if n < len(steps):
                    dsa_scores(n)
                if n:
                    dsa_rest(n - 1)
                ada_sum("dsa", n)
            pe.wait_ge(sem("gla_out_done"), GH)
            for n in (-2, -1):
                was_drained(pe, ("dsa_o", len(steps) + n))
            mix_out("m0", "ab_out", L0["mix"])
            ffn("f0", 0)

            norm_sum("n1")
            pe.wait_ge(sem("n1_h"), KC)
            stream("cd", 0, 16)
            for t in range(4):
                fm_tile(("u", t), t, h)
            for t in range(8):
                fm_tile(("sqk", t), t % 4, h)
                if t:
                    column_sum(("sqk_ss", t - 1), 6, sq[:, (t - 1) % 2, :], sem("sqk_squared"), t)
            column_sum(("sqk_ss", 7), 6, sq[:, 1, :], sem("sqk_squared"), 8)
            tm_group("sv", 0)
            for g in range(4):
                claim(7 - g % 2, ("py", g))
                pe.wait_ge(sem("pooled"), g + 1)
                pe.wait_ge(sem("pool_w_loaded"), 16)
                pe.matmul(ps[:, 7 - g % 2, :], poolw[:, g, :], L1["pooled"][:, g % 2, :],
                          start=True, stop=True).then_inc(full[7 - g % 2], 1)
            for hd in range(DH):
                for j in reversed(range(NT)):
                    claim(j, ("z", hd, j))
                    if hd == 0 and j == NT - 1:
                        pe.wait_ge(sem("sqk_normed"), 8)
                    pe.matmul(ps[:, j, 0:S - j * P], L1["qk"][:, 4 + hd, j * P:(j + 1) * P],
                              L1["qk"][:, hd, j * P:S], start=True, stop=True).then_inc(full[j], 1)
                for n, j in enumerate(reversed(range(NT))):
                    claim(4 + n % 2, ("aft", hd, j))
                    pe.wait_ge(sem("sb_nl"), NT * hd + n + 1)
                    mm = pe.matmul(ps[:, 4 + n % 2, 0:S - j * P], C("after"), B1["nl"][:, j, 0:S - j * P],
                                   start=True, stop=True)
                    for jj in range(j + 1, NT):
                        mm = pe.matmul(ps[:, 4 + n % 2, (jj - j) * P:S - j * P], ones[:, :],
                                       B1["nl"][:, jj, 0:S - jj * P], start=False, stop=True,
                                       skip_group_check=True)
                    mm.then_inc(full[4 + n % 2], 1)
                claim(6 + hd % 2, ("so", hd))
                pe.wait_ge(sem("sb_w"), NT * (hd + 1))
                for j in range(NT):
                    mm = pe.matmul(ps[:, 6 + hd % 2, j * P:S], L1["sv"][:, j, hd * P:(hd + 1) * P],
                                   B1["w"][:, j, 0:S - j * P], start=j == 0, stop=True,
                                   skip_group_check=True)
                mm.then_inc(full[6 + hd % 2], 1)
            was_drained(pe, ("py", 3))
            for hd in range(DH):
                was_drained(pe, ("so", hd))
            mix_out("m1", "cd_out", L1["mix"])
            ffn("f1", 1)

            norm_sum("mn", META)
            norm_sum("n2")
            pe.wait_ge(sem("mn_h"), KC)
            pe.wait_ge(sem("n2_h"), KC)
            h2 = h_of("n2", META)
            stream("in2", 0, 48)
            for t in range(4):
                fm_tile(("rq", t), t, h2)
            for t in range(4):
                wide_tile(("rk", t), 2 * (t % 2))
            for t in range(8):
                fm_tile(("rg", t), t % 4, h2)
            for g in range(2):
                tm_group(("rv", g), META, meta=g)
            for t in range(8):
                fm_tile(("dq", t), t % 4, h2)
            for t in range(8):
                wide_tile(("dk", t), 2 * (t % 2))
            for g in range(2):
                tm_group(("fv", g), META, meta=g)

            for hd in range(RH):
                for v in range(2):
                    claim(4 + v, ("ro", hd, v))
                for j in range(-1, NT):
                    n = 5 * hd + j + 1
                    q0, kp = (0, META) if j < 0 else (j * P, P)
                    k0 = 0 if j < 0 else META + j * P
                    claim(n % 2, ("rs", hd, j))
                    if n == 0:
                        pe.wait_ge(sem("tables2_loaded"), 16)
                    pe.matmul(ps[0:kp, n % 2, 0:S - q0], RET["rk"][:, hd, k0:k0 + kp], RET["rq"][:, hd, q0:S],
                              start=True, stop=True).then_inc(full[n % 2], 1)
                    was_drained(pe, ("rs", hd, j))
                    for v in range(2):
                        c = hd * RDV + v * P
                        vt = RET["rvm"][0:META, c:c + P] if j < 0 else RET["rv"][:, j, c:c + P]
                        mm = pe.matmul(ps[:, 4 + v, q0:S], vt, R2["sT"][0:kp, n % 2, 0:S - q0],
                                       start=j < 0, stop=True, skip_group_check=True)
                        if j == NT - 1:
                            mm.then_inc(full[4 + v], 1)
                        elif v == 1:
                            mm.then_inc(sem("ret_used"), 1)
                claim(6, ("rmu", hd))
                was_drained(pe, ("ro", hd, 1))
                for v in range(2):
                    mm = pe.matmul(ps[:, 6, :], ones[:, :], gate[:, v, :], start=v == 0, stop=v == 1)
                mm.then_inc(full[6], 1)
                claim(7, ("rvar", hd))
                pe.wait_ge(sem("ret_sq"), 2 * hd + 2)
                for v in range(2):
                    mm = pe.matmul(ps[:, 7, :], ones[:, :], sq[:, v, :], start=v == 0, stop=v == 1)
                mm.then_inc(full[7], 1)

            def branch(st, src, uname, src_done):
                stream(uname, 0, 2 * KC)
                src_done()
                slot = ring_loop(KC // 2, 4)
                take = bank_loop(KC // 2, range(4), [(st, "b", q) for q in range(4)])
                with pe.Fori(0, KC // 2) as i:
                    for q in range(4):
                        take(i, q)
                        s = slot(i, q)
                        for k in range(KC):
                            rhs = src[:, k, :] if q % 2 else hbuf[:, k, META:SM]
                            mm = pe.matmul(ps[:, q, :], ring[:, s, k * P:(k + 1) * P], rhs,
                                           start=k == 0, stop=k == KC - 1)
                        mm.then_inc(emptied[s], 1)
            branch("br0", RET["rg"], "br0", lambda: pe.wait_ge(sem("ret_out"), 8))

            claim(7, "lam")
            pe.wait_ge(sem("lam_prod"), 1)
            pe.matmul(ps[:, 7, 0:2], ones[0:FHD, :], lamp[0:FHD, :], start=True, stop=True).then_inc(full[7], 1)
            fsteps = [(hd, i) for hd in range(FH) for i in range(NT)]

            def diff_scores(n):
                hd, i = fsteps[n]
                if n == 0:
                    for b in (1, 3):
                        pe.wait_ge(drained[b], nuse[b])
                claim(0, ("fs", n))
                for m in range(2):
                    r = m * FHD
                    q = DF["dq"][r:r + FHD, hd, i * P:(i + 1) * P]
                    mm = pe.matmul(ps[:, m, 0:(i + 1) * P], q, DF["dk"][r:r + FHD, hd, META:META + (i + 1) * P],
                                   start=True, stop=True)
                mm.then_inc(full[0], 1)
                claim(2, ("fsm", n))
                for m in range(2):
                    r = m * FHD
                    q = DF["dq"][r:r + FHD, hd, i * P:(i + 1) * P]
                    mm = pe.matmul(ps[:, 2 + m, 0:META], q, DF["dk"][r:r + FHD, hd, 0:META],
                                   start=True, stop=True)
                mm.then_inc(full[2], 1)

            def diff_rest(n):
                hd, i = fsteps[n]
                claim(4, ("fpt", n))
                claim(5, ("fptm", n))
                pe.wait_ge(sem("diff_probs"), n + 1)
                src = F2["L"][:, n % 2, 0, :]
                for j in range(i + 1):
                    mm = pe.transpose(ps[:, 4, j * P:(j + 1) * P], src[:, META + j * P:META + (j + 1) * P], C("ident"))
                mm.then_inc(full[4], 1)
                pe.transpose(ps[0:META, 5, 0:P], src[:, 0:META], C("ident")).then_inc(full[5], 1)
                if i == 0:
                    claim(6 + hd % 2, ("fo", hd))
                was_drained(pe, ("fptm", n))
                o = ps[:, 6 + hd % 2, i * P:(i + 1) * P]
                pe.matmul(o, DF["dvm"][0:META, hd * P:(hd + 1) * P], F2["PTm"][0:META, n % 2, :],
                          start=True, stop=True, skip_group_check=True)
                for j in range(i + 1):
                    mm = pe.matmul(o, DF["dv"][:, j, hd * P:(hd + 1) * P], F2["PT"][:, n % 2, j * P:(j + 1) * P],
                                   start=False, stop=True, skip_group_check=True)
                if i == NT - 1:
                    mm.then_inc(full[6 + hd % 2], 1)
                else:
                    mm.then_inc(sem("diff_pv"), 1)
            for n in range(len(fsteps) + 1):
                if n < len(fsteps):
                    diff_scores(n)
                if n:
                    diff_rest(n - 1)
                    hd, i = fsteps[n - 1]
                    if i == 0 and hd:
                        column_sum(("fo_ss", hd - 1), 5, sq[:, (hd - 1) % 2, :], sem("fo_squared"), hd)
            column_sum(("fo_ss", FH - 1), 5, sq[:, (FH - 1) % 2, :], sem("fo_squared"), FH)
            branch("br1", OD["od"], "br1", lambda: pe.wait_ge(sem("diff_out"), FH))

            stream("in2", 48, 24)
            for t in range(8):
                wide_tile(("cc", t), 0)
                wide_tile(("cx", t), 2)
                fm_tile(("cb", t), 4 + t % 2, h2)
            branch("br2", CV["cv"], "br2", lambda: was_drained(pe, ("cb", KC - 1)))
            for b in (1, 3):
                pe.wait_ge(drained[b], nuse[b])
            mix_out("m2", "w_out2", RET["merged"])

            norm_sum("f2")
            pe.wait_ge(sem("f2_h"), KC)
            stream("up2", 0, FF2)
            slot = ring_loop(FF2 // 4, 4)
            take = bank_loop(FF2 // 4, range(4), [("f2", "up", q) for q in range(4)])
            with pe.Fori(0, FF2 // 4) as i:
                for q in range(4):
                    take(i, q)
                    s = slot(i, q)
                    for k in range(KC):
                        mm = pe.matmul(ps[:, q, :], ring[:, s, k * P:(k + 1) * P], hbuf[:, k, 0:S],
                                       start=k == 0, stop=k == KC - 1)
                    mm.then_inc(emptied[s], 1)
            stream("down2", 0, KC * 4)
            slot = ring_loop(2, 16)
            pe.wait_ge(sem("f2_hid"), FF2)
            take = bank_loop(2, range(4), [("f2", "y", q) for q in range(4)], 4)
            with pe.Fori(0, 2) as i:
                for q in range(4):
                    take(i, q)
                    for f in range(FF2):
                        if f % 8 == 0:
                            s = slot(i, 4 * q + f // 8)
                        mm = pe.matmul(ps[:, q, :], ring[:, s, (f % 8) * P:(f % 8 + 1) * P],
                                       HID["hid"][:, f, :], start=f == 0, stop=f == FF2 - 1)
                        if f % 8 == 7:
                            mm.then_inc(emptied[s], 1)
            norm_sum("nf")

        n_units = sum(c for _, _, c in units)
        assert n_units == state["u"] == N_UNITS, (n_units, state["u"])
        stream_dram = A["stream"]
        plan.extend(units)

        @block.sync
        def _(sp):
            for s in range(RING):
                sp.dma_start(ring[:, s, :], stream_dram[s, :, :]).then_inc(filled[s], 16)
            with sp.Fori(1, n_units // RING) as i:
                for s in range(RING):
                    sp.wait_ge(emptied[s], i)
                    sp.dma_start(ring[:, s, :], stream_dram[i * RING + s, :, :]).then_inc(filled[s], 16)
            for s in range(n_units % RING):
                sp.wait_ge(emptied[s], n_units // RING)
                sp.dma_start(ring[:, s, :], stream_dram[n_units - n_units % RING + s, :, :]).then_inc(filled[s], 16)
            for k in range(KC):
                sp.wait_ge(sem("nf_h"), k + 1)
                sp.dma_start(A["out"][:, k, :], hbuf[:, k, 0:S]).then_inc(sem("stored"), 16)
            sp.wait_ge(sem("stored"), 16 * KC)

        @block.scalar
        def _(act):
            chain = [0]

            def link(ins):
                chain[0] += 1
                ins.then_inc(sem("act_chain"), 1)
                act.wait_ge(sem("act_chain"), chain[0])

            def f(out, in_, func, **kw):
                return act.activation(out, in_, func, **kw)

            def drain(ins, b):
                return ins.then_inc(drained[b], 1)

            def drain_link(ins, name):
                drain(ins, uses[name][0])
                was_drained(act, name)

            act.dma_start(vecs[:, :], A["vecs"]).then_inc(sem("vecs_loaded"), 16)
            act.dma_start(consts[:, :], A["consts"]).then_inc(sem("consts_loaded"), 16)
            act.dma_start(L0["mix"][:, 0, :].bitcast(I32), A["positions"].partition_broadcast(P)).then_inc(sem("pos_loaded"), 16)
            act.dma_start(xres[:, :, :], A["x"]).then_inc(sem("x_loaded"), 16)
            act.dma_start(gate_up[:, :], A["gate_up"]).then_inc(sem("gate_up_loaded"), 16)
            act.dma_start(metaT[:, :, :], A["meta"]).then_inc(sem("meta_loaded"), 16)
            act.wait_ge(sem("vecs_loaded"), 16)
            f(cond[:, :], V("c", 0, KC), ACT.Silu).then_inc(sem("cond_ready"), 1)
            def tables():
                act.preload_act_table_set("natural_log_exp_and_others")

            def rstd(out, name, count, done):
                b = ready(act, name)
                drain_link(f(out, ps[:, b, 0:out.shape[-1]], ACT.Ln, scale=1.0 / count, bias=eps_col), name)
                f(out, out, ACT.Exp, scale=-0.5).then_inc(done, 1)

            def norm(st, src, ready_k, n=S):
                for k in range(KC):
                    ready_k(k)
                    if k >= 2:
                        act.wait_ge(sem(st + "_summed"), k - 1)
                    f(sq[:, k % 2, 0:n], src[:, k, :], ACT.Square).then_inc(sem(st + "_squared"), 1)
                rstd(rs[:, 0, 0:n], (st, "ss"), D, sem(st + "_rs"))

            def ffn(st):
                with act.Fori(0, FF // 2) as i:
                    for p in range(2):
                        g, u = (st, "up", 2 * p), (st, "up", 2 * p + 1)
                        b = ready(act, g, i)
                        act.wait_ge(drained[uses[u][0]], i + uses[u][1])
                        drain(f(gate[:, p, :], ps[:, b, :], ACT.Silu), b)

            act.wait_ge(sem("small_ready"), 1)
            act.wait_ge(sem("x_loaded"), 16)
            tables()
            norm("n0", xres, lambda k: None)
            b = ready(act, "glow")
            drain(f(L0["glow"][0:GRANK, :], ps[0:GRANK, b, :], ACT.Copy), b)
            b = ready(act, "iw")
            drain(f(L0["iw"].rearrange("p a b -> p (a b)"), ps[:, b, 0:3 * IH], ACT.Copy, scale=IDX_SCALE), b)
            for t in range(2):
                b = ready(act, ("gk", t))
                drain(f(L0["gk"][:, t, :], ps[:, b, :], ACT.Copy), b)
            for p in range(2):
                b = ready(act, ("gz", p))
                f(G["gL"][:, p, :], ps[:, b, :], ACT.Abs, bias=V("gate_b", p)).then_inc(sem("gz_abs"), 1)
            for t in range(2):
                b = ready(act, ("gq", t))
                drain(f(L0["gq"][:, t, :], ps[:, b, :], ACT.Copy, scale=GDK ** -0.5), b)
            for n, name in enumerate(("sin128", "cos128", "sin64", "cos64")):
                act.wait_ge(sem("angles"), n + 1)
                sc = C("sign")[:, n // 2:n // 2 + 1] if n % 2 == 0 else 1.0
                f(L0[name], L0[name], ACT.Sin, scale=sc).then_inc(sem("rope_tables"), 1)

            def ada_out(*place):
                if place not in ADA_SUMS:
                    return
                g, b = ADA_SUMS[place]
                act.wait_ge(sem(f"ada_summed{g % 2}"), g // 2 + 1)
                drain(f(mod[:, (ADA_FIRST + g) * NT:(ADA_FIRST + g + 1) * NT], ps[:, b, 0:NT], ACT.Copy), b)
            for t in range(4):
                b = ready(act, ("gr", t))
                drain(f(L0["gr"][:, t, :], ps[:, b, :], ACT.Silu), b)
                ada_out("gr", t)
            for j in range(4):
                ada_out("gv", j)
            tables()
            for p in range(2):
                act.wait_ge(sem("gz_abs"), p + 1)
                link(f(G["gL"][:, p, :], G["gL"][:, p, :], ACT.Exp, scale=-1.0))
                f(G["gL"][:, p, :], G["gL"][:, p, :], ACT.Ln, bias=one_col).then_inc(sem("gate_ln"), 1)
            for p in range(2):
                act.wait_ge(sem("gla_diffs"), p + 1)
                f(QD[:, p, :], G["gL"][:, p, :], ACT.Exp, scale=1.0 / 16.0)
                f(KD[:, p, :], KD[:, p, :], ACT.Exp, scale=1.0 / 16.0)
                f(G["gb"][:, p, :], G["eb"][:, p, :], ACT.Exp, scale=1.0 / 16.0)
                f(G["dec"][:, p, :], G["gL"][:, p, GCH - 1:S:GCH], ACT.Exp, scale=1.0 / 16.0)
                f(G["eb"][:, p, :], G["eb"][:, p, :], ACT.Exp, scale=-1.0 / 16.0).then_inc(sem("gla_exps"), 1)

            def qk_rstd(t):
                if t >= 2:
                    act.wait_ge(sem("qk_normed"), t - 1)
                rstd(rs[:, t % 2, :], ("qk_ss", t), P, sem("qk_rs"))
            for t in range(13):
                b = ready(act, ("qk", t))
                if t < 8:
                    drain_link(f(L0["qk"][:, t, :], ps[:, b, :], ACT.Copy), ("qk", t))
                    if t == 0:
                        act.wait_ge(sem("n0_h"), KC)
                    if t >= 2:
                        ready(act, ("qk_ss", t - 2))
                    f(sq[:, t % 2, :], L0["qk"][:, t, :], ACT.Square).then_inc(sem("qk_squared"), 1)
                else:
                    drain(f(L0["idx"][:, t - 8, :], ps[:, b, :], ACT.Copy), b)
                ada_out("qk", t)
                if 1 <= t <= 8:
                    qk_rstd(t - 1)
            for j in range(4):
                ada_out("dv", j)
            for p in range(2):
                b = ready(act, ("kdT", p))
                drain(f(G["kd_tm"][:, :, p * P:(p + 1) * P], ps[:, b, :].rearrange("p (i c) -> p i c", c=P), ACT.Copy),
                      b)
            act.wait_ge(sem("qk_normed"), 8)
            for head in range(GH):
                b = ready(act, ("go", head))
                if head >= 2:
                    act.wait_ge(sem("gla_out_done"), head - 1)
                    ready(act, ("go_ss", head - 2))
                drain_link(f(G["o"][:, head % 2, :], ps[:, b, :], ACT.Copy), ("go", head))
                f(sq[:, head % 2, :], G["o"][:, head % 2, :], ACT.Square).then_inc(sem("go_squared"), 1)
                ada_out("head", head)
                rstd(rs[:, head % 2, :], ("go_ss", head), P, sem("go_rs"))
            n = 0
            for i in range(1, NT):
                for hd in range(IH):
                    b = ready(act, ("rel", i, hd))
                    if n == 0:
                        act.wait_ge(sem("gla_out_done"), GH)
                    if n >= 2:
                        act.wait_ge(sem("idx_added"), n - 1)
                    drain(f(T["rel"][:, n % 2, 0:(i + 1) * P], ps[:, b, 0:(i + 1) * P], ACT.Relu), b)
                    ada_out("rel", n)
                    n += 1

            def dsa_exp(n):
                w = (n // DH + 1) * P
                act.wait_ge(sem("dsa_max"), n + 1)
                f(T["P"][:, n % 2, 0:w], T["P"][:, n % 2, 0:w], ACT.Exp, bias=T["stat"][:, n % 2, 0:1],
                  accum_out=T["stat"][:, n % 2, 1:2]).then_inc(sem("dsa_exp"), 1)

            def dsa_pt(n):
                w = (n // DH + 1) * P
                b = ready(act, ("dsa_pt", n))
                if n >= 2:
                    ready(act, ("dsa_o", n - 2))
                drain(f(T["PT"][:, n % 2, 0:w], ps[:, b, 0:w], ACT.Copy), b)

            def dsa_out(n):
                i, hd = n // DH, n % DH
                b = ready(act, ("dsa_o", n))
                drain(f(L0["mix"][:, 4 + hd, i * P:(i + 1) * P], ps[:, b, 0:P], ACT.Copy), b)
            NS = NT * DH
            for n in range(NS + 2):
                if n < NS:
                    dsa_exp(n)
                if 1 <= n <= NS:
                    dsa_pt(n - 1)
                ada_out("dsa", n)
                if n >= 2:
                    dsa_out(n - 2)
            norm("f0", xres, lambda k: x_chunk(act, "m0", k))
            ffn("f0")

            act.wait_ge(sem("n1_free"), 1)
            act.dma_start(big[:, atd:atd + NC_B], A["tables2"]).then_inc(sem("tables2_loaded"), 16)
            act.dma_start(poolw[:, :, :], A["pool_w"]).then_inc(sem("pool_w_loaded"), 16)
            tables()
            norm("n1", xres, lambda k: x_chunk(act, "f0", k))
            for t in range(4):
                b = ready(act, ("u", t))
                drain(f(L1["u"][:, t, META:SM], ps[:, b, :], ACT.Copy), b)

            def sqk_rstd(t):
                if t >= 2:
                    act.wait_ge(sem("sqk_normed"), t - 1)
                rstd(rs[:, t % 2, :], ("sqk_ss", t), P, sem("sqk_rs"))
            for t in range(8):
                b = ready(act, ("sqk", t))
                drain_link(f(L1["qk"][:, t, :], ps[:, b, :], ACT.Copy), ("sqk", t))
                if t == 0:
                    act.wait_ge(sem("n1_h"), KC)
                if t >= 2:
                    ready(act, ("sqk_ss", t - 2))
                f(sq[:, t % 2, :], L1["qk"][:, t, :], ACT.Square).then_inc(sem("sqk_squared"), 1)
                if t:
                    sqk_rstd(t - 1)
            sqk_rstd(7)
            for g in range(4):
                b = ready(act, ("py", g))
                drain(f(L1["mix"][:, g, :], ps[:, b, :], ACT.Copy, scale=V("pool_scale", g)), b)
            for hd in range(DH):
                for j in reversed(range(NT)):
                    w = S - j * P
                    b = ready(act, ("z", hd, j))
                    if hd:
                        act.wait_ge(sem("sb_nl"), NT * hd)
                    link(f(B1["L"][:, j, 0:w], ps[:, b, 0:w], ACT.Abs))
                    link(f(B1["L"][:, j, 0:w], B1["L"][:, j, 0:w], ACT.Exp, scale=-1.0))
                    f(B1["L"][:, j, 0:w], B1["L"][:, j, 0:w], ACT.Ln, bias=one_col).then_inc(sem("sb_ln"), 1)
                if hd:
                    b = ready(act, ("so", hd - 1))
                    drain(f(L1["mix"][:, 4 + hd - 1, :], ps[:, b, :], ACT.Copy), b)
                for n, j in enumerate(reversed(range(NT))):
                    w = S - j * P
                    was_drained(act, ("aft", hd, j))
                    f(B1["w"][:, j, 0:w], B1["lb"][:, j, 0:w], ACT.Exp).then_inc(sem("sb_e"), 1)
            b = ready(act, ("so", DH - 1))
            drain(f(L1["mix"][:, 7, :], ps[:, b, :], ACT.Copy), b)
            norm("f1", xres, lambda k: x_chunk(act, "m1", k))
            ffn("f1")

            act.wait_ge(sem("meta_loaded"), 16)
            x_chunk(act, "f1", KC - 1)
            tables()
            norm("mn", metaT, lambda k: None, META)
            act.wait_ge(sem("mn_h"), KC)
            norm("n2", xres, lambda k: x_chunk(act, "f1", k))
            for t in range(4):
                b = ready(act, ("rq", t))
                drain(f(RET["rq"][:, t, :], ps[:, b, :], ACT.Copy), b)

            def wide(dst, name, scale=1.0):
                for n in range(2):
                    b = ready(act, (name, n))
                    drain(f(dst[:, n * SM // 2:(n + 1) * SM // 2], ps[:, b, 0:SM // 2], ACT.Copy, scale=scale), b)
            for t in range(4):
                wide(RET["rk"][:, t, :], ("rk", t), HEAD_SCALE)
            for t in range(8):
                b = ready(act, ("rg", t))
                drain(f(RET["rg"][:, t, :], ps[:, b, :], ACT.Silu), b)
            tables()
            for t in range(8):
                b = ready(act, ("dq", t))
                drain(f(DF["dq"][:, t, :], ps[:, b, :], ACT.Copy, scale=FHD ** -0.5), b)
            for t in range(8):
                wide(DF["dk"][:, t, :], ("dk", t))
            for hd in range(RH):
                for v in range(2):
                    b = ready(act, ("ro", hd, v))
                    if hd:
                        act.wait_ge(sem("ret_out"), 2 * hd)
                    drain(f(gate[:, v, :], ps[:, b, :], ACT.Copy), b)
                for v in range(2):
                    if v:
                        was_drained(act, ("rmu", hd))
                    else:
                        act.wait_ge(sem("ret_yc"), hd + 1)
                    f(sq[:, v, :], gate[:, v, :], ACT.Square).then_inc(sem("ret_sq"), 1)
                rstd(rs[:, hd % 2, :], ("rvar", hd), RDV, sem("ret_rs"))

            def branch(st):
                with act.Fori(0, KC // 2) as i:
                    for p in range(2):
                        g, u = (st, "b", 2 * p), (st, "b", 2 * p + 1)
                        b = ready(act, g, i)
                        act.wait_ge(drained[uses[u][0]], i + uses[u][1])
                        drain(f(gate[:, p, :], ps[:, b, :], ACT.Sigmoid), b)
            act.wait_ge(sem("ret_out"), 8)
            branch("br0")
            b = ready(act, "lam")
            tables()
            drain(f(lam_e, ps[:, b, 0:2], ACT.Exp), b)

            def diff_exp(n):
                w = META + (n % NT + 1) * P
                act.wait_ge(sem("diff_max"), n + 1)
                for m in range(2):
                    ins = f(F2["L"][:, n % 2, m, 0:w], F2["L"][:, n % 2, m, 0:w], ACT.Exp,
                            bias=F2["stat"][:, n % 2, m:m + 1], accum_out=F2["stat"][:, n % 2, 2 + m:3 + m])
                ins.then_inc(sem("diff_exp"), 1)

            def diff_pt(n):
                w = (n % NT + 1) * P
                if n >= 2:
                    if (n - 2) % NT == NT - 1:
                        ready(act, ("fo", (n - 2) // NT))
                    else:
                        act.wait_ge(sem("diff_pv"), (NT - 1) * ((n - 2) // NT) + (n - 2) % NT + 1)
                b = ready(act, ("fpt", n))
                drain(f(F2["PT"][:, n % 2, 0:w], ps[:, b, 0:w], ACT.Copy), b)
                b = ready(act, ("fptm", n))
                drain(f(F2["PTm"][0:META, n % 2, :], ps[0:META, b, 0:P], ACT.Copy), b)

            def diff_square(hd):
                b = ready(act, ("fo", hd))
                if hd >= 2:
                    ready(act, ("fo_ss", hd - 2))
                drain_link(f(OD["od"][:, hd, :], ps[:, b, :], ACT.Copy), ("fo", hd))
                f(sq[:, hd % 2, :], OD["od"][:, hd, :], ACT.Square).then_inc(sem("fo_squared"), 1)

            def diff_rstd(hd):
                if hd >= 2:
                    act.wait_ge(sem("diff_out"), hd - 1)
                rstd(rs[:, hd % 2, :], ("fo_ss", hd), P, sem("fo_rs"))
            NF = FH * NT
            for n in range(NF + 1):
                if n < NF:
                    diff_exp(n)
                if n:
                    diff_pt(n - 1)
                    hd, i = (n - 1) // NT, (n - 1) % NT
                    if i == NT - 1:
                        diff_square(hd)
                    if i == 0 and hd:
                        diff_rstd(hd - 1)
            diff_rstd(FH - 1)
            act.wait_ge(sem("diff_out"), FH)
            branch("br1")
            for t in range(KC):
                if t >= 2:
                    was_drained(act, ("cb", t - 2))
                wide(CV["u"][:, t % 2, :], ("cc", t))
            branch("br2")
            tables()
            norm("f2", xres, lambda k: x_chunk(act, "m2", k))
            with act.Fori(0, FF2 // 4) as i:
                for q in range(4):
                    b = ready(act, ("f2", "up", q), i)
                    drain(f(gate[:, q % 2, :], ps[:, b, :], ACT.Relu), b)
                    was_drained(act, ("f2", "up", q), i)
                    f(HID["hid"][:, bass.ds(i * 4 + q, 1), :], gate[:, q % 2, :], ACT.Square).then_inc(sem("f2_hid"), 1)
            norm("nf", xres, lambda k: x_chunk(act, "f2", k))

        @block.gpsimd
        def _(pool):
            SLOTS = 2
            weights = G["ada_w"]

            def load(slot, unit):
                pool.dma_start(weights[:, slot, :, :], A["ada_rest"][unit, :, :, :]).then_inc(sem(f"ada_filled{slot}"), 16)

            def group(i, h, refill=ADA_UNITS, first=False):
                acc = G["ada_acc"][:, h, :]
                for j in range(ADA_UNITS):
                    slot = j % SLOTS
                    w = weights[:, slot, :, :]
                    pool.wait_ge(sem(f"ada_filled{slot}"), i * 64 + 16 * (2 * h + j // 2 + 1))
                    pool.tensor_tensor(w, w, cond[:, 2 * j:2 * j + 2].unsqueeze(2).broadcast_to((P, 2, S)), ALU.mult)                        .then_inc(sem("ada_scaled"), 1)
                    pool.wait_ge(sem("ada_scaled"), i * 8 + (4 * h + j + 1))
                    if j == 0:
                        if not first:
                            pool.wait_ge(sem(f"ada_summed{h}"), i)
                        pool.tensor_tensor(acc, w[:, 0, :], w[:, 1, :], ALU.add).then_inc(sem("ada_added"), 1)
                    else:
                        for kk in range(2):
                            pool.wait_ge(sem("ada_added"), i * (2 * ADA_ADDS) + (ADA_ADDS * h + 2 * j - 1 + kk))
                            pool.tensor_tensor(acc, acc, w[:, kk, :], ALU.add).then_inc(sem("ada_added"), 1)
                    if j < refill:
                        pool.wait_ge(sem("ada_added"), i * (2 * ADA_ADDS) + (ADA_ADDS * h + 2 * j + 1))
                        load(slot, i * 8 + (4 * h + j + SLOTS))
            pool.wait_ge(emptied[ADA_UNITS - 1], ADA_FIRST)
            for slot in range(SLOTS):
                load(slot, slot)
            for h in range(2):
                group(0, h, first=True)
            with pool.Fori(1, ADA_REST // 2 - 1) as i:
                for h in range(2):
                    group(i, h)
            group(ADA_REST // 2 - 1, 0)
            group(ADA_REST // 2 - 1, 1, refill=ADA_UNITS - SLOTS)

        @block.vector
        def _(dve):
            chain = [0]

            def link(ins):
                chain[0] += 1
                ins.then_inc(sem("dve_chain"), 1)
                dve.wait_ge(sem("dve_chain"), chain[0])

            def drain(ins, b):
                return ins.then_inc(drained[b], 1)

            def drain_link(ins, name):
                drain(ins, uses[name][0])
                was_drained(dve, name)

            tt, stt, ts = dve.tensor_tensor, dve.scalar_tensor_tensor, dve.tensor_scalar

            dve.memset(ones[:, :], 1.0)
            dve.memset(eps_col, EPS)
            link(dve.memset(one_col, 1.0))
            dve.wait_ge(sem("vecs_loaded"), 16)
            ts(subln_s, V("subln"), 1.0 - LAM_INIT, None, ALU.mult)
            ts(sbq_s, V("sb_q"), HEAD_SCALE, None, ALU.mult)
            tt(lamp[:, 0:1], V("lam", 0)[0:FHD], V("lam", 1)[0:FHD], ALU.mult)
            tt(lamp[:, 1:2], V("lam", 2)[0:FHD], V("lam", 3)[0:FHD], ALU.mult).then_inc(sem("lam_prod"), 1)
            dve.memset(G["att"], 0.0).then_inc(sem("small_ready"), 1)

            dve.wait_ge(sem("cond_ready"), 1)
            with dve.Fori(0, ADA_FIRST) as i:
                acc = ada_first[:, bass.ds(i, 1), :]
                for j in range(ADA_UNITS):
                    for kk in range(2):
                        w = ring[:, j:j + 1, kk * S:(kk + 1) * S]
                        ck = cond[:, 2 * j + kk:2 * j + kk + 1]
                        if kk == 0:
                            dve.wait_ge(filled[j], i * 16 + 16)
                        else:
                            dve.wait_ge(sem("ada_half"), i * ADA_UNITS + j + 1)
                        if j == kk == 0:
                            ins = ts(acc, w, ck, None, ALU.mult)
                        else:
                            if kk == 0:
                                dve.wait_ge(emptied[j - 1], i + 1)
                            ins = stt(acc, w, ck, acc, ALU.mult, ALU.add)
                        ins.then_inc(emptied[j] if kk else sem("ada_half"), 1)
            b = ready(dve, "ada_first")
            drain_link(tt(mod[:, 0:ADA_FIRST * NT], ps[:, b, 0:ADA_FIRST * NT], V("ada_b", 0, ADA_FIRST * NT), ALU.add),
                       "ada_first")

            def M(layer, part, k=0, n=1):
                a = layer * 48 + part * KC + k
                return mod[:, a:a + n]

            def norm(st, src, weight, dst, layer=None, part=0, n=S, src_ready=None):
                if layer is not None:
                    link(stt(coef[:, :], M(layer, part + 1, 0, KC), 1.0, weight, ALU.add, ALU.mult))
                    weight = coef[:, :]
                dve.wait_ge(sem(st + "_rs"), 1)
                for k in range(KC):
                    out = dst(k)
                    ins = stt(out, src[:, k, :], weight[:, k:k + 1], rs[:, 0, 0:n], ALU.mult, ALU.mult)
                    if layer is not None:
                        link(ins)
                        ins = ts(out, out, M(layer, part, k), None, ALU.add)
                    ins.then_inc(sem(st + "_h"), 1)

            def hd_(off=0, n=S):
                return lambda k: hbuf[:, k, off:off + n]

            def add_out(st, layer=None, part=0):
                with dve.Fori(0, 2) as i:
                    for q in range(4):
                        b = ready(dve, (st, "y", q), i)
                        xk = xres[:, bass.ds(i * 4 + q, 1), :]
                        y = ps[:, b:b + 1, :]
                        if layer is None:
                            drain(tt(xk, y, xk, ALU.add), b)
                        else:
                            g = mod[:, bass.ds(i * 4 + (layer * 48 + part * KC + q), 1)]
                            drain(stt(xk, y, g, xk, ALU.mult, ALU.add), b)

            def ffn(st):
                with dve.Fori(0, FF // 2) as i:
                    for p in range(2):
                        was_drained(dve, (st, "up", 2 * p), i)
                        b = ready(dve, (st, "up", 2 * p + 1), i)
                        drain(tt(HID["hid"][:, bass.ds(i * 2 + p, 1), :], gate[:, p:p + 1, :], ps[:, b:b + 1, :], ALU.mult), b)

            norm("n0", xres, V("mix_norm", 0, KC), hd_(), 0, 0)
            dve.wait_ge(sem("pos_loaded"), 16)
            dve.wait_ge(sem("consts_loaded"), 16)
            pos, ang, turns = L0["mix"][:, 1, :], L0["mix"][:, 2, :], L0["mix"][:, 3, :]
            link(dve.tensor_copy(pos, L0["mix"][:, 0, :].bitcast(I32)))
            MAGIC = 1.5 * 2.0 ** 23
            C1 = 6.28125
            C2 = float(np.float32(int((2 * np.pi - C1) * 2 ** 21) / 2.0 ** 21))
            C3 = float(np.float32(2 * np.pi - C1 - C2))
            for fr, names in enumerate((("sin128", "cos128"), ("sin64", "cos64"))):
                link(ts(ang, pos, C("invf")[:, fr:fr + 1], None, ALU.mult))
                for q, name in enumerate(names):
                    link(ts(turns, ang, float(1.0 / (2.0 * np.pi)), 0.25 * q, ALU.mult, ALU.add))
                    link(ts(turns, turns, MAGIC, MAGIC, ALU.add, ALU.subtract))
                    r = L0[name]
                    link(stt(r, turns, -C1, ang, ALU.mult, ALU.add))
                    link(stt(r, turns, -C2, r, ALU.mult, ALU.add))
                    link(stt(r, turns, -C3, r, ALU.mult, ALU.add))
                    if q:
                        link(ts(r, r, float(np.pi / 2), None, ALU.add))
                    ts(r, r, 3.1415925, -3.1415925, ALU.min, ALU.max).then_inc(sem("angles"), 1)
            for p in range(2):
                b = ready(dve, ("gz", p))
                dve.wait_ge(sem("gz_abs"), p + 1)
                drain(ts(G["gb"][:, p, :], ps[:, b, :], V("gate_b", p), 0.0, ALU.add, ALU.min), b)
            for i in range(NT):
                b = ready(dve, ("gv", i))
                drain(dve.tensor_copy(L0["gv"][:, i, :], ps[:, b, :]), b)
            for p in range(2):
                bv = G["gL"][:, p, :]
                b3 = bv.rearrange("p (n c) -> p n c", c=GCH)
                dve.wait_ge(sem("gate_ln"), p + 1)
                link(tt(G["gb"][:, p, :], G["gb"][:, p, :], bv, ALU.subtract))
                link(dve.tensor_tensor_scan(bv, C("chunk_carry"), G["gb"][:, p, :], 0.0, ALU.mult, ALU.add))
                tt(G["eb"][:, p, :].rearrange("p (n c) -> p n c", c=GCH), b3,
                   b3[:, :, GCH // 2 - 1:GCH // 2].broadcast_to((P, NCH, GCH)), ALU.subtract)
                tt(KD[:, p, :].rearrange("p (n c) -> p n c", c=GCH),
                   b3[:, :, GCH - 1:GCH].broadcast_to((P, NCH, GCH)), b3, ALU.subtract).then_inc(sem("gla_diffs"), 1)
            for p in range(2):
                dve.wait_ge(sem("gla_exps"), p + 1)
                was_drained(dve, ("gq", p))
                was_drained(dve, ("gk", p))
                tt(QD[:, p, :], QD[:, p, :], L0["gq"][:, p, :], ALU.mult)
                tt(KD[:, p, :], KD[:, p, :], L0["gk"][:, p, :], ALU.mult)
                tt(L0["gq"][:, p, :], L0["gq"][:, p, :], G["gb"][:, p, :], ALU.mult)
                tt(L0["gk"][:, p, :], L0["gk"][:, p, :], G["eb"][:, p, :], ALU.mult).then_inc(sem("gla_in"), 1)

            def rotate(t):
                v = L0["qk"][:, t, :] if t < 8 else L0["idx"][:, t - 8, :]
                sn, cs = (L0["sin128"], L0["cos128"]) if t < 8 else (L0["sin64"], L0["cos64"])
                b = ready(dve, ("qk_swap", t))
                if t:
                    dve.wait_ge(sem("qk_rotated"), t)
                drain(tt(gate[:, 1, :], ps[:, b, :], sn, ALU.mult), b)
                link(tt(v, v, cs, ALU.mult))
                tt(v, v, gate[:, 1, :], ALU.add).then_inc(sem("qk_rotated"), 1)
            dve.wait_ge(sem("rope_tables"), 4)
            for t in range(15):
                if t < 8:
                    dve.wait_ge(sem("qk_rs"), t + 1)
                    v = L0["qk"][:, t, :]
                    stt(v, v, V("dsa_q" if t < 4 else "dsa_k"), rs[:, t % 2, :], ALU.mult, ALU.mult)\
                        .then_inc(sem("qk_normed"), 1)
                if 1 <= t <= 13:
                    rotate(t - 1)
            for i in range(NT):
                b = ready(dve, ("dv", i))
                drain(dve.tensor_copy(L0["dv"][:, i, :], ps[:, b, :]), b)
            for p in range(2):
                for n in range(NCH - 1):
                    b = ready(dve, ("kv", p, n % 2))
                    kv = ps[:, b, (n // 2) * P:(n // 2 + 1) * P]
                    if n == 0:
                        ins = dve.tensor_copy(G["st"][:, p, 1, :], kv)
                    else:
                        ins = stt(G["st"][:, p, n + 1, :], G["st"][:, p, n, :], G["dec"][:, p, n:n + 1], kv,
                                  ALU.mult, ALU.add)
                    if n >= NCH - 3:
                        drain_link(ins, ("kv", p, n % 2))
                    else:
                        link(ins)

            def gla_mask(head):
                b = ready(dve, ("att", head))
                if head:
                    ready(dve, ("go", head - 1))
                for i in range(NT):
                    ins = dve.copy_predicated(G["att"][:, i, :], C("gla_mask").bitcast(I32), ps[:, b, i * P:(i + 1) * P])
                drain(ins, b)

            def gla_out(head):
                dve.wait_ge(sem("go_rs"), head + 1)
                o = G["o"][:, head % 2, :]
                link(stt(o, o, V("gla_out"), rs[:, head % 2, :], ALU.mult, ALU.mult))
                tt(L0["mix"][:, head, :], o, L0["gr"][:, head, :], ALU.mult).then_inc(sem("gla_out_done"), 1)
            for head in range(GH + 1):
                if head < GH:
                    gla_mask(head)
                if head:
                    gla_out(head - 1)

            link(dve.tensor_copy(T["keep"][:, 0, 0:P], C("tri_bias")))
            n = 0
            was_drained(dve, "iw")
            for i in range(1, NT):
                w = (i + 1) * P
                sc = T["score"][:, 0:w]
                for hd in range(IH):
                    was_drained(dve, ("rel", i, hd))
                    wt = L0["iw"][:, i - 1, hd:hd + 1]
                    if hd == 0:
                        ins = ts(sc, T["rel"][:, n % 2, 0:w], wt, None, ALU.mult)
                    else:
                        ins = stt(sc, T["rel"][:, n % 2, 0:w], wt, sc, ALU.mult, ALU.add)
                    ins.then_inc(sem("idx_added"), 1)
                    dve.wait_ge(sem("idx_added"), n + 1)
                    n += 1
                link(tt(sc[:, w - P:w], sc[:, w - P:w], C("tri_bias"), ALU.add))
                for r in range(TOPK // 8):
                    link(dve.max(T["top"], sc))
                    link(dve.match_replace(sc, T["top"], sc, TAKEN))
                link(ts(T["keep"][:, i, 0:w], sc, TAKEN / 2, NEG, ALU.is_gt, ALU.mult))

            def dsa_front(n):
                i, hd = n // DH, n % DH
                w = (i + 1) * P
                b = ready(dve, ("dsa_s", n))
                if n >= 2:
                    ready(dve, ("dsa_pt", n - 2))
                drain_link(stt(T["P"][:, n % 2, 0:w], ps[:, b, 0:w], HEAD_SCALE, T["keep"][:, i, 0:w],
                               ALU.mult, ALU.add), ("dsa_s", n))
                dve.tensor_reduce(T["stat"][:, n % 2, 0:1], T["P"][:, n % 2, 0:w], AX, ALU.max, negate=True)\
                    .then_inc(sem("dsa_max"), 1)

            def dsa_back(n):
                w = (n // DH + 1) * P
                dve.wait_ge(sem("dsa_exp"), n + 1)
                link(dve.reciprocal(T["stat"][:, n % 2, 2:3], T["stat"][:, n % 2, 1:2]))
                ts(T["P"][:, n % 2, 0:w], T["P"][:, n % 2, 0:w], T["stat"][:, n % 2, 2:3], None, ALU.mult)\
                    .then_inc(sem("dsa_probs"), 1)
            NS = NT * DH
            for n in range(NS + 1):
                if n < NS:
                    dsa_front(n)
                if n:
                    dsa_back(n - 1)
            was_drained(dve, ("ada", ADA_REST - 1))
            rest = mod[:, ADA_FIRST * NT:2 * 48]
            link(tt(rest, rest, V("ada_b", ADA_FIRST * NT, ADA_REST * NT), ALU.add))
            add_out("m0", 0, 2)
            norm("f0", xres, V("ffn_norm", 0, KC), hd_(), 0, 3)
            ffn("f0")
            add_out("f0", 0, 5)

            x_chunk(dve, "f0", KC - 1)
            dve.memset(L1["u"][:, :, 0:META], 0.0)
            link(dve.memset(L1["s"][:, :, 0:META], 0.0))
            dve.memset(L1["pooled"][:, :, 0:1], 0.0).then_inc(sem("n1_free"), 1)
            norm("n1", xres, V("mix_norm", KC, KC), hd_(), 1, 0)
            for t in range(8):
                dve.wait_ge(sem("sqk_rs"), t + 1)
                v = L1["qk"][:, t, :]
                stt(v, v, sbq_s if t < 4 else V("sb_k"), rs[:, t % 2, :], ALU.mult, ALU.mult)\
                    .then_inc(sem("sqk_normed"), 1)
            for i in range(NT):
                b = ready(dve, ("sv", i))
                drain(dve.tensor_copy(L1["sv"][:, i, :], ps[:, b, :]), b)
            for g, win in enumerate(WINDOWS):
                was_drained(dve, ("u", g))
                u = L1["u"][:, g, :]
                src, width, w = u, 1, 0
                while width < win:
                    dst = L1["s"][:, w, :]
                    link(tt(dst[:, META:SM], src[:, META:SM], src[:, META - width:SM - width], ALU.add))
                    src, width, w = dst, 2 * width, 1 - w
                if g >= 2:
                    ready(dve, ("py", g - 2))
                out = L1["pooled"][:, g % 2, :]
                link(stt(out, src[:, META:SM], 1.0 / win, u[:, META:SM], ALU.mult, ALU.subtract))
                link(tt(out[:, 0:16], src[:, META:META + 16], C("pool_rc")[:, g * 16:(g + 1) * 16], ALU.mult))
                tt(out[:, 0:16], out[:, 0:16], u[:, META:META + 16], ALU.subtract).then_inc(sem("pooled"), 1)
            for hd in range(DH):
                for n, j in enumerate(reversed(range(NT))):
                    w = S - j * P
                    dve.wait_ge(sem("sb_ln"), NT * hd + n + 1)
                    b = uses[("z", hd, j)][0]
                    link(stt(B1["nl"][:, j, 0:w], ps[:, b, 0:w], 0.0, B1["L"][:, j, 0:w], ALU.max, ALU.add))
                    drain(stt(B1["lb"][:, j, 0:w], ps[:, b, 0:w], 0.0, B1["L"][:, j, 0:w], ALU.min, ALU.subtract), b)
                    tt(B1["nl"][:, j, 0:P], B1["nl"][:, j, 0:P], C("strict"), ALU.mult).then_inc(sem("sb_nl"), 1)
                for n, j in enumerate(reversed(range(NT))):
                    w = S - j * P
                    b = ready(dve, ("aft", hd, j))
                    drain(tt(B1["lb"][:, j, 0:w], B1["lb"][:, j, 0:w], ps[:, b, 0:w], ALU.subtract), b)
                for n, j in enumerate(reversed(range(NT))):
                    dve.wait_ge(sem("sb_e"), NT * hd + n + 1)
                    tt(B1["w"][:, j, 0:P], B1["w"][:, j, 0:P], C("strict"), ALU.mult).then_inc(sem("sb_w"), 1)
            add_out("m1", 1, 2)
            norm("f1", xres, V("ffn_norm", KC, KC), hd_(), 1, 3)
            ffn("f1")
            add_out("f1", 1, 5)

            x_chunk(dve, "f1", KC - 1)
            norm("mn", metaT, V("norm1", 0, KC), hd_(0, META), n=META)
            norm("n2", xres, V("norm1", 0, KC), hd_(META))

            def token_major(name, dst, dstm):
                for g in range(2):
                    for i in range(NT):
                        b = ready(dve, ((name, g), i))
                        drain(dve.tensor_copy(dst[:, i, g * S:(g + 1) * S], ps[:, b, :]), b)
                    b = ready(dve, ((name, g), "m"))
                    drain(dve.tensor_copy(dstm[0:META, g * S:(g + 1) * S], ps[0:META, b, :]), b)
            token_major("rv", RET["rv"], RET["rvm"])
            token_major("fv", DF["dv"], DF["dvm"])
            dve.wait_ge(sem("tables2_loaded"), 16)
            for hd in range(RH):
                for j in range(-1, NT):
                    n = 5 * hd + j + 1
                    w, c0, kp = (S, META, META) if j < 0 else (S - j * P, 0, P)
                    b = ready(dve, ("rs", hd, j))
                    if n >= 2:
                        if (n - 2) % 5 == 4:
                            ready(dve, ("ro", (n - 2) // 5, 1))
                        else:
                            dve.wait_ge(sem("ret_used"), 4 * ((n - 2) // 5) + (n - 2) % 5 + 1)
                    drain(tt(R2["sT"][0:kp, n % 2, 0:w], ps[0:kp, b, 0:w], R2["decay"][0:kp, hd, c0:c0 + w], ALU.mult),
                          b)
                b = ready(dve, ("rmu", hd))
                was_drained(dve, ("ro", hd, 1))
                for v in range(2):
                    ins = stt(gate[:, v, :], ps[:, b, :], -1.0 / RDV, gate[:, v, :], ALU.mult, ALU.add)
                    ins.then_inc(drained[b] if v else sem("ret_yc"), 1)
                was_drained(dve, ("rg", 7))
                dve.wait_ge(sem("ret_rs"), hd + 1)
                for v in range(2):
                    link(tt(gate[:, v, :], gate[:, v, :], rs[:, hd % 2, :], ALU.mult))
                    r = RET["rg"][:, 2 * hd + v, :]
                    tt(r, r, gate[:, v, :], ALU.mult).then_inc(sem("ret_out"), 1)

            def branch(st, first):
                with dve.Fori(0, KC // 2) as i:
                    for p in range(2):
                        m = RET["merged"][:, bass.ds(i * 2 + p, 1), :]
                        was_drained(dve, (st, "b", 2 * p), i)
                        b = ready(dve, (st, "b", 2 * p + 1), i)
                        g, y = gate[:, p:p + 1, :], ps[:, b:b + 1, :]
                        if first:
                            drain(tt(m, g, y, ALU.mult), b)
                        else:
                            tt(sq[:, p:p + 1, :], g, y, ALU.mult).then_inc(sem(st + "_gated"), 1)
                            dve.wait_ge(sem(st + "_gated"), i * 2 + p + 1)
                            drain(tt(m, m, sq[:, p:p + 1, :], ALU.add), b)
            branch("br0", True)
            was_drained(dve, "lam")
            link(stt(neg_lam, small[:, 7:8], -LAM_INIT, small[:, 6:7], ALU.add, ALU.subtract))

            def diff_front(n):
                hd, i = n // NT, n % NT
                w = (i + 1) * P
                slope = float(2.0 ** (-8.0 / FH * (hd + 1.0)))
                if n >= 2:
                    ready(dve, ("fptm", n - 2))
                ready(dve, ("fs", n))
                L = F2["L"][:, n % 2, :, :]
                c0 = SM - w - META
                dist = R2["dist"].unsqueeze(1)
                drain(stt(L[:, :, META:META + w], dist[:, :, c0 + META:SM].broadcast_to((P, 2, w)), slope,
                          ps[:, 0:2, 0:w], ALU.mult, ALU.add), 0)
                ready(dve, ("fsm", n))
                drain_link(stt(L[:, :, 0:META], dist[:, :, c0:c0 + META].broadcast_to((P, 2, META)), slope,
                               ps[:, 2:4, 0:META], ALU.mult, ALU.add),
                           ("fsm", n))
                dve.tensor_reduce(F2["stat"][:, n % 2, 0:2], L[:, :, 0:META + w], AX, ALU.max, negate=True)\
                    .then_inc(sem("diff_max"), 1)

            def diff_back(n):
                w = META + (n % NT + 1) * P
                L, st = F2["L"][:, n % 2, :, 0:w], F2["stat"][:, n % 2, :]
                dve.wait_ge(sem("diff_exp"), n + 1)
                link(dve.reciprocal(st[:, 4:6], st[:, 2:4]))
                ts(st[:, 6:7], st[:, 5:6], neg_lam, None, ALU.mult)
                link(ts(L[:, 0, :], L[:, 0, :], st[:, 4:5], None, ALU.mult))
                stt(L[:, 0, :], L[:, 1, :], st[:, 6:7], L[:, 0, :], ALU.mult, ALU.add).then_inc(sem("diff_probs"), 1)

            def diff_norm(hd):
                dve.wait_ge(sem("fo_rs"), hd + 1)
                o = OD["od"][:, hd, :]
                stt(o, o, subln_s, rs[:, hd % 2, :], ALU.mult, ALU.mult).then_inc(sem("diff_out"), 1)
            NF = FH * NT
            for n in range(NF + 1):
                if n < NF:
                    diff_front(n)
                if n:
                    diff_back(n - 1)
                    hd, i = (n - 1) // NT, (n - 1) % NT
                    if i == 1 and hd:
                        diff_norm(hd - 1)
            diff_norm(FH - 1)
            branch("br1", False)
            for t in range(KC):
                u = CV["u"][:, t % 2, :]
                cv = CV["cv"][:, t, :]
                was_drained(dve, (("cc", t), 1))
                for n in range(2):
                    b = ready(dve, (("cx", t), n))
                    uh = u[:, n * SM // 2:(n + 1) * SM // 2]
                    drain_link(tt(uh, uh, ps[:, b, 0:SM // 2], ALU.mult), (("cx", t), n))
                link(ts(cv, u[:, META - 2:SM - 2], V("conv", t), None, ALU.mult))
                link(stt(cv, u[:, META - 1:SM - 1], V("conv", KC + t), cv, ALU.mult, ALU.add))
                link(stt(cv, u[:, META:SM], V("conv", 2 * KC + t), cv, ALU.mult, ALU.add))
                b = ready(dve, ("cb", t))
                drain(tt(cv, cv, ps[:, b, :], ALU.mult), b)
            branch("br2", False)
            add_out("m2")
            norm("f2", xres, V("norm2", 0, KC), hd_())
            add_out("f2")
            x_chunk(dve, "f2", KC - 1)
            norm("nf", xres, V("final", 0, KC), hd_())


def _fm(w, n0, n1):
    w = w[:, n0:n1]
    return w.reshape(KC, P, -1, P).transpose(2, 1, 0, 3).reshape(-1, P, UNIT)


def _tm(w, n0, n1):
    w = w[:, n0:n1]
    return w.reshape(4, 2, P, -1, S).transpose(3, 0, 2, 1, 4).reshape(-1, P, UNIT)


def _deep(w):
    f = w.shape[0] // P
    n = -(-f // 8)
    t = np.zeros((KC, P, n * 8, P), w.dtype)
    t[:, :, :f] = w.reshape(f, P, KC, P).transpose(2, 1, 0, 3)
    return t.reshape(KC, P, n, UNIT).transpose(0, 2, 1, 3).reshape(-1, P, UNIT)


def _pairs(a, b):
    return np.stack([a, b], 1).reshape(-1, P, UNIT)


def _cols(v):
    return np.asarray(v).reshape(-1, P).T


def _consts():
    i = np.arange(P)
    r, c = i[:, None], i[None, :]
    eye = np.eye(P, dtype=np.float32)
    same = (r // GCH) == (c // GCH)
    invf = np.stack([np.float32(10000.0) ** (-(i % h).astype(np.float32) / np.float32(h)) for h in (64, 32)], 1)
    sign = np.stack([np.where(i % (2 * h) < h, -1.0, 1.0) for h in (64, 32)], 1)
    carry = np.broadcast_to((np.arange(S) % GCH != 0), (P, S))
    rc = np.concatenate([1.0 / np.minimum(np.arange(16) + 1.0, w) for w in WINDOWS])
    parts = [eye, eye[(i + 64) % P], eye[(i // 64) * 64 + (i % 64 + 32) % 64], np.where(c <= r, 0.0, NEG),
             (r <= c) & same, r > c, r < c, carry, invf, sign, np.broadcast_to(rc, (P, 64))]
    a = np.concatenate([np.asarray(p, np.float32) for p in parts], 1)
    q = np.arange(SM)[None, :] - i[:, None]
    g = 1.0 - 2.0 ** (-5.0 - np.arange(RH))
    decay = [np.where(q >= 0, x ** np.maximum(q, 0), 0.0) for x in g]
    d = r - (np.arange(SM)[None, :] - (SM - P))
    dist = np.where(d >= 0, -d, -1.0e34)
    return np.ascontiguousarray(a), np.concatenate([*decay, dist], 1).astype(np.float32)


def kernel(**a):
    import concourse.bacc as bacc
    from concourse.bass_utils import run_bass_kernel_spmd

    a = {k: np.asarray(v) for k, v in a.items()}
    ab, w2 = a["ab_w_in"][0], a["w_in_2"][0]
    o = np.cumsum([0, 256, 256, 512, 16, 512, 512, 512, 512, 512, 64, 8])
    misc = np.zeros((D, P), ab.dtype)
    misc[:, :GRANK] = ab[:, o[3]:o[4]]
    misc[:, GRANK:GRANK + IH] = ab[:, o[10]:o[11]]
    ik = ab[:, o[9]:o[10]]
    ik = np.concatenate([ik, ik], 1)
    cd = a["cd_w_in"][0]

    def w1(layer):
        w = a["ffn_w1"][layer]
        return _pairs(_fm(w, 0, D_FF), _fm(w, D_FF, 2 * D_FF))

    def br(n):
        return _pairs(_fm(w2, 9216 + n * D, 9216 + (n + 1) * D), _fm(a["w_branch_2"][0, n], 0, D))
    conv = np.stack([_fm(w2, 7168, 8192), _fm(w2, 8192, 9216), _fm(w2, 6144, 7168)], 1).reshape(-1, P, UNIT)
    packs = {
        "ada_first": lambda: _tm(a["ada_w"][0], 0, 2 * D),
        "ab": lambda: np.concatenate([_fm(misc, 0, P), _fm(ab, o[1], o[2]), _fm(ab, o[0], o[1]), _fm(ab, o[4], o[5]),
                                      _tm(ab, o[2], o[3]), _fm(ab, o[5], o[7]), _fm(ab, o[8], o[9]), _fm(ik, 0, P),
                                      _tm(ab, o[7], o[8])]),
        "ab_out": lambda: _fm(a["ab_w_out"][0], 0, D), "w1_0": lambda: w1(0), "w1_1": lambda: w1(1),
        "w2_0": lambda: _deep(a["ffn_w2"][0]), "w2_1": lambda: _deep(a["ffn_w2"][1]),
        "cd": lambda: np.concatenate([_fm(cd, 0, 1536), _tm(cd, 1536, 2048)]),
        "cd_out": lambda: _fm(a["cd_w_out"][0], 0, D),
        "in2": lambda: np.concatenate([_fm(w2, 0, 1024), _fm(w2, 2048, 3072), _tm(w2, 1024, 2048),
                                       _fm(w2, 3072, 5120), _tm(w2, 5120, 6144), conv]),
        "br0": lambda: br(0), "br1": lambda: br(1), "br2": lambda: br(2),
        "w_out2": lambda: _fm(a["w_out_2"][0], 0, D), "up2": lambda: _fm(a["w_up_2"][0], 0, D_FF2),
        "down2": lambda: _deep(a["w_down_2"][0]),
    }
    lam = np.zeros((P, 4), a["diff_lambda_2"].dtype)
    lam[:FHD] = a["diff_lambda_2"][0].T
    vecs = np.concatenate([
        _cols(a["mix_norm"]), _cols(a["ffn_norm"]), _cols(a["ada_b"]), _cols(a["c"]), _cols(a["gla_gate_b"]),
        _cols(a["gla_out_norm"]), _cols(a["dsa_q_norm"]), _cols(a["dsa_k_norm"]), _cols(a["pool_scale"]),
        _cols(a["sb_q_norm"]), _cols(a["sb_k_norm"]), _cols(a["norm1_w_2"]), _cols(a["conv_w_2"]),
        _cols(a["diff_subln_w_2"]), _cols(a["norm2_w_2"]), _cols(a["final_norm_w_2"]), lam], 1)
    consts, tables2 = _consts()
    arrays = {
        "vecs": np.ascontiguousarray(vecs), "consts": consts, "tables2": tables2,
        "x": np.ascontiguousarray(a["x"][0].T.reshape(KC, P, S).transpose(1, 0, 2)),
        "meta": np.ascontiguousarray(a["meta_tokens_2"].T.reshape(KC, P, META).transpose(1, 0, 2)),
        "positions": np.ascontiguousarray(a["positions"]),
        "gate_up": np.ascontiguousarray(a["gla_gate_up"][0]),
        "pool_w": np.ascontiguousarray(a["pool_w"][0].transpose(1, 0, 2)),
    }
    ada_rest = np.concatenate([_tm(a["ada_w"][0], 2 * D, 6 * D), _tm(a["ada_w"][1], 0, 6 * D)])
    ada_rest = np.ascontiguousarray(ada_rest.reshape(-1, P, 2, S))
    arrays["ada_rest"] = ada_rest
    nc = bacc.Bacc("TRN2", target_bir_lowering=False, num_devices=1)
    n_units = N_UNITS
    A = {k: nc.dram_tensor(f"in_{k}", v.shape, mybir.dt.from_np(v.dtype), kind="ExternalInput").ap()
         for k, v in arrays.items()}
    A["stream"] = nc.dram_tensor("in_stream", (n_units, P, UNIT), F32, kind="ExternalInput").ap()
    A["out"] = nc.dram_tensor("out_0", (P, KC, S), F32, kind="ExternalOutput").ap()
    plan = []
    build(nc, A, plan)
    packed = {k: f() for k, f in packs.items()}
    arrays["stream"] = np.concatenate([packed[name][first:first + count] for name, first, count in plan])
    assert arrays["stream"].shape[0] == n_units
    r = run_bass_kernel_spmd(nc, [{f"in_{k}": v for k, v in arrays.items()}], core_ids=[0])
    got = r.results[0]["out_0"]
    return np.ascontiguousarray(got.transpose(1, 0, 2).reshape(D, S).T)[None]
```

```python
import numpy as np
from contextlib import ExitStack
import concourse.bass as bass
from concourse import mybir

F32 = mybir.dt.float32
F32R = mybir.dt.float32r
I32 = mybir.dt.int32
ALU = mybir.AluOpType
ACT = mybir.ActivationFunctionType
AX = mybir.AxisListType.X

P = 128
D = 1024
KC = D // P
S = 512
NT = S // P
META = 16
SM = S + META
UNIT = 1024
RING = 4
DEPTH = 2
D_FF = 2816
FF = D_FF // P
FFU = 3
D_FF2 = 4096
FF2 = D_FF2 // P
GH, GDK, GDV, GRANK, GCH = 4, 64, 128, 16, 64
NCH = S // GCH
DH = 4
IH, IDIM = 8, 64
TOPK = 128
RH, RDV = 4, 256
FH, FHD = 8, 64
EPS = 1e-6
IDX_SCALE = (IH ** -0.5) * (IDIM ** -0.5)
HEAD_SCALE = 128.0 ** -0.5
LAM_INIT = 0.8 - 0.6 * 1.0
NEG = -1.0e30
TAKEN = -3.0e38
WINDOWS = (2, 4, 8, 16)

_C = {}


def _lay(table, *items):
    at = 0
    for name, width in items:
        table[name] = (at, at + width)
        at += width
    return at


NC_A = _lay(_C, ("ident", P), ("swap128", P), ("swap64", P), ("tri_bias", P), ("gla_mask", P),
            ("after", P), ("strict", P), ("chunk_carry", S), ("invf", 2), ("sign", 2), ("pool_rc", 64))
_E = {}
NC_B = _lay(_E, ("decay", RH * SM), ("dist", SM))
_V = {}
NV = _lay(_V, ("mix_norm", 2 * KC), ("ffn_norm", 2 * KC), ("ada_b", 2 * 48), ("c", KC), ("gate_b", 2),
          ("gla_out", 1), ("dsa_q", 1), ("dsa_k", 1), ("pool_scale", 4), ("sb_q", 1), ("sb_k", 1),
          ("norm1", KC), ("conv", 3 * KC), ("subln", 1), ("norm2", KC), ("final", KC), ("lam", 4))

ADA_UNITS = 4
ADA_FIRST = 2 * D // S
ADA_LATE = FF // 2 - 1
ADA_REST = DEPTH * 6 * D // S - ADA_FIRST - ADA_LATE
ADA_ADDS = 2 * ADA_UNITS - 1

ADA_SUMS = {place: (g, b) for g, (place, b) in enumerate([
    (("gr", 1), 7), (("gv", 0), 0), (("gv", 3), 0), (("qk", 2), 5), (("qk", 5), 5), (("qk", 8), 5),
    (("qk", 12), 5), (("dv", 2), 0), (("head", 1), 0), (("head", 3), 0)])}
assert len(ADA_SUMS) == ADA_REST

CONV_PIECES = [(t, what) for t in range(KC) for what in (("cc", 0), ("cc", 1), ("cx", 0), ("cx", 1), ("cb", None))]


def conv_pieces(n):
    steps = FH * NT
    return CONV_PIECES[len(CONV_PIECES) * n // steps:len(CONV_PIECES) * (n + 1) // steps]


QK_ORDER = [*range(8, 13), *range(8)]
REL_STEPS = range(7, 13)
REL_PER = (NT - 1) * IH // len(REL_STEPS)
TOPK_ROUNDS = {8: (1, range(0, 4)), 9: (1, range(4, 10)), 10: (1, range(10, 16)),
               11: (2, range(0, 5)), 12: (2, range(5, 10)), 13: (2, range(10, 16)), 14: (3, range(16))}

def gla_part(n):
    return (n // 3, n % 3) if n < 3 * GH else (0, None)


N_UNITS = (ADA_FIRST * ADA_UNITS + 30 + KC + 16 + KC + 2 * (2 * FF + KC * FFU) + 72 + 3 * 2 * KC + KC + FF2 + KC * FF2 // 8)


def build(nc, A, plan):
    ctx = ExitStack()
    with ctx:
        def sb(name, shape, dt=F32):
            return ctx.enter_context(nc.sbuf_tensor(name, shape, dt))

        sems = {}

        def sem(name):
            if name not in sems:
                sems[name] = ctx.enter_context(nc.semaphore(name))
            return sems[name]

        filled = [sem(f"filled{s}") for s in range(RING)]
        emptied = [sem(f"emptied{s}") for s in range(RING)]
        upper_made = [sem(f"upper_made{s}") for s in range(RING)]
        halves_read = [sem(f"halves_read{s}") for s in range(RING)]
        full = [sem(f"full{b}") for b in range(8)]
        drained = [sem(f"drained{b}") for b in range(8)]

        ring = sb("ring", [P, RING, UNIT])
        xres = sb("xres", [P, KC, S])
        hbuf_at = nc.sbuf_base
        hbuf = sb("hbuf", [P, KC, SM])
        BIG = 34816
        big_at = nc.sbuf_base
        big = sb("big", [P, BIG])
        consts = sb("consts", [P, NC_A])
        vecs = sb("vecs", [P, NV])
        mod = sb("mod", [P, 2 * 48])
        coef = sb("coef", [P, KC])
        ones = sb("ones", [P, P])
        small = sb("small", [P, 64])
        sq = sb("sq", [P, 2, S])
        rs = sb("rs", [P, 2, S])
        gate = sb("gate", [P, 2, S])
        cond = sb("cond", [P, KC])
        gate_up = sb("gate_up", [GRANK, GH * GDK])
        metaT = sb("metaT", [P, KC, META])
        lamp = sb("lamp", [FHD, 2])
        ps = ctx.enter_context(nc.psum_tensor("ps", [P, 8, S], F32))

        late_w = [sq, rs]

        def f32r(name, at, *dims):
            return nc.alloc_sbuf_tensor_at(name, [P, *dims], F32R, offset=at).ap()

        x_hi = f32r("x_hi", hbuf_at, KC, S)
        x_lo = f32r("x_lo", big_at, KC, S)
        halves = f32r("halves", big_at + 4 * KC * S, RING, 2, UNIT)
        hid_at = big_at + 4 * (KC * S + RING * 2 * UNIT)
        hid = f32r("hid", hid_at, 2, FF, S)
        HALF2 = FF2 // 2
        hid2 = f32r("hid2", hid_at, 2, HALF2, S)

        def C(name):
            return consts[:, _C[name][0]:_C[name][1]]

        def V(name, i=0, n=1):
            a = _V[name][0] + i
            return vecs[:, a:a + n]

        def area(start, *items):
            out, at = {}, start
            for name, *dims in items:
                n = int(np.prod(dims))
                v = big[:, at:at + n]
                if len(dims) == 2:
                    v = v.rearrange("p (a b) -> p a b", b=dims[1])
                elif len(dims) == 3:
                    v = v.rearrange("p (a b c) -> p a b c", b=dims[1], c=dims[2])
                out[name] = v
                at += n
            assert at <= BIG, at
            return out, at

        eps_col, one_col = small[:, 0:1], small[:, 1:2]
        neg_lam, subln_s, sbq_s = small[:, 2:3], small[:, 3:4], small[:, 4:5]
        lam_e = small[:, 6:8]

        L0, at0 = area(0, ("mix", KC, S), ("cos128", S), ("sin128", S), ("cos64", S), ("sin64", S),
                     ("gk", 2, S), ("gq", 2, S), ("gr", 4, S), ("gv", NT, S), ("qk", 8, S), ("dv", NT, S),
                     ("idx", 5, S), ("iw", 3, IH), ("glow", S))
        G, _ = area(at0, ("gb", 2, S), ("gL", 2, S), ("eb", 2, S), ("QD", 2, S), ("KD", 2, S),
                    ("kd_tm", NT, 2 * P), ("st", 2, NCH, P), ("att", 4, P), ("o", 2, S), ("dec", 2, NCH),
                    ("ada_acc", 2, S), ("ada_w", 2, 2, S), ("keep1", 2 * P), ("top", 8))
        ada_first = G["st"].rearrange("p a b c -> p (a b c)").rearrange("p (a b) -> p a b", b=S)
        QD, KD = G["QD"], G["KD"]
        T, _ = area(at0, ("P", 2, S), ("PT", 2, S), ("stat", 2, 4))
        REL, SCORE = L0["mix"][:, 4:6, :], L0["mix"][:, 6:8, :]
        KEEP = [C("tri_bias"), G["keep1"], L0["idx"][:, 0, :], L0["idx"][:, 1, :]]
        L1, at1 = area(KC * S + RING * 2 * UNIT, ("qk", 8, S), ("sv", NT, S), ("u", 4, SM), ("s", 2, SM),
                       ("pooled", 2, S), ("poolw", 4, P))
        L1.update(area(0, ("mix", KC, S))[0])
        poolw = L1["poolw"]
        B1, _ = area(at1, ("L", 4, S), ("nl", 4, S), ("lb", 4, S), ("w", 4, S))
        RET, atr = area(0, ("rq", 4, S), ("rk", 4, SM), ("rg", 8, S), ("rv", NT, D), ("rvm", D),
                        ("merged", KC, S))
        DF, atd = area(atr, ("dq", 8, S), ("dk", 8, SM), ("dv", NT, D), ("dvm", D))
        R2, _ = area(atd, ("decay", RH, SM), ("dist", SM), ("sT", 2, S))
        F2, atf = area(0, ("L", 2, 2, SM), ("PT", 2, S), ("PTm", 2, P), ("stat", 2, 8))
        OD, _ = area(4 * S + 4 * SM + 8 * S, ("od", 8, S))
        assert atf <= 4 * S + 4 * SM
        CV = {"u": R2["decay"][:, 0:2, :], "cv": RET["rg"]}

        uses = {}
        full_count = {}
        by_unit = {}

        def ready(eng, name, i=None):
            b, k = uses[name]
            if name in by_unit:
                read, n, step = by_unit[name]
                eng.wait_ge(read, n if i is None else i * step + n)
            else:
                eng.wait_ge(full[b], full_count[name])
            return b

        def was_drained(eng, name, i=None):
            b, k = uses[name]
            eng.wait_ge(drained[b], k + 1 if i is None else i + (k + 1))

        def x_chunk(eng, st, k):
            b, use = uses[(st, "y", k % 4)]
            eng.wait_ge(drained[b], use + k // 4 + 1)

        block = ctx.enter_context(nc.Block())
        units = []
        state = {"u": 0, "split": None}
        split_at = {}
        nuse = [0] * 8
        nfull = [0] * 8

        @block.tensor
        def _(pe):
            def claim(b, name, unit_ends=False):
                if nuse[b]:
                    pe.wait_ge(drained[b], nuse[b])
                uses[name] = (b, nuse[b])
                nuse[b] += 1
                if not unit_ends:
                    nfull[b] += 1
                    full_count[name] = nfull[b]

            def with_unit(*names):
                u = state["u"] - 1
                if state["split"]:
                    base, _, before = state["split"]
                    for name in names:
                        by_unit[name] = (halves_read[u % RING], before + (u - base) // RING + 1, 0)
                else:
                    for name in names:
                        by_unit[name] = (emptied[u % RING], u // RING + 1, 0)

            def read(s):
                return (halves_read if state["split"] else emptied)[s]

            def unit():
                u = state["u"]
                state["u"] += 1
                if state["split"]:
                    pe.wait_ge(emptied[u % RING], u // RING + 1)
                else:
                    pe.wait_ge(filled[u % RING], 16 * (u // RING + 1))
                return u % RING

            def begin_split(section, count):
                before = sum(n for _, n, _ in split_at.values()) // RING
                split_at[(section,)] = state["split"] = (state["u"], count, before)

            def products(out, s, k, hi, lo, start, stop):
                upper, lower = halves[:, s, 0, k * P:(k + 1) * P], halves[:, s, 1, k * P:(k + 1) * P]
                pe.matmul(out, upper, hi, start=start, stop=False)
                pe.matmul(out, upper, lo, start=False, stop=False)
                return pe.matmul(out, lower, hi, start=False, stop=stop)

            def stream(name, first, count):
                units.append((name, first, count))

            def fm_tile(name, b, rhs=None):
                claim(b, name, True)
                s = unit()
                with_unit(name)
                for k in range(KC):
                    if state["split"]:
                        mm = products(ps[:, b, :], s, k, x_hi[:, k, :], x_lo[:, k, :], k == 0, k == KC - 1)
                    else:
                        mm = pe.matmul(ps[:, b, :], ring[:, s, k * P:(k + 1) * P], rhs(k),
                                       start=k == 0, stop=k == KC - 1)
                mm.then_inc(read(s), 1)

            def first_tiles(st, names, rhs=None):
                slots = []
                for b, name in enumerate(names):
                    claim(b, name, True)
                    slots.append(unit())
                    with_unit(name)
                for k in range(KC):
                    pe.wait_ge(sem(st + "_h"), k + 1)
                    for b, s in enumerate(slots):
                        if state["split"]:
                            mm = products(ps[:, b, :], s, k, x_hi[:, k, :], x_lo[:, k, :], k == 0, k == KC - 1)
                        else:
                            mm = pe.matmul(ps[:, b, :], ring[:, s, k * P:(k + 1) * P], rhs(k),
                                           start=k == 0, stop=k == KC - 1)
                        if k == KC - 1:
                            mm.then_inc(read(s), 1)

            def wide_tile(name, b):
                claim(b, (name, 0), True)
                claim(b + 1, (name, 1), True)
                s = unit()
                with_unit((name, 0), (name, 1))
                for k in range(KC):
                    for n in range(2):
                        mm = pe.matmul(ps[:, b + n, 0:SM // 2], ring[:, s, k * P:(k + 1) * P],
                                       hbuf[:, k, n * SM // 2:(n + 1) * SM // 2],
                                       start=k == 0, stop=k == KC - 1)
                mm.then_inc(emptied[s], 1)

            def tm_group(name, off, meta=None):
                for i in range(NT):
                    claim(4 + i, (name, i), True)
                if meta is not None:
                    claim(meta, (name, "m"), True)
                for j in range(4):
                    s = unit()
                    for kk in range(2):
                        k = 2 * j + kk
                        w = ring[:, s, kk * S:(kk + 1) * S]
                        if state["split"]:
                            upper, lower = (halves[:, s, part, kk * S:(kk + 1) * S] for part in range(2))
                            for i in range(NT):
                                hi, lo = x_hi[:, k, i * P:(i + 1) * P], x_lo[:, k, i * P:(i + 1) * P]
                                pe.matmul(ps[:, 4 + i, :], hi, upper, start=k == 0, stop=False)
                                pe.matmul(ps[:, 4 + i, :], hi, lower, start=False, stop=False)
                                mm = pe.matmul(ps[:, 4 + i, :], lo, upper, start=False, stop=k == KC - 1)
                            continue
                        for i in range(NT):
                            mm = pe.matmul(ps[:, 4 + i, :], hbuf[:, k, off + i * P:off + (i + 1) * P], w,
                                           start=k == 0, stop=k == KC - 1)
                        if meta is not None:
                            mm = pe.matmul(ps[0:META, meta, :], hbuf[:, k, 0:META], w,
                                           start=k == 0, stop=k == KC - 1)
                    mm.then_inc(read(s), 1)
                    ada_sum(name, j)
                with_unit(*[(name, i) for i in (*range(NT), *(["m"] if meta is not None else []))])

            def column_sum(name, b, src, sem_in, count, n=S):
                claim(b, name)
                pe.wait_ge(sem_in, count)
                pe.matmul(ps[:, b, 0:n], ones[:, :], src, start=True, stop=True).then_inc(full[b], 1)

            def norm_sum(st, n=S):
                claim(6, (st, "ss"))
                for k in range(KC):
                    pe.wait_ge(sem(st + "_squared"), k + 1)
                    mm = pe.matmul(ps[:, 6, 0:n], ones[:, :], sq[:, k % 2, 0:n], start=k == 0, stop=k == KC - 1)
                    if k < KC - 1:
                        mm.then_inc(sem(st + "_summed"), 1)
                mm.then_inc(full[6], 1)

            def h_of(st, off=0):
                def f(k):
                    return hbuf[:, k, off:off + S]
                return f

            loop = {}

            def ring_loop(n_iter, per_iter, split=None):
                assert per_iter % RING == 0
                base = state["u"]
                state["u"] += n_iter * per_iter
                before = sum(n for _, n, _ in split_at.values()) // RING
                if split:
                    split_at[split] = (base, n_iter * per_iter, before)
                loop.update(base=base, step=per_iter // RING, split=split, before=before)

                def slot(i, n):
                    u = base + n
                    if split:
                        pe.wait_ge(emptied[u % RING], i * (per_iter // RING) + (u // RING + 1))
                    else:
                        pe.wait_ge(filled[u % RING], i * (16 * per_iter // RING) + 16 * (u // RING + 1))
                    return u % RING
                return slot

            def bank_loop(n_iter, banks, names, per_result=1):
                base = {}
                for n, (b, name) in enumerate(zip(banks, names)):
                    uses[name] = (b, nuse[b])
                    u = loop["base"] + (n + 1) * per_result - 1
                    if loop["split"]:
                        count = loop["before"] + ((n + 1) * per_result - 1) // RING + 1
                        by_unit[name] = (halves_read[u % RING], count, loop["step"])
                    else:
                        by_unit[name] = (emptied[u % RING], u // RING + 1, loop["step"])
                    base[b] = nuse[b]
                    nuse[b] += n_iter

                def take(i, b):
                    pe.wait_ge(drained[b], i + base[b])
                return take

            def ada_sum(*place):
                if place not in ADA_SUMS:
                    return
                g, b = ADA_SUMS[place]
                claim(b, ("ada", g), True)
                pe.wait_ge(sem("ada_added"), ADA_ADDS * (g + 1))
                for c in range(NT):
                    mm = pe.matmul(ps[:, b, c:c + 1], G["ada_acc"][:, g % 2, c * P:(c + 1) * P], ones[:, 0:1],
                                   start=True, stop=True)
                mm.then_inc(sem(f"ada_summed{g % 2}"), 1)

            stream("ada_first", 0, ADA_FIRST * ADA_UNITS)
            state["u"] += ADA_FIRST * ADA_UNITS
            norm_sum("n0")
            claim(7, "ada_first")
            for g in range(ADA_FIRST):
                pe.wait_ge(emptied[ADA_UNITS - 1], g + 1)
                for c in range(NT):
                    mm = pe.matmul(ps[:, 7, g * NT + c:g * NT + c + 1], ada_first[:, g, c * P:(c + 1) * P],
                                   ones[:, 0:1], start=True, stop=True, skip_group_check=True)
            mm.then_inc(full[7], 1)

            def first_pass(st, slot, take):
                slots = []
                for q in range(4):
                    take(0, q)
                    slots.append(slot(0, q))
                for k in range(KC):
                    pe.wait_ge(sem(st + "_h"), k + 1)
                    for q in range(4):
                        mm = products(ps[:, q, :], slots[q], k, x_hi[:, k, :], x_lo[:, k, :], k == 0, k == KC - 1)
                        if k == KC - 1:
                            mm.then_inc(halves_read[slots[q]], 1)

            def late_sum(i):
                pe.wait_ge(sem("late_read1"), i * 2 + 2)
                for c in range(NT):
                    mm = pe.matmul(ps[:, 7, bass.ds(i * NT + c, 1)], C("chunk_carry")[:, c * P:(c + 1) * P],
                                   ones[:, 0:1], start=True, stop=True, skip_group_check=True)
                mm.then_inc(sem("late_sum_free"), 1)

            def ffn(st, layer):
                norm_sum(st)
                stream(f"w1_{layer}", 0, 2 * FF)
                slot = ring_loop(FF // 2, 4, (st, "up"))
                take = bank_loop(FF // 2, range(4), [(st, "up", q) for q in range(4)])
                first_pass(st, slot, take)
                if layer == 0:
                    claim(7, "late", True)
                with pe.Fori(1, FF // 2) as i:
                    for q in range(4):
                        take(i, q)
                        s = slot(i, q)
                        for k in range(KC):
                            mm = products(ps[:, q, :], s, k, x_hi[:, k, :], x_lo[:, k, :], k == 0, k == KC - 1)
                        mm.then_inc(halves_read[s], 1)
                    if layer == 0:
                        late_sum(i - 1)
                stream(f"w2_{layer}", 0, KC * FFU)
                slot = ring_loop(2, 4 * FFU, (st, "down"))
                for b in (1, 3):
                    pe.wait_ge(drained[b], nuse[b])
                take = bank_loop(2, range(4), [(st, "y", q) for q in range(4)], FFU)
                with pe.Fori(0, 2) as i:
                    for q in range(4):
                        take(i, q)
                        for f in range(FF):
                            if f % 8 == 0:
                                s = slot(i, FFU * q + f // 8)
                            mm = products(ps[:, q, :], s, f % 8, hid[:, 0, f, :], hid[:, 1, f, :],
                                          f == 0, f == FF - 1)
                            if f % 8 == 7:
                                mm.then_inc(halves_read[s], 1)
                        mm.then_inc(halves_read[s], 1)

            def mix_out(st, name):
                pe.wait_ge(sem(st + "_split"), KC)
                stream(name, 0, KC)
                slot = ring_loop(2, 4, (st, "out"))
                take = bank_loop(2, range(4), [(st, "y", q) for q in range(4)])
                with pe.Fori(0, 2) as i:
                    for q in range(4):
                        take(i, q)
                        s = slot(i, q)
                        for k in range(KC):
                            mm = products(ps[:, q, :], s, k, x_hi[:, k, :], x_lo[:, k, :], k == 0, k == KC - 1)
                        mm.then_inc(halves_read[s], 1)

            stream("ab", 0, 30)
            h = h_of("n0")
            claim(0, "glow")
            claim(1, "iw", True)
            s = unit()
            with_unit("iw")
            for k in range(KC):
                pe.wait_ge(sem("n0_h"), k + 1)
                mm = pe.matmul(ps[0:GRANK, 0, :], ring[:, s, k * P:k * P + GRANK], h(k), start=k == 0, stop=k == KC - 1)
            mm.then_inc(full[0], 1)
            for i in range(1, NT):
                for k in range(KC):
                    mm = pe.matmul(ps[:, 1, (i - 1) * IH:i * IH], hbuf[:, k, i * P:(i + 1) * P],
                                   ring[:, s, k * P + GRANK:k * P + GRANK + IH], start=k == 0, stop=k == KC - 1)
            mm.then_inc(emptied[s], 1)
            for t in range(2):
                fm_tile(("gk", t), 2 + t, h)
            for p in range(2):
                claim(4 + p, ("gz", p))
                was_drained(pe, "glow")
                pe.wait_ge(sem("gate_up_loaded"), 16)
                pe.matmul(ps[:, 4 + p, :], gate_up[0:GRANK, p * P:(p + 1) * P], L0["glow"][0:GRANK, :],
                          start=True, stop=True).then_inc(full[4 + p], 1)
            for t in range(2):
                fm_tile(("gq", t), t, h)
            for t in range(4):
                fm_tile(("gr", t), (2 + t) % 4, h)
                ada_sum("gr", t)
            tm_group("gv", 0)

            def qk_sum(t):
                column_sum(("qk_ss", t), 6, sq[:, t % 2, :], sem("qk_squared"), t + 1)

            def qk_swap(t):
                claim(7, ("qk_swap", t))
                if t < 8:
                    pe.wait_ge(sem("qk_normed"), t + 1)
                    pe.matmul(ps[:, 7, :], C("swap128"), L0["qk"][:, t, :], start=True, stop=True).then_inc(full[7], 1)
                else:
                    was_drained(pe, ("qk", t))
                    pe.matmul(ps[:, 7, :], C("swap64"), L0["idx"][:, t - 8, :], start=True, stop=True).then_inc(full[7], 1)

            def rel_product(n):
                i, hd = n // IH + 1, n % IH
                b = (0, 1, 4)[n % 3]
                r = (hd % 2) * IDIM
                claim(b, ("rel", n))
                if n == 0:
                    pe.wait_ge(sem("qk_rotated"), 5)
                pe.matmul(ps[:, b, 0:(i + 1) * P], L0["idx"][r:r + IDIM, hd // 2, i * P:(i + 1) * P],
                          L0["idx"][r:r + IDIM, 4, 0:(i + 1) * P], start=True, stop=True).then_inc(full[b], 1)
            for step in range(15):
                if step < 13:
                    fm_tile(("qk", QK_ORDER[step]), 2 + step % 2, h)
                    ada_sum("qk", step)
                if step and step <= 13 and QK_ORDER[step - 1] < 8:
                    qk_sum(QK_ORDER[step - 1])
                if 2 <= step:
                    qk_swap(QK_ORDER[step - 2])
                if step in REL_STEPS:
                    for m in range(REL_PER):
                        rel_product(REL_PER * (step - REL_STEPS[0]) + m)
            tm_group("dv", 0)

            pe.wait_ge(sem("gla_in"), 2)
            for p in range(2):
                claim(p, ("kdT", p))
                for i in range(NT):
                    mm = pe.transpose(ps[:, p, i * P:(i + 1) * P], KD[:, p, i * P:(i + 1) * P], C("ident"))
                mm.then_inc(full[p], 1)
            for p in range(2):
                was_drained(pe, ("kdT", p))
                for n in range(NCH - 1):
                    if n < 2:
                        claim(2 + n, ("kv", p, n))
                    r = (n % 2) * GCH
                    for hh in range(2):
                        head = 2 * p + hh
                        b, c = 2 + n % 2, (n // 2) * P
                        mm = pe.matmul(ps[hh * GDK:(hh + 1) * GDK, b, c:c + P],
                                       G["kd_tm"][r:r + GCH, n // 2, p * P + hh * GDK:p * P + (hh + 1) * GDK],
                                       L0["gv"][r:r + GCH, n // 2, head * GDV:(head + 1) * GDV],
                                       start=True, stop=True, skip_group_check=True)
                    if n >= NCH - 3:
                        mm.then_inc(full[2 + n % 2], 1)

            def gla_head(head, part):
                p, r = head // 2, (head % 2) * GDK
                if part == 0:
                    claim(0, ("att", head))
                    for i in range(NT):
                        mm = pe.matmul(ps[:, 0, i * P:(i + 1) * P], L0["gk"][r:r + GDK, p, i * P:(i + 1) * P],
                                       L0["gq"][r:r + GDK, p, i * P:(i + 1) * P], start=True, stop=True)
                    mm.then_inc(full[0], 1)
                elif part == 1:
                    claim(1, ("go", head))
                    was_drained(pe, ("att", head))
                    was_drained(pe, ("kv", 1, 0))
                    for i in range(NT):
                        pe.matmul(ps[:, 1, i * P:(i + 1) * P], L0["gv"][:, i, head * GDV:(head + 1) * GDV],
                                  G["att"][:, i, :], start=True, stop=True, skip_group_check=True)
                        for n in (2 * i, 2 * i + 1):
                            if n:
                                mm = pe.matmul(ps[:, 1, n * GCH:(n + 1) * GCH],
                                               G["st"][r:r + GDK, p, n, :], QD[r:r + GDK, p, n * GCH:(n + 1) * GCH],
                                               start=False, stop=True, skip_group_check=True)
                    mm.then_inc(full[1], 1)
                elif part == 2:
                    column_sum(("go_ss", head), 0, sq[:, head % 2, :], sem("go_squared"), head + 1)
                    ada_sum("head", head)

            steps = [(i, hd) for i in range(NT) for hd in range(DH)]

            def dsa_scores(n):
                i, hd = steps[n]
                claim(2 + n % 2, ("dsa_s", n))
                pe.matmul(ps[:, 2 + n % 2, 0:(i + 1) * P], L0["qk"][:, hd, i * P:(i + 1) * P],
                          L0["qk"][:, 4 + hd, 0:(i + 1) * P], start=True, stop=True).then_inc(full[2 + n % 2], 1)

            def dsa_transposes(n):
                i, hd = steps[n]
                claim(4 + n % 2, ("dsa_pt", n))
                pe.wait_ge(sem("dsa_probs"), n + 1)
                for j in range(i + 1):
                    mm = pe.transpose(ps[:, 4 + n % 2, j * P:(j + 1) * P], T["P"][:, n % 2, j * P:(j + 1) * P],
                                      C("ident"))
                mm.then_inc(full[4 + n % 2], 1)

            def dsa_outputs(n):
                i, hd = steps[n]
                claim(6 + n % 2, ("dsa_o", n))
                was_drained(pe, ("dsa_pt", n))
                for j in range(i + 1):
                    mm = pe.matmul(ps[:, 6 + n % 2, 0:P], L0["dv"][:, j, hd * P:(hd + 1) * P],
                                   T["PT"][:, n % 2, j * P:(j + 1) * P], start=j == 0, stop=j == i)
                mm.then_inc(full[6 + n % 2], 1)
            dsa_scores(0)
            for n in range(len(steps) + 1):
                if n:
                    dsa_transposes(n - 1)
                if n + 1 < len(steps):
                    dsa_scores(n + 1)
                gla_head(*gla_part(n))
                if n:
                    dsa_outputs(n - 1)
            pe.wait_ge(sem("gla_out_done"), GH)
            for n in (-2, -1):
                was_drained(pe, ("dsa_o", len(steps) + n))
            mix_out("m0", "ab_out")
            ffn("f0", 0)

            norm_sum("n1")
            stream("cd", 0, 16)
            begin_split("cd", 16)
            first_tiles("n1", [("u", t) for t in range(4)])
            for t in range(8):
                fm_tile(("sqk", t), t % 4)
                if t:
                    column_sum(("sqk_ss", t - 1), 6, sq[:, (t - 1) % 2, :], sem("sqk_squared"), t)
            column_sum(("sqk_ss", 7), 6, sq[:, 1, :], sem("sqk_squared"), 8)
            tm_group("sv", 0)
            state["split"] = None
            for g in range(4):
                claim(7 - g % 2, ("py", g))
                pe.wait_ge(sem("pooled"), g + 1)
                pe.wait_ge(sem("pool_w_loaded"), 16)
                pe.matmul(ps[:, 7 - g % 2, :], poolw[:, g, :], L1["pooled"][:, g % 2, :],
                          start=True, stop=True).then_inc(full[7 - g % 2], 1)
            def sb_scores(hd):
                for j in reversed(range(NT)):
                    claim(j, ("z", hd, j))
                    if hd == 0 and j == NT - 1:
                        pe.wait_ge(sem("sqk_normed"), 8)
                    pe.matmul(ps[:, j, 0:S - j * P], L1["qk"][:, 4 + hd, j * P:(j + 1) * P],
                              L1["qk"][:, hd, j * P:S], start=True, stop=True).then_inc(full[j], 1)
            sb_scores(0)
            for hd in range(DH):
                for n, j in enumerate(reversed(range(NT))):
                    claim(4 + n % 2, ("aft", hd, j))
                    pe.wait_ge(sem("sb_nl"), NT * hd + n + 1)
                    mm = pe.matmul(ps[:, 4 + n % 2, 0:S - j * P], C("after"), B1["nl"][:, j, 0:S - j * P],
                                   start=True, stop=True)
                    for jj in range(j + 1, NT):
                        mm = pe.matmul(ps[:, 4 + n % 2, (jj - j) * P:S - j * P], ones[:, :],
                                       B1["nl"][:, jj, 0:S - jj * P], start=False, stop=True,
                                       skip_group_check=True)
                    mm.then_inc(full[4 + n % 2], 1)
                if hd < DH - 1:
                    sb_scores(hd + 1)
                claim(6 + hd % 2, ("so", hd))
                pe.wait_ge(sem("sb_w"), NT * (hd + 1))
                for j in range(NT):
                    mm = pe.matmul(ps[:, 6 + hd % 2, j * P:S], L1["sv"][:, j, hd * P:(hd + 1) * P],
                                   B1["w"][:, j, 0:S - j * P], start=j == 0, stop=True,
                                   skip_group_check=True)
                mm.then_inc(full[6 + hd % 2], 1)
            was_drained(pe, ("py", 3))
            for hd in range(DH):
                was_drained(pe, ("so", hd))
            mix_out("m1", "cd_out")
            ffn("f1", 1)

            norm_sum("mn", META)
            norm_sum("n2")
            pe.wait_ge(sem("mn_h"), KC)
            h2 = h_of("n2", META)
            stream("in2", 0, 48)
            first_tiles("n2", [("rq", t) for t in range(4)], h2)
            for t in range(4):
                wide_tile(("rk", t), 2 * (t % 2))
            for t in range(8):
                fm_tile(("rg", t), t % 4, h2)
            for g in range(2):
                tm_group(("rv", g), META, meta=g)

            def diff_tile(t):
                if t < 8:
                    fm_tile(("dq", t), 2 + t % 2, h2)
                else:
                    wide_tile(("dk", t - 8), 2)

            def ret_scores(n):
                hd, j = n // 5, n % 5 - 1
                q0, kp = (0, META) if j < 0 else (j * P, P)
                k0 = 0 if j < 0 else META + j * P
                claim(n % 2, ("rs", hd, j))
                pe.matmul(ps[0:kp, n % 2, 0:S - q0], RET["rk"][:, hd, k0:k0 + kp], RET["rq"][:, hd, q0:S],
                          start=True, stop=True).then_inc(full[n % 2], 1)
            for hd in range(RH):
                for v in range(2):
                    claim(4 + v, ("ro", hd, v))
                for j in range(-1, NT):
                    n = 5 * hd + j + 1
                    q0, kp = (0, META) if j < 0 else (j * P, P)
                    if n == 0:
                        ret_scores(0)
                    if n + 1 < 5 * RH:
                        ret_scores(n + 1)
                    if j < NT - 1:
                        diff_tile(NT * hd + j + 1)
                    was_drained(pe, ("rs", hd, j))
                    for v in range(2):
                        c = hd * RDV + v * P
                        vt = RET["rvm"][0:META, c:c + P] if j < 0 else RET["rv"][:, j, c:c + P]
                        mm = pe.matmul(ps[:, 4 + v, q0:S], vt, R2["sT"][0:kp, n % 2, 0:S - q0],
                                       start=j < 0, stop=True, skip_group_check=True)
                        if j == NT - 1:
                            mm.then_inc(full[4 + v], 1)
                        elif v == 1:
                            mm.then_inc(sem("ret_used"), 1)
                claim(6, ("rmu", hd))
                was_drained(pe, ("ro", hd, 1))
                for v in range(2):
                    mm = pe.matmul(ps[:, 6, :], ones[:, :], gate[:, v, :], start=v == 0, stop=v == 1)
                mm.then_inc(full[6], 1)
                claim(7, ("rvar", hd))
                pe.wait_ge(sem("ret_sq"), 2 * hd + 2)
                for v in range(2):
                    mm = pe.matmul(ps[:, 7, :], ones[:, :], sq[:, v, :], start=v == 0, stop=v == 1)
                mm.then_inc(full[7], 1)

            for g in range(2):
                tm_group(("fv", g), META, meta=g)

            def branch(st, src, uname, src_done):
                stream(uname, 0, 2 * KC)
                src_done()
                slot = ring_loop(KC // 2, 4)
                take = bank_loop(KC // 2, range(4), [(st, "b", q) for q in range(4)])
                with pe.Fori(0, KC // 2) as i:
                    for q in range(4):
                        take(i, q)
                        s = slot(i, q)
                        for k in range(KC):
                            rhs = src[:, k, :] if q % 2 else hbuf[:, k, META:SM]
                            mm = pe.matmul(ps[:, q, :], ring[:, s, k * P:(k + 1) * P], rhs,
                                           start=k == 0, stop=k == KC - 1)
                        mm.then_inc(emptied[s], 1)
            branch("br0", RET["rg"], "br0", lambda: pe.wait_ge(sem("ret_out"), 8))

            claim(7, "lam")
            pe.wait_ge(sem("lam_prod"), 1)
            pe.matmul(ps[:, 7, 0:2], ones[0:FHD, :], lamp[0:FHD, :], start=True, stop=True).then_inc(full[7], 1)
            fsteps = [(hd, i) for hd in range(FH) for i in range(NT)]

            def diff_scores(n):
                hd, i = fsteps[n]
                if n == 0:
                    for b in (1, 3):
                        pe.wait_ge(drained[b], nuse[b])
                claim(0, ("fs", n))
                for m in range(2):
                    r = m * FHD
                    q = DF["dq"][r:r + FHD, hd, i * P:(i + 1) * P]
                    mm = pe.matmul(ps[:, m, 0:(i + 1) * P], q, DF["dk"][r:r + FHD, hd, META:META + (i + 1) * P],
                                   start=True, stop=True)
                mm.then_inc(full[0], 1)
                claim(2, ("fsm", n))
                for m in range(2):
                    r = m * FHD
                    q = DF["dq"][r:r + FHD, hd, i * P:(i + 1) * P]
                    mm = pe.matmul(ps[:, 2 + m, 0:META], q, DF["dk"][r:r + FHD, hd, 0:META],
                                   start=True, stop=True)
                mm.then_inc(full[2], 1)

            def diff_transposes(n):
                hd, i = fsteps[n]
                claim(4, ("fpt", n))
                claim(5, ("fptm", n))
                pe.wait_ge(sem("diff_probs"), n + 1)
                src = F2["L"][:, n % 2, 0, :]
                for j in range(i + 1):
                    mm = pe.transpose(ps[:, 4, j * P:(j + 1) * P], src[:, META + j * P:META + (j + 1) * P], C("ident"))
                mm.then_inc(full[4], 1)
                pe.transpose(ps[0:META, 5, 0:P], src[:, 0:META], C("ident")).then_inc(full[5], 1)

            def diff_outputs(n):
                hd, i = fsteps[n]
                if i == 0:
                    claim(6, ("fo", hd))
                was_drained(pe, ("fptm", n))
                o = ps[:, 6, i * P:(i + 1) * P]
                pe.matmul(o, DF["dvm"][0:META, hd * P:(hd + 1) * P], F2["PTm"][0:META, n % 2, :],
                          start=True, stop=True, skip_group_check=True)
                for j in range(i + 1):
                    mm = pe.matmul(o, DF["dv"][:, j, hd * P:(hd + 1) * P], F2["PT"][:, n % 2, j * P:(j + 1) * P],
                                   start=False, stop=True, skip_group_check=True)
                if i == NT - 1:
                    mm.then_inc(full[6], 1)
                else:
                    mm.then_inc(sem("diff_pv"), 1)

            conv_slot = {}

            def conv_piece(t, what):
                name, half = what
                if half is None:
                    fm_tile(("cb", t), 7, h2)
                    return
                claim(7, (name, t, half), half == 1)
                if half == 0:
                    conv_slot[name] = unit()
                s = conv_slot[name]
                for k in range(KC):
                    mm = pe.matmul(ps[:, 7, 0:SM // 2], ring[:, s, k * P:(k + 1) * P],
                                   hbuf[:, k, half * SM // 2:(half + 1) * SM // 2], start=k == 0, stop=k == KC - 1)
                if half == 0:
                    mm.then_inc(full[7], 1)
                else:
                    with_unit((name, t, half))
                    mm.then_inc(emptied[s], 1)

            stream("in2", 48, 24)
            diff_scores(0)
            for n in range(len(fsteps) + 1):
                pieces = conv_pieces(n)
                if n:
                    diff_transposes(n - 1)
                if n + 1 < len(fsteps):
                    diff_scores(n + 1)
                for piece in pieces[:-1]:
                    conv_piece(*piece)
                for piece in pieces[-1:]:
                    conv_piece(*piece)
                if n:
                    diff_outputs(n - 1)
                    hd, i = fsteps[n - 1]
                    if i == 0 and hd:
                        column_sum(("fo_ss", hd - 1), 5, sq[:, (hd - 1) % 2, :], sem("fo_squared"), hd)
            column_sum(("fo_ss", FH - 1), 5, sq[:, (FH - 1) % 2, :], sem("fo_squared"), FH)
            branch("br1", OD["od"], "br1", lambda: pe.wait_ge(sem("diff_out"), FH))

            branch("br2", CV["cv"], "br2", lambda: was_drained(pe, ("cb", KC - 1)))
            for b in (1, 3):
                pe.wait_ge(drained[b], nuse[b])
            mix_out("m2", "w_out2")

            norm_sum("f2")
            for half in range(2):
                st = f"f2{half}"
                stream("up2", half * HALF2, HALF2)
                slot = ring_loop(HALF2 // 4, 4, (st, "up"))
                take = bank_loop(HALF2 // 4, range(4), [(st, "up", q) for q in range(4)])
                if half == 0:
                    first_pass("f2", slot, take)
                with pe.Fori(1 - half, HALF2 // 4) as i:
                    for q in range(4):
                        take(i, q)
                        s = slot(i, q)
                        for k in range(KC):
                            mm = products(ps[:, q, :], s, k, x_hi[:, k, :], x_lo[:, k, :], k == 0, k == KC - 1)
                        mm.then_inc(halves_read[s], 1)
                stream("down2", half * KC * 2, KC * 2)
                slot = ring_loop(2, 8, (st, "down"))
                for b in range(4):
                    pe.wait_ge(drained[b], nuse[b])
                take = bank_loop(2, range(4), [(st, "y", q) for q in range(4)], 2)
                with pe.Fori(0, 2) as i:
                    for q in range(4):
                        take(i, q)
                        for f in range(HALF2):
                            if f % 8 == 0:
                                s = slot(i, 2 * q + f // 8)
                            mm = products(ps[:, q, :], s, f % 8, hid2[:, 0, f, :], hid2[:, 1, f, :],
                                          f == 0, f == HALF2 - 1)
                            if f % 8 == 7:
                                mm.then_inc(halves_read[s], 1)
            norm_sum("nf")

        n_units = sum(c for _, _, c in units)
        assert n_units == state["u"] == N_UNITS, (n_units, state["u"])
        stream_dram = A["stream"]
        plan.extend(units)

        @block.sync
        def _(sp):
            for s in range(RING):
                sp.dma_start(ring[:, s, :], stream_dram[s, :, :]).then_inc(filled[s], 16)
            with sp.Fori(1, n_units // RING) as i:
                for s in range(RING):
                    sp.wait_ge(emptied[s], i)
                    sp.dma_start(ring[:, s, :], stream_dram[i * RING + s, :, :]).then_inc(filled[s], 16)
            for s in range(n_units % RING):
                sp.wait_ge(emptied[s], n_units // RING)
                sp.dma_start(ring[:, s, :], stream_dram[n_units - n_units % RING + s, :, :]).then_inc(filled[s], 16)
            for k in range(KC):
                sp.wait_ge(sem("nf_h"), k + 1)
                sp.dma_start(A["out"][:, k, :], hbuf[:, k, 0:S]).then_inc(sem("stored"), 16)
            sp.wait_ge(sem("stored"), 16 * KC)

        @block.scalar
        def _(act):
            chain = [0]

            def link(ins):
                chain[0] += 1
                ins.then_inc(sem("act_chain"), 1)
                act.wait_ge(sem("act_chain"), chain[0])

            def f(out, in_, func, **kw):
                return act.activation(out, in_, func, **kw)

            def drain(ins, b):
                return ins.then_inc(drained[b], 1)

            def drain_link(ins, name):
                drain(ins, uses[name][0])
                was_drained(act, name)

            act.dma_start(vecs[:, :], A["vecs"]).then_inc(sem("vecs_loaded"), 16)
            act.dma_start(consts[:, :], A["consts"]).then_inc(sem("consts_loaded"), 16)
            act.dma_start(L0["mix"][:, 0, :].bitcast(I32), A["positions"].partition_broadcast(P)).then_inc(sem("pos_loaded"), 16)
            act.dma_start(xres[:, :, :], A["x"]).then_inc(sem("x_loaded"), 16)
            act.dma_start(gate_up[:, :], A["gate_up"]).then_inc(sem("gate_up_loaded"), 16)
            act.dma_start(metaT[:, :, :], A["meta"]).then_inc(sem("meta_loaded"), 16)
            act.wait_ge(sem("vecs_loaded"), 16)
            f(cond[:, :], V("c", 0, KC), ACT.Silu).then_inc(sem("cond_ready"), 1)
            def tables():
                act.preload_act_table_set("natural_log_exp_and_others")

            def rstd(out, name, count, done):
                b = ready(act, name)
                drain_link(f(out, ps[:, b, 0:out.shape[-1]], ACT.Ln, scale=1.0 / count, bias=eps_col), name)
                f(out, out, ACT.Exp, scale=-0.5).then_inc(done, 1)

            def norm(st, src, ready_k, n=S):
                for k in range(KC):
                    ready_k(k)
                    if k >= 2:
                        act.wait_ge(sem(st + "_summed"), k - 1)
                    f(sq[:, k % 2, 0:n], src[:, k, :], ACT.Square).then_inc(sem(st + "_squared"), 1)
                rstd(rs[:, 0, 0:n], (st, "ss"), D, sem(st + "_rs"))

            def late_load(unit, m):
                act.dma_start(late_w[m][:, :, :], A["ada_late"][unit, :, :, :]).then_inc(sem(f"late_filled{m}"), 16)

            def ffn(st):
                if st == "f0":
                    act.wait_ge(sem("f0_h"), KC)
                    for m in range(2):
                        late_load(m, m)
                    with act.Fori(0, ADA_LATE - 1) as i:
                        ffn_pass(st, i, late=2)
                    ffn_pass(st, ADA_LATE - 1, late=1)
                    ffn_pass(st, ADA_LATE)
                    for m in range(2):
                        act.wait_ge(sem(f"late_read{m}"), 2 * ADA_LATE)
                else:
                    with act.Fori(0, FF // 2) as i:
                        ffn_pass(st, i)

            def ffn_pass(st, i, late=0):
                for p in range(2):
                    g, u = (st, "up", 2 * p), (st, "up", 2 * p + 1)
                    b = ready(act, g, i)
                    act.wait_ge(drained[uses[u][0]], i + uses[u][1])
                    drain(f(gate[:, p, :], ps[:, b, :], ACT.Silu), b)
                    if p < late:
                        for m in range(2):
                            act.wait_ge(sem(f"late_read{m}"), i * 2 + (p + 1))
                            late_load(i * 4 + (2 * p + m + 2), m)

            act.wait_ge(sem("small_ready"), 1)
            act.wait_ge(sem("x_loaded"), 16)
            tables()
            norm("n0", xres, lambda k: None)
            b = ready(act, "glow")
            drain(f(L0["glow"][0:GRANK, :], ps[0:GRANK, b, :], ACT.Copy), b)
            b = ready(act, "iw")
            drain(f(L0["iw"].rearrange("p a b -> p (a b)"), ps[:, b, 0:3 * IH], ACT.Copy, scale=IDX_SCALE), b)
            for t in range(2):
                b = ready(act, ("gk", t))
                drain(f(L0["gk"][:, t, :], ps[:, b, :], ACT.Copy), b)
            for p in range(2):
                b = ready(act, ("gz", p))
                f(G["gL"][:, p, :], ps[:, b, :], ACT.Abs, bias=V("gate_b", p)).then_inc(sem("gz_abs"), 1)
            for t in range(2):
                b = ready(act, ("gq", t))
                drain(f(L0["gq"][:, t, :], ps[:, b, :], ACT.Copy, scale=GDK ** -0.5), b)
            for n, name in enumerate(("sin128", "cos128", "sin64", "cos64")):
                act.wait_ge(sem("angles"), n + 1)
                sc = C("sign")[:, n // 2:n // 2 + 1] if n % 2 == 0 else 1.0
                f(L0[name], L0[name], ACT.Sin, scale=sc).then_inc(sem("rope_tables"), 1)

            def ada_out(*place):
                if place not in ADA_SUMS:
                    return
                g, b = ADA_SUMS[place]
                act.wait_ge(sem(f"ada_summed{g % 2}"), g // 2 + 1)
                drain(f(mod[:, (ADA_FIRST + g) * NT:(ADA_FIRST + g + 1) * NT], ps[:, b, 0:NT], ACT.Copy), b)
            for t in range(4):
                b = ready(act, ("gr", t))
                drain(f(L0["gr"][:, t, :], ps[:, b, :], ACT.Silu), b)
                ada_out("gr", t)
            for j in range(4):
                ada_out("gv", j)
            tables()
            for p in range(2):
                act.wait_ge(sem("gz_abs"), p + 1)
                link(f(G["gL"][:, p, :], G["gL"][:, p, :], ACT.Exp, scale=-1.0))
                f(G["gL"][:, p, :], G["gL"][:, p, :], ACT.Ln, bias=one_col).then_inc(sem("gate_ln"), 1)
            for p in range(2):
                act.wait_ge(sem("gla_diffs"), p + 1)
                f(QD[:, p, :], G["gL"][:, p, :], ACT.Exp, scale=1.0 / 16.0)
                f(KD[:, p, :], KD[:, p, :], ACT.Exp, scale=1.0 / 16.0)
                f(G["gb"][:, p, :], G["eb"][:, p, :], ACT.Exp, scale=1.0 / 16.0)
                f(G["dec"][:, p, :], G["gL"][:, p, GCH - 1:S:GCH], ACT.Exp, scale=1.0 / 16.0)
                f(G["eb"][:, p, :], G["eb"][:, p, :], ACT.Exp, scale=-1.0 / 16.0).then_inc(sem("gla_exps"), 1)

            def qk_rstd(t):
                if t >= 2:
                    act.wait_ge(sem("qk_normed"), t - 1)
                rstd(rs[:, t % 2, :], ("qk_ss", t), P, sem("qk_rs"))

            def rel_relu(n):
                w = (n // IH + 2) * P
                b = ready(act, ("rel", n))
                if n >= 2:
                    act.wait_ge(sem("idx_added"), n - 1)
                drain(f(REL[:, n % 2, 0:w], ps[:, b, 0:w], ACT.Relu), b)
            for step in range(14):
                if step < 13:
                    t = QK_ORDER[step]
                    b = ready(act, ("qk", t))
                    if t < 8:
                        drain_link(f(L0["qk"][:, t, :], ps[:, b, :], ACT.Copy), ("qk", t))
                        if t == 0:
                            act.wait_ge(sem("n0_h"), KC)
                        if t >= 2:
                            ready(act, ("qk_ss", t - 2))
                        f(sq[:, t % 2, :], L0["qk"][:, t, :], ACT.Square).then_inc(sem("qk_squared"), 1)
                    else:
                        drain(f(L0["idx"][:, t - 8, :], ps[:, b, :], ACT.Copy), b)
                    ada_out("qk", step)
                if step and QK_ORDER[step - 1] < 8:
                    qk_rstd(QK_ORDER[step - 1])
                if step in REL_STEPS:
                    for m in range(REL_PER):
                        rel_relu(REL_PER * (step - REL_STEPS[0]) + m)
            for j in range(4):
                ada_out("dv", j)
            for p in range(2):
                b = ready(act, ("kdT", p))
                drain(f(G["kd_tm"][:, :, p * P:(p + 1) * P], ps[:, b, :].rearrange("p (i c) -> p i c", c=P), ACT.Copy),
                      b)
            act.wait_ge(sem("qk_normed"), 8)

            def gla_head(head, part):
                if part == 1:
                    b = ready(act, ("go", head))
                    if head >= 2:
                        act.wait_ge(sem("gla_out_done"), head - 1)
                        ready(act, ("go_ss", head - 2))
                    drain_link(f(G["o"][:, head % 2, :], ps[:, b, :], ACT.Copy), ("go", head))
                    f(sq[:, head % 2, :], G["o"][:, head % 2, :], ACT.Square).then_inc(sem("go_squared"), 1)
                elif part == 2:
                    rstd(rs[:, head % 2, :], ("go_ss", head), P, sem("go_rs"))
                    ada_out("head", head)

            def dsa_exp(n):
                w = (n // DH + 1) * P
                act.wait_ge(sem("dsa_max"), n + 1)
                f(T["P"][:, n % 2, 0:w], T["P"][:, n % 2, 0:w], ACT.Exp, bias=T["stat"][:, n % 2, 0:1],
                  accum_out=T["stat"][:, n % 2, 1:2]).then_inc(sem("dsa_exp"), 1)

            def dsa_pt(n):
                w = (n // DH + 1) * P
                b = ready(act, ("dsa_pt", n))
                if n >= 2:
                    ready(act, ("dsa_o", n - 2))
                drain(f(T["PT"][:, n % 2, 0:w], ps[:, b, 0:w], ACT.Copy), b)

            def dsa_out(n):
                i, hd = n // DH, n % DH
                b = ready(act, ("dsa_o", n))
                drain(f(L0["mix"][:, 4 + hd, i * P:(i + 1) * P], ps[:, b, 0:P], ACT.Copy), b)
            NS = NT * DH
            for n in range(NS + 2):
                if n < NS:
                    dsa_exp(n)
                if 1 <= n <= NS:
                    gla_head(*gla_part(n - 1))
                    dsa_pt(n - 1)
                if n >= 2:
                    dsa_out(n - 2)
            norm("f0", xres, lambda k: x_chunk(act, "m0", k))
            ffn("f0")

            act.wait_ge(sem("n1_free"), 1)
            act.dma_start(poolw[:, :, :], A["pool_w"]).then_inc(sem("pool_w_loaded"), 16)
            tables()
            norm("n1", xres, lambda k: x_chunk(act, "f0", k))
            for t in range(4):
                b = ready(act, ("u", t))
                drain(f(L1["u"][:, t, META:SM], ps[:, b, :], ACT.Copy), b)

            def sqk_rstd(t):
                if t >= 2:
                    act.wait_ge(sem("sqk_normed"), t - 1)
                rstd(rs[:, t % 2, :], ("sqk_ss", t), P, sem("sqk_rs"))
            for t in range(8):
                b = ready(act, ("sqk", t))
                drain_link(f(L1["qk"][:, t, :], ps[:, b, :], ACT.Copy), ("sqk", t))
                if t == 0:
                    act.wait_ge(sem("n1_h"), KC)
                if t >= 2:
                    ready(act, ("sqk_ss", t - 2))
                f(sq[:, t % 2, :], L1["qk"][:, t, :], ACT.Square).then_inc(sem("sqk_squared"), 1)
                if t:
                    sqk_rstd(t - 1)
            sqk_rstd(7)
            for g in range(4):
                b = ready(act, ("py", g))
                drain(f(L1["mix"][:, g, :], ps[:, b, :], ACT.Copy, scale=V("pool_scale", g)), b)
            def sb_log(hd):
                for j in reversed(range(NT)):
                    w = S - j * P
                    b = ready(act, ("z", hd, j))
                    if hd:
                        act.wait_ge(sem("sb_nl"), NT * hd)
                    link(f(B1["L"][:, j, 0:w], ps[:, b, 0:w], ACT.Abs))
                    link(f(B1["L"][:, j, 0:w], B1["L"][:, j, 0:w], ACT.Exp, scale=-1.0))
                    f(B1["L"][:, j, 0:w], B1["L"][:, j, 0:w], ACT.Ln, bias=one_col).then_inc(sem("sb_ln"), 1)
            sb_log(0)
            for hd in range(DH):
                for n, j in enumerate(reversed(range(NT))):
                    w = S - j * P
                    was_drained(act, ("aft", hd, j))
                    if hd:
                        ready(act, ("so", hd - 1))
                    f(B1["w"][:, j, 0:w], B1["lb"][:, j, 0:w], ACT.Exp).then_inc(sem("sb_e"), 1)
                if hd < DH - 1:
                    sb_log(hd + 1)
                b = ready(act, ("so", hd))
                drain(f(L1["mix"][:, 4 + hd, :], ps[:, b, :], ACT.Copy), b)
            norm("f1", xres, lambda k: x_chunk(act, "m1", k))
            ffn("f1")

            act.wait_ge(sem("meta_loaded"), 16)
            x_chunk(act, "f1", KC - 1)
            act.dma_start(big[:, atd:atd + NC_B], A["tables2"]).then_inc(sem("tables2_loaded"), 16)
            tables()
            norm("mn", metaT, lambda k: None, META)
            act.wait_ge(sem("mn_h"), KC)
            norm("n2", xres, lambda k: x_chunk(act, "f1", k))
            for t in range(4):
                b = ready(act, ("rq", t))
                drain(f(RET["rq"][:, t, :], ps[:, b, :], ACT.Copy), b)

            def wide(dst, name, scale=1.0):
                for n in range(2):
                    b = ready(act, (name, n))
                    drain(f(dst[:, n * SM // 2:(n + 1) * SM // 2], ps[:, b, 0:SM // 2], ACT.Copy, scale=scale), b)
            for t in range(4):
                wide(RET["rk"][:, t, :], ("rk", t), HEAD_SCALE)
            for t in range(8):
                b = ready(act, ("rg", t))
                drain(f(RET["rg"][:, t, :], ps[:, b, :], ACT.Silu), b)
            tables()
            for hd in range(RH):
                for t in range(NT * hd, NT * hd + NT):
                    if t < 8:
                        b = ready(act, ("dq", t))
                        drain(f(DF["dq"][:, t, :], ps[:, b, :], ACT.Copy, scale=FHD ** -0.5), b)
                    else:
                        wide(DF["dk"][:, t - 8, :], ("dk", t - 8))
                for v in range(2):
                    b = ready(act, ("ro", hd, v))
                    if hd:
                        act.wait_ge(sem("ret_out"), 2 * hd)
                    drain(f(gate[:, v, :], ps[:, b, :], ACT.Copy), b)
                for v in range(2):
                    if v:
                        was_drained(act, ("rmu", hd))
                    else:
                        act.wait_ge(sem("ret_yc"), hd + 1)
                    f(sq[:, v, :], gate[:, v, :], ACT.Square).then_inc(sem("ret_sq"), 1)
                rstd(rs[:, hd % 2, :], ("rvar", hd), RDV, sem("ret_rs"))

            def branch(st):
                with act.Fori(0, KC // 2) as i:
                    for p in range(2):
                        g, u = (st, "b", 2 * p), (st, "b", 2 * p + 1)
                        b = ready(act, g, i)
                        act.wait_ge(drained[uses[u][0]], i + uses[u][1])
                        drain(f(gate[:, p, :], ps[:, b, :], ACT.Sigmoid), b)
            act.wait_ge(sem("ret_out"), 8)
            branch("br0")
            b = ready(act, "lam")
            tables()
            drain(f(lam_e, ps[:, b, 0:2], ACT.Exp), b)

            def diff_exp(n):
                w = META + (n % NT + 1) * P
                act.wait_ge(sem("diff_max"), n + 1)
                for m in range(2):
                    ins = f(F2["L"][:, n % 2, m, 0:w], F2["L"][:, n % 2, m, 0:w], ACT.Exp,
                            bias=F2["stat"][:, n % 2, m:m + 1], accum_out=F2["stat"][:, n % 2, 2 + m:3 + m])
                ins.then_inc(sem("diff_exp"), 1)

            def diff_pt(n):
                w = (n % NT + 1) * P
                if n >= 2:
                    if (n - 2) % NT == NT - 1:
                        ready(act, ("fo", (n - 2) // NT))
                    else:
                        act.wait_ge(sem("diff_pv"), (NT - 1) * ((n - 2) // NT) + (n - 2) % NT + 1)
                b = ready(act, ("fpt", n))
                drain(f(F2["PT"][:, n % 2, 0:w], ps[:, b, 0:w], ACT.Copy), b)
                b = ready(act, ("fptm", n))
                drain(f(F2["PTm"][0:META, n % 2, :], ps[0:META, b, 0:P], ACT.Copy), b)

            def diff_square(hd):
                b = ready(act, ("fo", hd))
                if hd >= 2:
                    ready(act, ("fo_ss", hd - 2))
                drain_link(f(OD["od"][:, hd, :], ps[:, b, :], ACT.Copy), ("fo", hd))
                f(sq[:, hd % 2, :], OD["od"][:, hd, :], ACT.Square).then_inc(sem("fo_squared"), 1)

            def diff_rstd(hd):
                if hd >= 2:
                    act.wait_ge(sem("diff_out"), hd - 1)
                rstd(rs[:, hd % 2, :], ("fo_ss", hd), P, sem("fo_rs"))
            NF = FH * NT

            def conv_copy(t, what):
                name, half = what
                if name == "cc":
                    if t >= 2:
                        was_drained(act, ("cb", t - 2))
                    b = ready(act, (name, t, half))
                    drain(f(CV["u"][:, t % 2, half * SM // 2:(half + 1) * SM // 2], ps[:, b, 0:SM // 2], ACT.Copy), b)
            for n in range(NF + 1):
                if n < NF:
                    diff_exp(n)
                if n:
                    for piece in conv_pieces(n - 1):
                        conv_copy(*piece)
                    diff_pt(n - 1)
                    hd, i = (n - 1) // NT, (n - 1) % NT
                    if i == NT - 1:
                        diff_square(hd)
                    if i == 0 and hd:
                        diff_rstd(hd - 1)
            diff_rstd(FH - 1)
            act.wait_ge(sem("diff_out"), FH)
            branch("br1")
            branch("br2")
            tables()
            norm("f2", xres, lambda k: x_chunk(act, "m2", k))
            for half in range(2):
                st = f"f2{half}"
                with act.Fori(0, HALF2 // 4) as i:
                    for q in range(4):
                        b2, use = uses[(st, "up", (q + 2) % 4)]
                        act.wait_ge(drained[b2], i + (use + (1 if q >= 2 else 0)))
                        b = ready(act, (st, "up", q), i)
                        f(gate[:, q % 2, :], ps[:, b, :], ACT.Relu).then_inc(sem("f2_relu"), 1)
                        act.wait_ge(sem("f2_relu"), i * 4 + (half * HALF2 + q + 1))
                        f(sq[:, q % 2, :], gate[:, q % 2, :], ACT.Square).then_inc(sem("f2_squares"), 1)
            norm("nf", xres, lambda k: x_chunk(act, "f21", k))

        @block.gpsimd
        def _(pool):
            SLOTS = 2
            weights = G["ada_w"]

            def load(slot, unit):
                pool.dma_start(weights[:, slot, :, :], A["ada_rest"][unit, :, :, :]).then_inc(sem(f"ada_filled{slot}"), 16)

            def group(i, h, refill=ADA_UNITS, first=False):
                acc = G["ada_acc"][:, h, :]
                for j in range(ADA_UNITS):
                    slot = j % SLOTS
                    w = weights[:, slot, :, :]
                    pool.wait_ge(sem(f"ada_filled{slot}"), i * 64 + 16 * (2 * h + j // 2 + 1))
                    pool.tensor_tensor(w, w, cond[:, 2 * j:2 * j + 2].unsqueeze(2).broadcast_to((P, 2, S)), ALU.mult)                        .then_inc(sem("ada_scaled"), 1)
                    pool.wait_ge(sem("ada_scaled"), i * 8 + (4 * h + j + 1))
                    if j == 0:
                        if not first:
                            pool.wait_ge(sem(f"ada_summed{h}"), i)
                        pool.tensor_tensor(acc, w[:, 0, :], w[:, 1, :], ALU.add).then_inc(sem("ada_added"), 1)
                    else:
                        for kk in range(2):
                            pool.wait_ge(sem("ada_added"), i * (2 * ADA_ADDS) + (ADA_ADDS * h + 2 * j - 1 + kk))
                            pool.tensor_tensor(acc, acc, w[:, kk, :], ALU.add).then_inc(sem("ada_added"), 1)
                    if j < refill:
                        pool.wait_ge(sem("ada_added"), i * (2 * ADA_ADDS) + (ADA_ADDS * h + 2 * j + 1))
                        load(slot, i * 8 + (4 * h + j + SLOTS))
            pool.wait_ge(emptied[ADA_UNITS - 1], ADA_FIRST)
            for slot in range(SLOTS):
                load(slot, slot)
            for h in range(2):
                group(0, h, first=True)
            with pool.Fori(1, ADA_REST // 2 - 1) as i:
                for h in range(2):
                    group(i, h)
            group(ADA_REST // 2 - 1, 0)
            group(ADA_REST // 2 - 1, 1, refill=ADA_UNITS - SLOTS)

            def split_units(*section):
                base, count, before = split_at[section]

                def one_pass(i, fresh=False):
                    for n in range(RING):
                        u = base + n
                        s = u % RING
                        w = ring[:, s, :]
                        pool.wait_ge(filled[s], i * 16 + 16 * (u // RING + 1))
                        if not fresh:
                            pool.wait_ge(halves_read[s], i + before)
                        pool.tensor_tensor(halves[:, s, 0, :], w, ones[:, 0:1].broadcast_to((P, UNIT)), ALU.mult)\
                            .then_inc(upper_made[s], 1)
                        pool.wait_ge(upper_made[s], i + (before + 1))
                        pool.tensor_tensor(halves[:, s, 1, :], w, halves[:, s, 0, :].bitcast(F32), ALU.subtract)\
                            .then_inc(emptied[s], 1)
                first = 0 if before else 1
                if first:
                    one_pass(0, fresh=True)
                with pool.Fori(first, count // RING) as i:
                    one_pass(i)
            pool.wait_ge(sem("gla_out_done"), GH)
            split_units("m0", "out")
            split_units("f0", "up")
            split_units("f0", "down")
            split_units("cd")
            split_units("m1", "out")
            split_units("f1", "up")
            split_units("f1", "down")
            pool.wait_ge(drained[3], uses[("br2", "b", 3)][1] + KC // 2)
            split_units("m2", "out")
            for half in range(2):
                split_units(f"f2{half}", "up")
                split_units(f"f2{half}", "down")

        @block.vector
        def _(dve):
            chain = [0]

            def link(ins):
                chain[0] += 1
                ins.then_inc(sem("dve_chain"), 1)
                dve.wait_ge(sem("dve_chain"), chain[0])

            def drain(ins, b):
                return ins.then_inc(drained[b], 1)

            def drain_link(ins, name):
                drain(ins, uses[name][0])
                was_drained(dve, name)

            tt, stt, ts = dve.tensor_tensor, dve.scalar_tensor_tensor, dve.tensor_scalar

            dve.memset(ones[:, :], 1.0)
            dve.memset(eps_col, EPS)
            link(dve.memset(one_col, 1.0))
            dve.wait_ge(sem("vecs_loaded"), 16)
            ts(subln_s, V("subln"), 1.0 - LAM_INIT, None, ALU.mult)
            ts(sbq_s, V("sb_q"), HEAD_SCALE, None, ALU.mult)
            tt(lamp[:, 0:1], V("lam", 0)[0:FHD], V("lam", 1)[0:FHD], ALU.mult)
            tt(lamp[:, 1:2], V("lam", 2)[0:FHD], V("lam", 3)[0:FHD], ALU.mult).then_inc(sem("lam_prod"), 1)
            dve.memset(G["att"], 0.0).then_inc(sem("small_ready"), 1)

            dve.wait_ge(sem("cond_ready"), 1)
            with dve.Fori(0, ADA_FIRST) as i:
                acc = ada_first[:, bass.ds(i, 1), :]
                for j in range(ADA_UNITS):
                    for kk in range(2):
                        w = ring[:, j:j + 1, kk * S:(kk + 1) * S]
                        ck = cond[:, 2 * j + kk:2 * j + kk + 1]
                        if kk == 0:
                            dve.wait_ge(filled[j], i * 16 + 16)
                        else:
                            dve.wait_ge(sem("ada_half"), i * ADA_UNITS + j + 1)
                        if j == kk == 0:
                            ins = ts(acc, w, ck, None, ALU.mult)
                        else:
                            if kk == 0:
                                dve.wait_ge(emptied[j - 1], i + 1)
                            ins = stt(acc, w, ck, acc, ALU.mult, ALU.add)
                        ins.then_inc(emptied[j] if kk else sem("ada_half"), 1)
            b = ready(dve, "ada_first")
            drain_link(tt(mod[:, 0:ADA_FIRST * NT], ps[:, b, 0:ADA_FIRST * NT], V("ada_b", 0, ADA_FIRST * NT), ALU.add),
                       "ada_first")

            def M(layer, part, k=0, n=1):
                a = layer * 48 + part * KC + k
                return mod[:, a:a + n]

            def split(v, st, k):
                link(dve.tensor_copy(x_hi[:, k, :], v))
                tt(x_lo[:, k, :], v, x_hi[:, k, :].bitcast(F32), ALU.subtract).then_inc(sem(st + "_split"), 1)

            def split_norm(st, src, weight, layer=None, part=0):
                if layer is not None:
                    link(stt(coef[:, :], M(layer, part + 1, 0, KC), 1.0, weight, ALU.add, ALU.mult))
                    weight = coef[:, :]
                dve.wait_ge(sem(st + "_rs"), 1)

                def scaled(k):
                    stt(gate[:, k % 2, :], src[:, k, :], weight[:, k:k + 1], rs[:, 0, :], ALU.mult, ALU.mult)\
                        .then_inc(sem(st + "_scaled"), 1)

                def upper(k):
                    shift = 0.0 if layer is None else M(layer, part, k)
                    dve.wait_ge(sem(st + "_scaled"), k + 1)
                    ts(x_hi[:, k, :], gate[:, k % 2, :], shift, None, ALU.add).then_inc(sem(st + "_upper"), 1)

                def lower(k):
                    shift = 0.0 if layer is None else M(layer, part, k)
                    dve.wait_ge(sem(st + "_upper"), k + 1)
                    stt(x_lo[:, k, :], gate[:, k % 2, :], shift, x_hi[:, k, :].bitcast(F32), ALU.add, ALU.subtract)\
                        .then_inc(sem(st + "_h"), 1)
                for k in range(KC):
                    if k >= 2:
                        dve.wait_ge(sem(st + "_h"), k - 1)
                    scaled(k)
                    upper(k)
                    lower(k)

            def norm(st, src, weight, dst, layer=None, part=0, n=S):
                if layer is not None:
                    link(stt(coef[:, :], M(layer, part + 1, 0, KC), 1.0, weight, ALU.add, ALU.mult))
                    weight = coef[:, :]
                dve.wait_ge(sem(st + "_rs"), 1)
                for k in range(KC):
                    out = dst(k)
                    ins = stt(out, src[:, k, :], weight[:, k:k + 1], rs[:, 0, 0:n], ALU.mult, ALU.mult)
                    if layer is not None:
                        link(ins)
                        ins = ts(out, out, M(layer, part, k), None, ALU.add)
                    ins.then_inc(sem(st + "_h"), 1)

            def hd_(off=0, n=S):
                return lambda k: hbuf[:, k, off:off + n]

            def add_out(st, layer=None, part=0):
                with dve.Fori(0, 2) as i:
                    for q in range(4):
                        b = ready(dve, (st, "y", q), i)
                        xk = xres[:, bass.ds(i * 4 + q, 1), :]
                        y = ps[:, b:b + 1, :]
                        if layer is None:
                            drain(tt(xk, y, xk, ALU.add), b)
                        else:
                            g = mod[:, bass.ds(i * 4 + (layer * 48 + part * KC + q), 1)]
                            drain(stt(xk, y, g, xk, ALU.mult, ALU.add), b)

            def late_unit(i, j):
                m = j % 2
                acc = ps[:, 5, :]
                w = late_w[m]
                dve.wait_ge(sem(f"late_filled{m}"), i * 32 + 16 * (j // 2 + 1))
                for kk in range(2):
                    n = 2 * j + kk
                    ck = cond[:, n:n + 1]
                    if n == 0:
                        ins = ts(acc, w[:, kk, :], ck, None, ALU.mult)
                    else:
                        dve.wait_ge(sem("late_half") if kk else sem(f"late_read{1 - m}"),
                                    i * (ADA_UNITS if kk else 2) + (j + 1 if kk else (j - 1) // 2 + 1))
                        last = n == 2 * ADA_UNITS - 1
                        if last:
                            dve.wait_ge(sem("late_sum_free"), i + 1)
                        ins = stt(C("chunk_carry") if last else acc, w[:, kk, :], ck, acc, ALU.mult, ALU.add)
                    ins.then_inc(sem(f"late_read{m}") if kk else sem("late_half"), 1)

            def ffn(st):
                if st == "f0":
                    dve.memset(C("chunk_carry"), 0.0).then_inc(sem("late_sum_free"), 1)
                    with dve.Fori(0, ADA_LATE) as i:
                        ffn_pass(st, i, True)
                    ffn_pass(st, ADA_LATE, False)
                else:
                    with dve.Fori(0, FF // 2) as i:
                        ffn_pass(st, i, False)

            def ffn_pass(st, i, late):
                for p in range(2):
                    was_drained(dve, (st, "up", 2 * p), i)
                    b = ready(dve, (st, "up", 2 * p + 1), i)
                    g = gate[:, p:p + 1, :]
                    if type(i) is int:
                        at = slice(i * 2 + p, i * 2 + p + 1)
                    else:
                        at = bass.ds(i * 2 + p, 1)
                    hi, lo = hid[:, 0, at, :], hid[:, 1, at, :]
                    tt(g, g, ps[:, b:b + 1, :], ALU.mult).then_inc(sem(st + "_hidden"), 1)
                    dve.wait_ge(sem(st + "_hidden"), i * 2 + p + 1)
                    dve.tensor_copy(hi, g).then_inc(sem(st + "_upper_half"), 1)
                    dve.wait_ge(sem(st + "_upper_half"), i * 2 + p + 1)
                    drain(tt(lo, g, hi.bitcast(F32), ALU.subtract), b)
                    if late:
                        late_unit(i, 2 * p)
                        late_unit(i, 2 * p + 1)

            norm("n0", xres, V("mix_norm", 0, KC), hd_(), 0, 0)
            dve.wait_ge(sem("pos_loaded"), 16)
            dve.wait_ge(sem("consts_loaded"), 16)
            pos, ang, turns = L0["mix"][:, 1, :], L0["mix"][:, 2, :], L0["mix"][:, 3, :]
            link(dve.tensor_copy(pos, L0["mix"][:, 0, :].bitcast(I32)))
            MAGIC = 1.5 * 2.0 ** 23
            C1 = 6.28125
            C2 = float(np.float32(int((2 * np.pi - C1) * 2 ** 21) / 2.0 ** 21))
            C3 = float(np.float32(2 * np.pi - C1 - C2))
            for fr, names in enumerate((("sin128", "cos128"), ("sin64", "cos64"))):
                link(ts(ang, pos, C("invf")[:, fr:fr + 1], None, ALU.mult))
                for q, name in enumerate(names):
                    link(ts(turns, ang, float(1.0 / (2.0 * np.pi)), 0.25 * q, ALU.mult, ALU.add))
                    link(ts(turns, turns, MAGIC, MAGIC, ALU.add, ALU.subtract))
                    r = L0[name]
                    link(stt(r, turns, -C1, ang, ALU.mult, ALU.add))
                    link(stt(r, turns, -C2, r, ALU.mult, ALU.add))
                    link(stt(r, turns, -C3, r, ALU.mult, ALU.add))
                    if q:
                        link(ts(r, r, float(np.pi / 2), None, ALU.add))
                    ts(r, r, 3.1415925, -3.1415925, ALU.min, ALU.max).then_inc(sem("angles"), 1)
            for p in range(2):
                b = ready(dve, ("gz", p))
                dve.wait_ge(sem("gz_abs"), p + 1)
                drain(ts(G["gb"][:, p, :], ps[:, b, :], V("gate_b", p), 0.0, ALU.add, ALU.min), b)
            for i in range(NT):
                b = ready(dve, ("gv", i))
                drain(dve.tensor_copy(L0["gv"][:, i, :], ps[:, b, :]), b)
            for p in range(2):
                bv = G["gL"][:, p, :]
                b3 = bv.rearrange("p (n c) -> p n c", c=GCH)
                dve.wait_ge(sem("gate_ln"), p + 1)
                link(tt(G["gb"][:, p, :], G["gb"][:, p, :], bv, ALU.subtract))
                link(dve.tensor_tensor_scan(bv, C("chunk_carry"), G["gb"][:, p, :], 0.0, ALU.mult, ALU.add))
                tt(G["eb"][:, p, :].rearrange("p (n c) -> p n c", c=GCH), b3,
                   b3[:, :, GCH // 2 - 1:GCH // 2].broadcast_to((P, NCH, GCH)), ALU.subtract)
                tt(KD[:, p, :].rearrange("p (n c) -> p n c", c=GCH),
                   b3[:, :, GCH - 1:GCH].broadcast_to((P, NCH, GCH)), b3, ALU.subtract).then_inc(sem("gla_diffs"), 1)
            for p in range(2):
                dve.wait_ge(sem("gla_exps"), p + 1)
                was_drained(dve, ("gq", p))
                was_drained(dve, ("gk", p))
                tt(QD[:, p, :], QD[:, p, :], L0["gq"][:, p, :], ALU.mult)
                tt(KD[:, p, :], KD[:, p, :], L0["gk"][:, p, :], ALU.mult)
                tt(L0["gq"][:, p, :], L0["gq"][:, p, :], G["gb"][:, p, :], ALU.mult)
                tt(L0["gk"][:, p, :], L0["gk"][:, p, :], G["eb"][:, p, :], ALU.mult).then_inc(sem("gla_in"), 1)

            def rotate(t, turn):
                v = L0["qk"][:, t, :] if t < 8 else L0["idx"][:, t - 8, :]
                sn, cs = (L0["sin128"], L0["cos128"]) if t < 8 else (L0["sin64"], L0["cos64"])
                b = ready(dve, ("qk_swap", t))
                if turn:
                    dve.wait_ge(sem("qk_rotated"), turn)
                drain(tt(gate[:, 1, :], ps[:, b, :], sn, ALU.mult), b)
                link(tt(v, v, cs, ALU.mult))
                tt(v, v, gate[:, 1, :], ALU.add).then_inc(sem("qk_rotated"), 1)
            dve.wait_ge(sem("rope_tables"), 4)

            def index_add(n):
                i, hd = n // IH + 1, n % IH
                w = (i + 1) * P
                sc = SCORE[:, i % 2, 0:w]
                was_drained(dve, ("rel", n))
                wt = L0["iw"][:, i - 1, hd:hd + 1]
                if hd == 0:
                    ins = ts(sc, REL[:, n % 2, 0:w], wt, None, ALU.mult)
                else:
                    ins = stt(sc, REL[:, n % 2, 0:w], wt, sc, ALU.mult, ALU.add)
                ins.then_inc(sem("idx_added"), 1)
                dve.wait_ge(sem("idx_added"), n + 1)

            def topk_rounds(i, rounds):
                w = (i + 1) * P
                sc = SCORE[:, i % 2, 0:w]
                for r in rounds:
                    if r == 0:
                        link(tt(sc[:, w - P:w], sc[:, w - P:w], C("tri_bias"), ALU.add))
                    link(dve.max(G["top"], sc))
                    link(dve.match_replace(sc, G["top"], sc, TAKEN))
                    if r == TOPK // 8 - 1:
                        link(ts(KEEP[i][:, 0:w], sc, TAKEN / 2, NEG, ALU.is_gt, ALU.mult))
            was_drained(dve, "iw")
            for step in range(15):
                if step in REL_STEPS:
                    for m in range(REL_PER):
                        index_add(REL_PER * (step - REL_STEPS[0]) + m)
                if step < 13 and QK_ORDER[step] < 8:
                    t = QK_ORDER[step]
                    dve.wait_ge(sem("qk_rs"), t + 1)
                    v = L0["qk"][:, t, :]
                    stt(v, v, V("dsa_q" if t < 4 else "dsa_k"), rs[:, t % 2, :], ALU.mult, ALU.mult)\
                        .then_inc(sem("qk_normed"), 1)
                if 1 <= step <= 13:
                    rotate(QK_ORDER[step - 1], step - 1)
                if step in TOPK_ROUNDS:
                    topk_rounds(*TOPK_ROUNDS[step])
            for i in range(NT):
                b = ready(dve, ("dv", i))
                drain(dve.tensor_copy(L0["dv"][:, i, :], ps[:, b, :]), b)
            for p in range(2):
                for n in range(NCH - 1):
                    b = ready(dve, ("kv", p, n % 2))
                    kv = ps[:, b, (n // 2) * P:(n // 2 + 1) * P]
                    if n == 0:
                        ins = dve.tensor_copy(G["st"][:, p, 1, :], kv)
                    else:
                        ins = stt(G["st"][:, p, n + 1, :], G["st"][:, p, n, :], G["dec"][:, p, n:n + 1], kv,
                                  ALU.mult, ALU.add)
                    if n >= NCH - 3:
                        drain_link(ins, ("kv", p, n % 2))
                    else:
                        link(ins)

            def gla_mask(head):
                b = ready(dve, ("att", head))
                if head:
                    ready(dve, ("go", head - 1))
                for i in range(NT):
                    ins = dve.copy_predicated(G["att"][:, i, :], C("gla_mask").bitcast(I32), ps[:, b, i * P:(i + 1) * P])
                drain(ins, b)

            def gla_out(head):
                dve.wait_ge(sem("go_rs"), head + 1)
                o = G["o"][:, head % 2, :]
                link(stt(o, o, V("gla_out"), rs[:, head % 2, :], ALU.mult, ALU.mult))
                tt(L0["mix"][:, head, :], o, L0["gr"][:, head, :], ALU.mult).then_inc(sem("gla_out_done"), 1)
            def dsa_front(n):
                i, hd = n // DH, n % DH
                w = (i + 1) * P
                b = ready(dve, ("dsa_s", n))
                if n >= 2:
                    ready(dve, ("dsa_pt", n - 2))
                drain_link(stt(T["P"][:, n % 2, 0:w], ps[:, b, 0:w], HEAD_SCALE, KEEP[i][:, 0:w],
                               ALU.mult, ALU.add), ("dsa_s", n))
                dve.tensor_reduce(T["stat"][:, n % 2, 0:1], T["P"][:, n % 2, 0:w], AX, ALU.max, negate=True)\
                    .then_inc(sem("dsa_max"), 1)

            def dsa_back(n):
                w = (n // DH + 1) * P
                dve.wait_ge(sem("dsa_exp"), n + 1)
                link(dve.reciprocal(T["stat"][:, n % 2, 2:3], T["stat"][:, n % 2, 1:2]))
                ts(T["P"][:, n % 2, 0:w], T["P"][:, n % 2, 0:w], T["stat"][:, n % 2, 2:3], None, ALU.mult)\
                    .then_inc(sem("dsa_probs"), 1)
            NS = NT * DH
            for n in range(NS + 1):
                if n < NS:
                    dsa_front(n)
                if n:
                    dsa_back(n - 1)
                head, part = gla_part(n - 1) if n else (0, None)
                if part == 0:
                    gla_mask(head)
                elif part == 2:
                    gla_out(head)
                    dve.wait_ge(sem("gla_out_done"), head + 1)
                    split(L0["mix"][:, head, :], "m0", head)
            was_drained(dve, ("ada", ADA_REST - 1))
            rest = mod[:, ADA_FIRST * NT:(ADA_FIRST + ADA_REST) * NT]
            link(tt(rest, rest, V("ada_b", ADA_FIRST * NT, ADA_REST * NT), ALU.add))
            for hd in range(DH):
                was_drained(dve, ("dsa_o", NS - DH + hd))
                split(L0["mix"][:, GH + hd, :], "m0", GH + hd)
            add_out("m0", 0, 2)
            split_norm("f0", xres, V("ffn_norm", 0, KC), 0, 3)
            ffn("f0")
            add_out("f0", 0, 5)
            dve.wait_ge(sem("late_sum_free"), ADA_LATE + 1)
            first = (ADA_FIRST + ADA_REST) * NT
            drain_link(tt(mod[:, first:2 * 48], ps[:, 7, 0:ADA_LATE * NT], V("ada_b", first, ADA_LATE * NT), ALU.add), "late")

            x_chunk(dve, "f0", KC - 1)
            dve.memset(L1["u"][:, :, 0:META], 0.0)
            link(dve.memset(L1["s"][:, :, 0:META], 0.0))
            dve.memset(L1["pooled"][:, :, 0:1], 0.0).then_inc(sem("n1_free"), 1)
            split_norm("n1", xres, V("mix_norm", KC, KC), 1, 0)
            for t in range(8):
                dve.wait_ge(sem("sqk_rs"), t + 1)
                v = L1["qk"][:, t, :]
                stt(v, v, sbq_s if t < 4 else V("sb_k"), rs[:, t % 2, :], ALU.mult, ALU.mult)\
                    .then_inc(sem("sqk_normed"), 1)
            for i in range(NT):
                b = ready(dve, ("sv", i))
                drain(dve.tensor_copy(L1["sv"][:, i, :], ps[:, b, :]), b)
            for g, win in enumerate(WINDOWS):
                was_drained(dve, ("u", g))
                u = L1["u"][:, g, :]
                src, width, w = u, 1, 0
                while width < win:
                    dst = L1["s"][:, w, :]
                    link(tt(dst[:, META:SM], src[:, META:SM], src[:, META - width:SM - width], ALU.add))
                    src, width, w = dst, 2 * width, 1 - w
                if g >= 2:
                    ready(dve, ("py", g - 2))
                out = L1["pooled"][:, g % 2, :]
                link(stt(out, src[:, META:SM], 1.0 / win, u[:, META:SM], ALU.mult, ALU.subtract))
                link(tt(out[:, 0:16], src[:, META:META + 16], C("pool_rc")[:, g * 16:(g + 1) * 16], ALU.mult))
                tt(out[:, 0:16], out[:, 0:16], u[:, META:META + 16], ALU.subtract).then_inc(sem("pooled"), 1)
            def sb_parts(hd):
                for n, j in enumerate(reversed(range(NT))):
                    w = S - j * P
                    dve.wait_ge(sem("sb_ln"), NT * hd + n + 1)
                    b = uses[("z", hd, j)][0]
                    link(stt(B1["nl"][:, j, 0:w], ps[:, b, 0:w], 0.0, B1["L"][:, j, 0:w], ALU.max, ALU.add))
                    drain(stt(B1["lb"][:, j, 0:w], ps[:, b, 0:w], 0.0, B1["L"][:, j, 0:w], ALU.min, ALU.subtract), b)
                    tt(B1["nl"][:, j, 0:P], B1["nl"][:, j, 0:P], C("strict"), ALU.mult).then_inc(sem("sb_nl"), 1)
            sb_parts(0)
            for hd in range(DH):
                for n, j in enumerate(reversed(range(NT))):
                    w = S - j * P
                    b = ready(dve, ("aft", hd, j))
                    drain(tt(B1["lb"][:, j, 0:w], B1["lb"][:, j, 0:w], ps[:, b, 0:w], ALU.subtract), b)
                for n, j in enumerate(reversed(range(NT))):
                    dve.wait_ge(sem("sb_e"), NT * hd + n + 1)
                    tt(B1["w"][:, j, 0:P], B1["w"][:, j, 0:P], C("strict"), ALU.mult).then_inc(sem("sb_w"), 1)
                if hd < DH - 1:
                    sb_parts(hd + 1)
                if hd == 0:
                    for k in range(4):
                        was_drained(dve, ("py", k))
                        split(L1["mix"][:, k, :], "m1", k)
                else:
                    was_drained(dve, ("so", hd - 1))
                    split(L1["mix"][:, 3 + hd, :], "m1", 3 + hd)
            was_drained(dve, ("so", DH - 1))
            split(L1["mix"][:, KC - 1, :], "m1", KC - 1)
            add_out("m1", 1, 2)
            split_norm("f1", xres, V("ffn_norm", KC, KC), 1, 3)
            ffn("f1")
            add_out("f1", 1, 5)

            x_chunk(dve, "f1", KC - 1)
            norm("mn", metaT, V("norm1", 0, KC), hd_(0, META), n=META)
            norm("n2", xres, V("norm1", 0, KC), hd_(META))

            def token_major(name, dst, dstm):
                for g in range(2):
                    for i in range(NT):
                        b = ready(dve, ((name, g), i))
                        drain(dve.tensor_copy(dst[:, i, g * S:(g + 1) * S], ps[:, b, :]), b)
                    b = ready(dve, ((name, g), "m"))
                    drain(dve.tensor_copy(dstm[0:META, g * S:(g + 1) * S], ps[0:META, b, :]), b)
            token_major("rv", RET["rv"], RET["rvm"])
            dve.wait_ge(sem("tables2_loaded"), 16)
            for hd in range(RH):
                for j in range(-1, NT):
                    n = 5 * hd + j + 1
                    w, c0, kp = (S, META, META) if j < 0 else (S - j * P, 0, P)
                    b = ready(dve, ("rs", hd, j))
                    if n >= 2:
                        if (n - 2) % 5 == 4:
                            ready(dve, ("ro", (n - 2) // 5, 1))
                        else:
                            dve.wait_ge(sem("ret_used"), 4 * ((n - 2) // 5) + (n - 2) % 5 + 1)
                    drain(tt(R2["sT"][0:kp, n % 2, 0:w], ps[0:kp, b, 0:w], R2["decay"][0:kp, hd, c0:c0 + w], ALU.mult),
                          b)
                b = ready(dve, ("rmu", hd))
                was_drained(dve, ("ro", hd, 1))
                for v in range(2):
                    ins = stt(gate[:, v, :], ps[:, b, :], -1.0 / RDV, gate[:, v, :], ALU.mult, ALU.add)
                    ins.then_inc(drained[b] if v else sem("ret_yc"), 1)
                was_drained(dve, ("rg", 7))
                dve.wait_ge(sem("ret_rs"), hd + 1)
                for v in range(2):
                    link(tt(gate[:, v, :], gate[:, v, :], rs[:, hd % 2, :], ALU.mult))
                    r = RET["rg"][:, 2 * hd + v, :]
                    tt(r, r, gate[:, v, :], ALU.mult).then_inc(sem("ret_out"), 1)

            def branch(st, first):
                with dve.Fori(0, KC // 2) as i:
                    for p in range(2):
                        m = RET["merged"][:, bass.ds(i * 2 + p, 1), :]
                        was_drained(dve, (st, "b", 2 * p), i)
                        b = ready(dve, (st, "b", 2 * p + 1), i)
                        g, y = gate[:, p:p + 1, :], ps[:, b:b + 1, :]
                        if first:
                            drain(tt(m, g, y, ALU.mult), b)
                        else:
                            tt(sq[:, p:p + 1, :], g, y, ALU.mult).then_inc(sem(st + "_gated"), 1)
                            dve.wait_ge(sem(st + "_gated"), i * 2 + p + 1)
                            drain(tt(m, m, sq[:, p:p + 1, :], ALU.add), b)
            token_major("fv", DF["dv"], DF["dvm"])
            branch("br0", True)
            was_drained(dve, "lam")
            link(stt(neg_lam, small[:, 7:8], -LAM_INIT, small[:, 6:7], ALU.add, ALU.subtract))

            def diff_front(n):
                hd, i = n // NT, n % NT
                w = (i + 1) * P
                slope = float(2.0 ** (-8.0 / FH * (hd + 1.0)))
                if n >= 2:
                    ready(dve, ("fptm", n - 2))
                ready(dve, ("fs", n))
                L = F2["L"][:, n % 2, :, :]
                c0 = SM - w - META
                dist = R2["dist"].unsqueeze(1)
                drain(stt(L[:, :, META:META + w], dist[:, :, c0 + META:SM].broadcast_to((P, 2, w)), slope,
                          ps[:, 0:2, 0:w], ALU.mult, ALU.add), 0)
                ready(dve, ("fsm", n))
                drain_link(stt(L[:, :, 0:META], dist[:, :, c0:c0 + META].broadcast_to((P, 2, META)), slope,
                               ps[:, 2:4, 0:META], ALU.mult, ALU.add),
                           ("fsm", n))
                dve.tensor_reduce(F2["stat"][:, n % 2, 0:2], L[:, :, 0:META + w], AX, ALU.max, negate=True)\
                    .then_inc(sem("diff_max"), 1)

            def diff_back(n):
                w = META + (n % NT + 1) * P
                L, st = F2["L"][:, n % 2, :, 0:w], F2["stat"][:, n % 2, :]
                dve.wait_ge(sem("diff_exp"), n + 1)
                link(dve.reciprocal(st[:, 4:6], st[:, 2:4]))
                ts(st[:, 6:7], st[:, 5:6], neg_lam, None, ALU.mult)
                link(ts(L[:, 0, :], L[:, 0, :], st[:, 4:5], None, ALU.mult))
                stt(L[:, 0, :], L[:, 1, :], st[:, 6:7], L[:, 0, :], ALU.mult, ALU.add).then_inc(sem("diff_probs"), 1)

            def diff_norm(hd):
                dve.wait_ge(sem("fo_rs"), hd + 1)
                o = OD["od"][:, hd, :]
                stt(o, o, subln_s, rs[:, hd % 2, :], ALU.mult, ALU.mult).then_inc(sem("diff_out"), 1)
            NF = FH * NT

            def conv_part(t, what):
                name, half = what
                u = CV["u"][:, t % 2, :]
                cv = CV["cv"][:, t, :]
                if name == "cx":
                    was_drained(dve, ("cc", t, half))
                    b = ready(dve, (name, t, half))
                    uh = u[:, half * SM // 2:(half + 1) * SM // 2]
                    drain_link(tt(uh, uh, ps[:, b, 0:SM // 2], ALU.mult), (name, t, half))
                elif name == "cb":
                    link(ts(cv, u[:, META - 2:SM - 2], V("conv", t), None, ALU.mult))
                    link(stt(cv, u[:, META - 1:SM - 1], V("conv", KC + t), cv, ALU.mult, ALU.add))
                    link(stt(cv, u[:, META:SM], V("conv", 2 * KC + t), cv, ALU.mult, ALU.add))
                    b = ready(dve, ("cb", t))
                    drain(tt(cv, cv, ps[:, b, :], ALU.mult), b)
            for n in range(NF + 1):
                if n < NF:
                    diff_front(n)
                if n:
                    diff_back(n - 1)
                if n:
                    for piece in conv_pieces(n - 1):
                        conv_part(*piece)
                    hd, i = (n - 1) // NT, (n - 1) % NT
                    if i == 1 and hd:
                        diff_norm(hd - 1)
            diff_norm(FH - 1)
            branch("br1", False)
            branch("br2", False)
            for k in range(KC):
                split(RET["merged"][:, k, :], "m2", k)
            add_out("m2")
            split_norm("f2", xres, V("norm2", 0, KC))
            for half in range(2):
                st = f"f2{half}"
                with dve.Fori(0, HALF2 // 4) as i:
                    for q in range(4):
                        hi, lo = (hid2[:, part, bass.ds(i * 4 + q, 1), :] for part in range(2))
                        v = sq[:, q % 2:q % 2 + 1, :]
                        dve.wait_ge(sem("f2_squares"), i * 4 + (half * HALF2 + q + 1))
                        dve.tensor_copy(hi, v).then_inc(sem("f2_upper_half"), 1)
                        dve.wait_ge(sem("f2_upper_half"), i * 4 + (half * HALF2 + q + 1))
                        drain(tt(lo, v, hi.bitcast(F32), ALU.subtract), uses[(st, "up", q)][0])
                add_out(st)
            x_chunk(dve, "f21", KC - 1)
            norm("nf", xres, V("final", 0, KC), hd_())


def _fm(w, n0, n1):
    w = w[:, n0:n1]
    return w.reshape(KC, P, -1, P).transpose(2, 1, 0, 3).reshape(-1, P, UNIT)


def _tm(w, n0, n1):
    w = w[:, n0:n1]
    return w.reshape(4, 2, P, -1, S).transpose(3, 0, 2, 1, 4).reshape(-1, P, UNIT)


def _deep(w):
    f = w.shape[0] // P
    n = -(-f // 8)
    t = np.zeros((KC, P, n * 8, P), w.dtype)
    t[:, :, :f] = w.reshape(f, P, KC, P).transpose(2, 1, 0, 3)
    return t.reshape(KC, P, n, UNIT).transpose(0, 2, 1, 3).reshape(-1, P, UNIT)


def _pairs(a, b):
    return np.stack([a, b], 1).reshape(-1, P, UNIT)


def _cols(v):
    return np.asarray(v).reshape(-1, P).T


def _consts():
    i = np.arange(P)
    r, c = i[:, None], i[None, :]
    eye = np.eye(P, dtype=np.float32)
    same = (r // GCH) == (c // GCH)
    invf = np.stack([np.float32(10000.0) ** (-(i % h).astype(np.float32) / np.float32(h)) for h in (64, 32)], 1)
    sign = np.stack([np.where(i % (2 * h) < h, -1.0, 1.0) for h in (64, 32)], 1)
    carry = np.broadcast_to((np.arange(S) % GCH != 0), (P, S))
    rc = np.concatenate([1.0 / np.minimum(np.arange(16) + 1.0, w) for w in WINDOWS])
    parts = [eye, eye[(i + 64) % P], eye[(i // 64) * 64 + (i % 64 + 32) % 64], np.where(c <= r, 0.0, NEG),
             (r <= c) & same, r > c, r < c, carry, invf, sign, np.broadcast_to(rc, (P, 64))]
    a = np.concatenate([np.asarray(p, np.float32) for p in parts], 1)
    q = np.arange(SM)[None, :] - i[:, None]
    g = 1.0 - 2.0 ** (-5.0 - np.arange(RH))
    decay = [np.where(q >= 0, x ** np.maximum(q, 0), 0.0) for x in g]
    d = r - (np.arange(SM)[None, :] - (SM - P))
    dist = np.where(d >= 0, -d, -1.0e34)
    return np.ascontiguousarray(a), np.concatenate([*decay, dist], 1).astype(np.float32)


def kernel(**a):
    import concourse.bacc as bacc
    from concourse.bass_utils import run_bass_kernel_spmd

    a = {k: np.asarray(v) for k, v in a.items()}
    ab, w2 = a["ab_w_in"][0], a["w_in_2"][0]
    o = np.cumsum([0, 256, 256, 512, 16, 512, 512, 512, 512, 512, 64, 8])
    misc = np.zeros((D, P), ab.dtype)
    misc[:, :GRANK] = ab[:, o[3]:o[4]]
    misc[:, GRANK:GRANK + IH] = ab[:, o[10]:o[11]]
    ik = ab[:, o[9]:o[10]]
    ik = np.concatenate([ik, ik], 1)
    cd = a["cd_w_in"][0]

    def w1(layer):
        w = a["ffn_w1"][layer]
        return _pairs(_fm(w, 0, D_FF), _fm(w, D_FF, 2 * D_FF))

    def br(n):
        return _pairs(_fm(w2, 9216 + n * D, 9216 + (n + 1) * D), _fm(a["w_branch_2"][0, n], 0, D))
    conv = np.stack([_fm(w2, 7168, 8192), _fm(w2, 8192, 9216), _fm(w2, 6144, 7168)], 1).reshape(-1, P, UNIT)
    packs = {
        "ada_first": lambda: _tm(a["ada_w"][0], 0, 2 * D),
        "ab": lambda: np.concatenate([_fm(misc, 0, P), _fm(ab, o[1], o[2]), _fm(ab, o[0], o[1]), _fm(ab, o[4], o[5]),
                                      _tm(ab, o[2], o[3]), _fm(ab, o[8], o[9]), _fm(ik, 0, P), _fm(ab, o[5], o[7]),
                                      _tm(ab, o[7], o[8])]),
        "ab_out": lambda: _fm(a["ab_w_out"][0], 0, D), "w1_0": lambda: w1(0), "w1_1": lambda: w1(1),
        "w2_0": lambda: _deep(a["ffn_w2"][0]), "w2_1": lambda: _deep(a["ffn_w2"][1]),
        "cd": lambda: np.concatenate([_fm(cd, 0, 1536), _tm(cd, 1536, 2048)]),
        "cd_out": lambda: _fm(a["cd_w_out"][0], 0, D),
        "in2": lambda: np.concatenate([_fm(w2, 0, 1024), _fm(w2, 2048, 3072), _tm(w2, 1024, 2048),
                                       _fm(w2, 3072, 5120), _tm(w2, 5120, 6144), conv]),
        "br0": lambda: br(0), "br1": lambda: br(1), "br2": lambda: br(2),
        "w_out2": lambda: _fm(a["w_out_2"][0], 0, D), "up2": lambda: _fm(a["w_up_2"][0], 0, D_FF2),
        "down2": lambda: np.concatenate([_deep(a["w_down_2"][0][:D_FF2 // 2]), _deep(a["w_down_2"][0][D_FF2 // 2:])]),
    }
    lam = np.zeros((P, 4), a["diff_lambda_2"].dtype)
    lam[:FHD] = a["diff_lambda_2"][0].T
    vecs = np.concatenate([
        _cols(a["mix_norm"]), _cols(a["ffn_norm"]), _cols(a["ada_b"]), _cols(a["c"]), _cols(a["gla_gate_b"]),
        _cols(a["gla_out_norm"]), _cols(a["dsa_q_norm"]), _cols(a["dsa_k_norm"]), _cols(a["pool_scale"]),
        _cols(a["sb_q_norm"]), _cols(a["sb_k_norm"]), _cols(a["norm1_w_2"]), _cols(a["conv_w_2"]),
        _cols(a["diff_subln_w_2"]), _cols(a["norm2_w_2"]), _cols(a["final_norm_w_2"]), lam], 1)
    consts, tables2 = _consts()
    arrays = {
        "vecs": np.ascontiguousarray(vecs), "consts": consts, "tables2": tables2,
        "x": np.ascontiguousarray(a["x"][0].T.reshape(KC, P, S).transpose(1, 0, 2)),
        "meta": np.ascontiguousarray(a["meta_tokens_2"].T.reshape(KC, P, META).transpose(1, 0, 2)),
        "positions": np.ascontiguousarray(a["positions"]),
        "gate_up": np.ascontiguousarray(a["gla_gate_up"][0]),
        "pool_w": np.ascontiguousarray(a["pool_w"][0].transpose(1, 0, 2)),
    }
    ada_rest = np.concatenate([_tm(a["ada_w"][0], 2 * D, 6 * D), _tm(a["ada_w"][1], 0, 6 * D)])
    ada_rest = np.ascontiguousarray(ada_rest.reshape(-1, P, 2, S))
    arrays["ada_rest"], arrays["ada_late"] = ada_rest[:ADA_REST * ADA_UNITS], ada_rest[ADA_REST * ADA_UNITS:]
    nc = bacc.Bacc("TRN2", target_bir_lowering=False, num_devices=1)
    n_units = N_UNITS
    A = {k: nc.dram_tensor(f"in_{k}", v.shape, mybir.dt.from_np(v.dtype), kind="ExternalInput").ap()
         for k, v in arrays.items()}
    A["stream"] = nc.dram_tensor("in_stream", (n_units, P, UNIT), F32, kind="ExternalInput").ap()
    A["out"] = nc.dram_tensor("out_0", (P, KC, S), F32, kind="ExternalOutput").ap()
    plan = []
    build(nc, A, plan)
    packed = {k: f() for k, f in packs.items()}
    arrays["stream"] = np.concatenate([packed[name][first:first + count] for name, first, count in plan])
    assert arrays["stream"].shape[0] == n_units
    r = run_bass_kernel_spmd(nc, [{f"in_{k}": v for k, v in arrays.items()}], core_ids=[0])
    got = r.results[0]["out_0"]
    return np.ascontiguousarray(got.transpose(1, 0, 2).reshape(D, S).T)[None]
```
